# Optimizing a Trainium2 kernel written in Bass

```python
import math
import jax, jax.numpy as jnp
from jax import lax
import numpy as np

D_MODEL = 1024
BATCH = 1
SEQ = 512
DEPTH = 1

GRID_W = 64
D_MIX = D_MODEL
EPS = 1e-6
CONV_W = 256
CONV_K = 3
NA_HEADS = 4
NA_DH = 64
NA_W = NA_HEADS * NA_DH
NA_KH = 8
NA_KW = 16
GDN_HEADS = 4
GDN_DK = 128
GDN_DV = 128
GDN_W = GDN_HEADS * GDN_DV
GDN_CONV_K = 3
GDN_CHUNK = 64
GDN_QKV = 2 * GDN_HEADS * GDN_DK + GDN_W
IN_SPLITS = (CONV_W, CONV_W, CONV_W, NA_W, NA_W, NA_W, GDN_QKV, GDN_W, 2 * GDN_HEADS, 2 * GDN_HEADS)
D_IN = 3 * CONV_W + 3 * NA_W + GDN_QKV + GDN_W + 4 * GDN_HEADS
N_GROUPS = 4
EXPERTS_PER_GROUP = 8
N_EXPERTS = N_GROUPS * EXPERTS_PER_GROUP
TOP_K = 2
D_EXPERT = 512
MOE_BLOCK = 256


def _rmsnorm(x, w):
    xf = x.astype(jnp.float32)
    y = xf * lax.rsqrt(jnp.mean(xf * xf, axis=-1, keepdims=True) + EPS)
    return (y * w.astype(jnp.float32)).astype(x.dtype)

def _l2norm(x):
    xf = x.astype(jnp.float32)
    return xf * lax.rsqrt(jnp.sum(xf * xf, axis=-1, keepdims=True) + EPS)

def _dwconv(x, w):
    ch = x.shape[-1]
    return lax.conv_general_dilated(x, w[:, None, :].astype(x.dtype), window_strides=(1,), padding='SAME',
                                    dimension_numbers=('NWC', 'WIO', 'NWC'), feature_group_count=ch)

def _neighbourhood_attention(q, k, v, rpb):
    bsz, t, h, dh = q.shape
    rows = t // GRID_W
    kh = min(NA_KH, rows)
    qg = q.reshape(bsz, rows, GRID_W, h, dh)
    kg = k.reshape(bsz, rows, GRID_W, h, dh)
    vg = v.reshape(bsz, rows, GRID_W, h, dh)
    col = jnp.arange(GRID_W)
    col_idx = jnp.clip(col - NA_KW // 2, 0, GRID_W - NA_KW)[:, None] + jnp.arange(NA_KW)[None, :]
    dc = col_idx - col[:, None] + (NA_KW - 1)
    row_start = jnp.clip(jnp.arange(rows) - kh // 2, 0, rows - kh)
    scale = dh ** -0.5

    def one_row(r):
        rs = row_start[r]
        q_r = lax.dynamic_index_in_dim(qg, r, axis=1, keepdims=False)
        k_rows = lax.dynamic_slice_in_dim(kg, rs, kh, axis=1)
        v_rows = lax.dynamic_slice_in_dim(vg, rs, kh, axis=1)
        k_win = k_rows[:, :, col_idx]
        v_win = v_rows[:, :, col_idx]
        dr = rs + jnp.arange(kh) - r + (NA_KH - 1)
        bias = rpb[:, dr][:, :, dc]
        s = jnp.einsum('bchd,brckhd->bhcrk', q_r, k_win).astype(jnp.float32) * scale
        s = s + jnp.transpose(bias, (0, 2, 1, 3)).astype(jnp.float32)[None]
        p = jax.nn.softmax(s.reshape(bsz, h, GRID_W, kh * NA_KW), axis=-1).reshape(s.shape).astype(v.dtype)
        return jnp.einsum('bhcrk,brckhd->bchd', p, v_win)

    out = lax.map(one_row, jnp.arange(rows))
    return jnp.transpose(out, (1, 0, 2, 3, 4)).reshape(bsz, t, h * dh)

def _gated_delta_chunked(q, k, v, g, beta):
    bsz, h, t, dk = q.shape
    dv = v.shape[-1]
    n = t // GDN_CHUNK
    cs = lambda a: a.reshape((bsz, h, n, GDN_CHUNK) + a.shape[3:])
    q, k, v, g, beta = cs(q), cs(k), cs(v), cs(g), cs(beta)
    g = jnp.cumsum(g, axis=-1)
    idx = jnp.arange(GDN_CHUNK)
    strict = idx[:, None] > idx[None, :]
    incl = idx[:, None] >= idx[None, :]
    diff = g[..., :, None] - g[..., None, :]
    dec_strict = jnp.exp(jnp.where(strict, diff, -jnp.inf))
    dec_incl = jnp.exp(jnp.where(incl, diff, -jnp.inf))
    kb = k * beta[..., None]
    lower = jnp.einsum('bhncd,bhnsd->bhncs', kb, k) * dec_strict
    rhs = jnp.concatenate([v * beta[..., None], kb * jnp.exp(g)[..., None]], axis=-1)
    sol = lax.linalg.triangular_solve(lower, rhs, left_side=True, lower=True, unit_diagonal=True)
    u, w = sol[..., :dv], sol[..., dv:]
    intra = jnp.einsum('bhncd,bhnsd->bhncs', q, k) * dec_incl
    q_dec = q * jnp.exp(g)[..., None]
    g_last = g[..., -1]
    k_dec = k * jnp.exp(g_last[..., None] - g)[..., None]

    def step(state, xs):
        u_c, w_c, intra_c, q_c, k_c, gl_c = xs
        v_new = u_c - jnp.einsum('bhcd,bhde->bhce', w_c, state)
        o_c = jnp.einsum('bhcd,bhde->bhce', q_c, state) + jnp.einsum('bhcs,bhse->bhce', intra_c, v_new)
        state = state * jnp.exp(gl_c)[..., None, None] + jnp.einsum('bhcd,bhce->bhde', k_c, v_new)
        return state, o_c

    xs = tuple(jnp.moveaxis(a, 2, 0) for a in (u, w, intra, q_dec, k_dec, g_last))
    s0 = jnp.zeros((bsz, h, dk, dv), jnp.float32)
    _, o = lax.scan(step, s0, xs)
    return jnp.moveaxis(o, 0, 2).reshape(bsz, h, t, dv)

def _gdn_mixer(qkv, z, a, b, conv_w, a_log, dt_bias, norm_w):
    bsz, t, _ = qkv.shape
    qkv = jax.nn.silu(_dwconv(qkv, conv_w))
    q = qkv[..., :GDN_HEADS * GDN_DK].reshape(bsz, t, GDN_HEADS, GDN_DK)
    k = qkv[..., GDN_HEADS * GDN_DK:2 * GDN_HEADS * GDN_DK].reshape(bsz, t, GDN_HEADS, GDN_DK)
    v = qkv[..., 2 * GDN_HEADS * GDN_DK:].reshape(bsz, t, GDN_HEADS, GDN_DV)
    q = jnp.transpose(_l2norm(q) * (GDN_DK ** -0.5), (0, 2, 1, 3))
    k = jnp.transpose(_l2norm(k), (0, 2, 1, 3))
    v = jnp.transpose(v.astype(jnp.float32), (0, 2, 1, 3))
    a = a.astype(jnp.float32).reshape(bsz, t, 2, GDN_HEADS)
    b = b.astype(jnp.float32).reshape(bsz, t, 2, GDN_HEADS)
    g = -jnp.exp(a_log.astype(jnp.float32)) * jax.nn.softplus(a + dt_bias.astype(jnp.float32))
    beta = jax.nn.sigmoid(b)
    g = jnp.transpose(g, (2, 0, 3, 1))
    beta = jnp.transpose(beta, (2, 0, 3, 1))
    flip = lambda a_: jnp.flip(a_, axis=2)
    o_fwd = _gated_delta_chunked(q, k, v, g[0], beta[0])
    o_bwd = flip(_gated_delta_chunked(flip(q), flip(k), flip(v), flip(g[1]), flip(beta[1])))
    o = jnp.transpose(o_fwd + o_bwd, (0, 2, 1, 3))
    o = o * lax.rsqrt(jnp.mean(o * o, axis=-1, keepdims=True) + EPS) * norm_w.astype(jnp.float32)
    o = o * jax.nn.silu(z.astype(jnp.float32).reshape(bsz, t, GDN_HEADS, GDN_DV))
    return o.reshape(bsz, t, GDN_W).astype(qkv.dtype)

def _hier_moe(h, wg, bg, we, be, w1, w3, w2):
    bsz, t, d = h.shape
    xt = h.reshape(bsz * t, d)
    n = xt.shape[0]
    pg = jax.nn.softmax((xt @ wg + bg).astype(jnp.float32), axis=-1)
    grp = jnp.argmax(pg, axis=-1)
    pg_top = jnp.take_along_axis(pg, grp[:, None], axis=-1)
    el = (xt @ we + be).astype(jnp.float32).reshape(n, N_GROUPS, EXPERTS_PER_GROUP)
    el_grp = jnp.take_along_axis(el, grp[:, None, None], axis=1)[:, 0]
    top_logit, top_e = lax.top_k(el_grp, TOP_K)
    gate = pg_top * jax.nn.softmax(top_logit, axis=-1)
    expert = (grp[:, None] * EXPERTS_PER_GROUP + top_e).reshape(-1)
    n_slots = n * TOP_K
    order = jnp.argsort(expert)
    sorted_e = expert[order]
    tok = order // TOP_K
    sizes = jnp.bincount(expert, length=N_EXPERTS)
    padded = (sizes + MOE_BLOCK - 1) // MOE_BLOCK * MOE_BLOCK
    pad_end = jnp.cumsum(padded)
    pad_start = pad_end - padded
    seg_start = jnp.cumsum(sizes) - sizes
    dest = pad_start[sorted_e] + jnp.arange(n_slots) - seg_start[sorted_e]
    padded_rows = (n_slots + N_EXPERTS * (MOE_BLOCK - 1) + MOE_BLOCK - 1) // MOE_BLOCK * MOE_BLOCK
    n_blocks = padded_rows // MOE_BLOCK
    buf = jnp.zeros((padded_rows, d), xt.dtype).at[dest].set(xt[tok])
    block_e = jnp.minimum(jnp.searchsorted(pad_end, jnp.arange(n_blocks) * MOE_BLOCK, side='right'), N_EXPERTS - 1)

    def expert_block(args):
        xb, e = args
        return (jax.nn.silu(xb @ w1[e]) * (xb @ w3[e])) @ w2[e]

    ys = lax.map(expert_block, (buf.reshape(n_blocks, MOE_BLOCK, d), block_e)).reshape(padded_rows, d)[dest]
    ys = ys * gate.reshape(-1)[order][:, None].astype(ys.dtype)
    return jnp.zeros_like(xt).at[tok].add(ys).reshape(bsz, t, d)

def first_inputs(seed: int = 0) -> dict:
    key = jax.random.key(seed)
    ks = jax.random.split(key, 22)
    f32 = jnp.float32
    nrm = lambda k_, shape, s: jax.random.normal(k_, shape, f32) * s
    x = nrm(ks[0], (BATCH, SEQ, D_MODEL), 1.0)
    c = nrm(ks[1], (BATCH, D_MODEL), 1.0)
    norm_mix_w = 1.0 + nrm(ks[2], (DEPTH, D_MODEL), 0.02)
    norm_ffn_w = 1.0 + nrm(ks[3], (DEPTH, D_MODEL), 0.02)
    w_ada = nrm(ks[4], (DEPTH, D_MODEL, 6 * D_MODEL), 0.5 * D_MODEL ** -0.5)
    b_ada = nrm(ks[5], (DEPTH, 6 * D_MODEL), 0.02)
    w_in = nrm(ks[6], (DEPTH, D_MODEL, D_IN), D_MODEL ** -0.5)
    conv_a_w = nrm(ks[7], (DEPTH, CONV_K, CONV_W), CONV_K ** -0.5)
    na_rpb = nrm(ks[8], (DEPTH, NA_HEADS, 2 * NA_KH - 1, 2 * NA_KW - 1), 0.1)
    gdn_conv_w = nrm(ks[9], (DEPTH, GDN_CONV_K, GDN_QKV), GDN_CONV_K ** -0.5)
    gdn_a_log = jnp.log(jax.random.uniform(ks[10], (DEPTH, 2, GDN_HEADS), f32, 1.0, 16.0))
    dt = jnp.exp(jax.random.uniform(ks[11], (DEPTH, 2, GDN_HEADS), f32, math.log(1e-3), math.log(1e-1)))
    gdn_dt_bias = dt + jnp.log(-jnp.expm1(-dt))
    gdn_norm_w = 1.0 + nrm(ks[12], (DEPTH, GDN_DV), 0.02)
    w_out = nrm(ks[13], (DEPTH, D_MIX, D_MODEL), D_MIX ** -0.5)
    router_group_w = nrm(ks[14], (DEPTH, D_MODEL, N_GROUPS), D_MODEL ** -0.5)
    router_group_b = nrm(ks[15], (DEPTH, N_GROUPS), 0.01)
    router_expert_w = nrm(ks[16], (DEPTH, D_MODEL, N_EXPERTS), D_MODEL ** -0.5)
    router_expert_b = nrm(ks[17], (DEPTH, N_EXPERTS), 0.01)
    expert_w1 = nrm(ks[18], (DEPTH, N_EXPERTS, D_MODEL, D_EXPERT), D_MODEL ** -0.5)
    expert_w3 = nrm(ks[19], (DEPTH, N_EXPERTS, D_MODEL, D_EXPERT), D_MODEL ** -0.5)
    expert_w2 = nrm(ks[20], (DEPTH, N_EXPERTS, D_EXPERT, D_MODEL), D_EXPERT ** -0.5)
    final_norm_w = 1.0 + nrm(ks[21], (D_MODEL,), 0.02)
    return {"x": x, "c": c, "norm_mix_w": norm_mix_w, "norm_ffn_w": norm_ffn_w, "w_ada": w_ada, "b_ada": b_ada,
            "w_in": w_in, "conv_a_w": conv_a_w, "na_rpb": na_rpb, "gdn_conv_w": gdn_conv_w,
            "gdn_a_log": gdn_a_log, "gdn_dt_bias": gdn_dt_bias, "gdn_norm_w": gdn_norm_w, "w_out": w_out,
            "router_group_w": router_group_w, "router_group_b": router_group_b,
            "router_expert_w": router_expert_w, "router_expert_b": router_expert_b,
            "expert_w1": expert_w1, "expert_w3": expert_w3, "expert_w2": expert_w2, "final_norm_w": final_norm_w}

def first_block(x, c, norm_mix_w, norm_ffn_w, w_ada, b_ada, w_in, conv_a_w, na_rpb, gdn_conv_w, gdn_a_log,
              gdn_dt_bias, gdn_norm_w, w_out, router_group_w, router_group_b, router_expert_w, router_expert_b,
              expert_w1, expert_w3, expert_w2, final_norm_w):
    bsz, t, _ = x.shape
    cond = jax.nn.silu(c)
    split_at = np.cumsum(IN_SPLITS)[:-1].tolist()
    for l in range(DEPTH):
        mod = cond @ w_ada[l] + b_ada[l]
        shift1, scale1, gate1, shift2, scale2, gate2 = [m[:, None, :] for m in jnp.split(mod, 6, axis=-1)]
        hmix = _rmsnorm(x, norm_mix_w[l]) * (1.0 + scale1) + shift1
        proj = hmix @ w_in[l]
        cb, cc, cx, nq, nk, nv, gqkv, gz, ga, gb = jnp.split(proj, split_at, axis=-1)
        y_conv = cb * _dwconv(cc * cx, conv_a_w[l])
        y_na = _neighbourhood_attention(nq.reshape(bsz, t, NA_HEADS, NA_DH), nk.reshape(bsz, t, NA_HEADS, NA_DH),
                                        nv.reshape(bsz, t, NA_HEADS, NA_DH), na_rpb[l])
        y_gdn = _gdn_mixer(gqkv, gz, ga, gb, gdn_conv_w[l], gdn_a_log[l], gdn_dt_bias[l], gdn_norm_w[l])
        mixed = jnp.concatenate([y_conv, y_na, y_gdn], axis=-1) @ w_out[l]
        x = x + gate1 * mixed
        hffn = _rmsnorm(x, norm_ffn_w[l]) * (1.0 + scale2) + shift2
        y_moe = _hier_moe(hffn, router_group_w[l], router_group_b[l], router_expert_w[l], router_expert_b[l],
                          expert_w1[l], expert_w3[l], expert_w2[l])
        x = x + gate2 * y_moe
    return _rmsnorm(x, final_norm_w)


CHUNK = 64
HEAD_DIM = 64
N_HEADS_FOX = 8
N_HEADS_CHUNK = 8
WIDTH_FOX = N_HEADS_FOX * HEAD_DIM
WIDTH_CHUNK = N_HEADS_CHUNK * HEAD_DIM
LEFT_CHUNKS = 8
BAND_CHUNKS = LEFT_CHUNKS + 1
REL_CLIP = 128
Q_BLOCK = 128
D_FF = 2816
CONV_WIDTH = 3
LN_EPS = 1e-5
N_MOD = 6
PROJ_SIZES = (WIDTH_FOX, WIDTH_FOX, WIDTH_FOX, N_HEADS_FOX,
              WIDTH_CHUNK, WIDTH_CHUNK, WIDTH_CHUNK, D_MODEL, D_MODEL)
PROJ_COLS = sum(PROJ_SIZES)


def _layer_norm(x, gain=None, bias=None):
    xf = x.astype(jnp.float32)
    mu = jnp.mean(xf, axis=-1, keepdims=True)
    var = jnp.mean(jnp.square(xf - mu), axis=-1, keepdims=True)
    y = (xf - mu) * lax.rsqrt(var + LN_EPS)
    if gain is not None:
        y = y * gain.astype(jnp.float32) + bias.astype(jnp.float32)
    return y.astype(x.dtype)

def _forgetting_attention(q, k, v, f_logit):
    b, s, h, dh = q.shape
    n_blk = s // Q_BLOCK
    log_f = jax.nn.log_sigmoid(f_logit.astype(jnp.float32))
    cum = jnp.cumsum(log_f, axis=1).transpose(0, 2, 1)
    scale = 1.0 / math.sqrt(dh)
    k_pos = jnp.arange(s)
    q_blocks = q.reshape(b, n_blk, Q_BLOCK, h, dh).transpose(1, 0, 2, 3, 4)
    cum_blocks = cum.reshape(b, h, n_blk, Q_BLOCK).transpose(2, 0, 1, 3)
    neg = jnp.finfo(jnp.float32).min

    def block(args):
        qb, cq, i = args
        q_pos = i * Q_BLOCK + jnp.arange(Q_BLOCK)
        logits = jnp.einsum('bqhd,bkhd->bhqk', qb, k).astype(jnp.float32) * scale
        logits = logits + cq[:, :, :, None] - cum[:, :, None, :]
        mask = k_pos[None, :] <= q_pos[:, None]
        logits = jnp.where(mask[None, None], logits, neg)
        p = jax.nn.softmax(logits, axis=-1).astype(v.dtype)
        return jnp.einsum('bhqk,bkhd->bqhd', p, v)

    out = lax.map(block, (q_blocks, cum_blocks, jnp.arange(n_blk)))
    return out.transpose(1, 0, 2, 3, 4).reshape(b, s, h * dh)

def _chunk_band_attention(q, k, v, rel_table):
    b, s, h, dh = q.shape
    n_c = s // CHUNK
    band = BAND_CHUNKS * CHUNK
    qc = q.reshape(b, n_c, CHUNK, h, dh)
    pad = ((0, 0), (LEFT_CHUNKS, 0), (0, 0), (0, 0), (0, 0))
    kp = jnp.pad(k.reshape(b, n_c, CHUNK, h, dh), pad)
    vp = jnp.pad(v.reshape(b, n_c, CHUNK, h, dh), pad)
    band_idx = jnp.arange(n_c)[:, None] + jnp.arange(BAND_CHUNKS)[None, :]
    kb = kp[:, band_idx].reshape(b, n_c, band, h, dh)
    vb = vp[:, band_idx].reshape(b, n_c, band, h, dh)
    valid = jnp.repeat(band_idx >= LEFT_CHUNKS, CHUNK, axis=1)
    q_off = LEFT_CHUNKS * CHUNK + np.arange(CHUNK)
    rel = np.clip(q_off[:, None] - np.arange(band)[None, :], -REL_CLIP, REL_CLIP) + REL_CLIP
    bias = rel_table[:, rel].astype(jnp.float32)
    scale = 1.0 / math.sqrt(dh)
    logits = jnp.einsum('bcqhd,bckhd->bchqk', qc, kb).astype(jnp.float32) * scale
    logits = logits + bias[None, None]
    logits = jnp.where(valid[None, :, None, None, :], logits, jnp.finfo(jnp.float32).min)
    p = jax.nn.softmax(logits, axis=-1).astype(v.dtype)
    out = jnp.einsum('bchqk,bckhd->bcqhd', p, vb)
    return out.reshape(b, s, h * dh)

def _causal_depthwise_conv(u, w, bias):
    s = u.shape[1]
    up = jnp.pad(u, ((0, 0), (CONV_WIDTH - 1, 0), (0, 0)))
    y = bias
    for j in range(CONV_WIDTH):
        y = y + w[j] * up[:, j:j + s]
    return y

def second_inputs(seed: int = 0) -> dict:
    key = jax.random.key(seed)
    ks = jax.random.split(key, 20)
    beta = (8.0 * DEPTH) ** -0.25
    f32 = jnp.float32
    nrm = lambda k, shape: jax.random.normal(k, shape, f32)
    col_scale = np.concatenate([
        np.ones(2 * WIDTH_FOX), beta * np.ones(WIDTH_FOX), 0.5 * np.ones(N_HEADS_FOX),
        np.ones(2 * WIDTH_CHUNK), beta * np.ones(WIDTH_CHUNK), np.ones(2 * D_MODEL)]).astype(np.float32)
    w_in = nrm(ks[2], (DEPTH, D_MODEL, PROJ_COLS)) * (D_MODEL ** -0.5) * jnp.asarray(col_scale)
    b_f = jnp.linspace(1.0, 5.0, N_HEADS_FOX, dtype=f32)[None, :] + 0.1 * nrm(ks[3], (DEPTH, N_HEADS_FOX))
    rel_bias = 0.5 * nrm(ks[4], (DEPTH, N_HEADS_CHUNK, 2 * REL_CLIP + 1))
    w_br_fox = nrm(ks[5], (DEPTH, WIDTH_FOX, D_MODEL)) * WIDTH_FOX ** -0.5
    w_br_chunk = nrm(ks[6], (DEPTH, WIDTH_CHUNK, D_MODEL)) * WIDTH_CHUNK ** -0.5
    w_out = nrm(ks[7], (DEPTH, D_MODEL, D_MODEL)) * (D_MODEL ** -0.5) * beta
    w_up = nrm(ks[8], (DEPTH, D_MODEL, 2 * D_FF)) * D_MODEL ** -0.5
    conv_w = 0.3 * nrm(ks[9], (DEPTH, CONV_WIDTH, 2 * D_FF)) + jnp.array([0.0, 0.0, 1.0], f32)[None, :, None]
    conv_b = 0.01 * nrm(ks[10], (DEPTH, 2 * D_FF))
    w_down = nrm(ks[11], (DEPTH, D_FF, D_MODEL)) * (D_FF ** -0.5) * beta
    w_ada = 0.2 * nrm(ks[12], (DEPTH, D_MODEL, N_MOD * D_MODEL)) * D_MODEL ** -0.5
    b_ada = 0.01 * nrm(ks[13], (DEPTH, N_MOD * D_MODEL))
    ln1_g = 1.0 + 0.05 * nrm(ks[14], (DEPTH, D_MODEL))
    ln1_b = 0.01 * nrm(ks[15], (DEPTH, D_MODEL))
    ln2_g = 1.0 + 0.05 * nrm(ks[16], (DEPTH, D_MODEL))
    ln2_b = 0.01 * nrm(ks[17], (DEPTH, D_MODEL))
    x = nrm(ks[0], (BATCH, SEQ, D_MODEL))
    c = nrm(ks[1], (BATCH, D_MODEL))
    return {"x": x, "c": c, "w_in": w_in, "b_f": b_f, "rel_bias": rel_bias,
            "w_br_fox": w_br_fox, "w_br_chunk": w_br_chunk, "w_out": w_out,
            "w_up": w_up, "conv_w": conv_w, "conv_b": conv_b, "w_down": w_down,
            "w_ada": w_ada, "b_ada": b_ada, "ln1_g": ln1_g, "ln1_b": ln1_b,
            "ln2_g": ln2_g, "ln2_b": ln2_b}

def second_block(x, c, w_in, b_f, rel_bias, w_br_fox, w_br_chunk, w_out, w_up, conv_w,
              conv_b, w_down, w_ada, b_ada, ln1_g, ln1_b, ln2_g, ln2_b):
    alpha = (2.0 * DEPTH) ** 0.25
    b, s, _ = x.shape
    split_points = list(np.cumsum(PROJ_SIZES)[:-1])
    cond = jax.nn.silu(c)
    for l in range(DEPTH):
        mod = cond @ w_ada[l] + b_ada[l]
        sh1, sc1, g1, sh2, sc2, g2 = jnp.split(mod[:, None, :], N_MOD, axis=-1)

        h = _layer_norm(x) * (1.0 + sc1) + sh1
        proj = h @ w_in[l]
        q_a, k_a, v_a, f_a, q_c, k_c, v_c, gate_a, gate_c = jnp.split(proj, split_points, axis=-1)
        heads_a = lambda t: t.reshape(b, s, N_HEADS_FOX, HEAD_DIM)
        heads_c = lambda t: t.reshape(b, s, N_HEADS_CHUNK, HEAD_DIM)
        o_a = _forgetting_attention(heads_a(q_a), heads_a(k_a), heads_a(v_a), f_a + b_f[l])
        o_c = _chunk_band_attention(heads_c(q_c), heads_c(k_c), heads_c(v_c), rel_bias[l])
        merged = (jax.nn.sigmoid(gate_a) * (o_a @ w_br_fox[l])
                  + jax.nn.sigmoid(gate_c) * (o_c @ w_br_chunk[l]))
        mix = merged @ w_out[l]
        x = _layer_norm(alpha * x + (1.0 + g1) * mix, ln1_g[l], ln1_b[l])

        h = _layer_norm(x) * (1.0 + sc2) + sh2
        u = _causal_depthwise_conv(h @ w_up[l], conv_w[l], conv_b[l])
        a, val = jnp.split(u, 2, axis=-1)
        y = (jax.nn.silu(a) * val) @ w_down[l]
        x = _layer_norm(alpha * x + (1.0 + g2) * y, ln2_g[l], ln2_b[l])
    return x


def setup_inputs(seed=0):
    out = dict(first_inputs(seed))
    for name, value in second_inputs(seed + 1).items():
        if name != "x":
            out[name + "_2"] = value
    return out


def reference(
    x, c, norm_mix_w, norm_ffn_w, w_ada, b_ada, w_in, conv_a_w, na_rpb, gdn_conv_w, gdn_a_log,
    gdn_dt_bias, gdn_norm_w, w_out, router_group_w, router_group_b, router_expert_w,
    router_expert_b, expert_w1, expert_w3, expert_w2, final_norm_w, c_2, w_in_2, b_f_2,
    rel_bias_2, w_br_fox_2, w_br_chunk_2, w_out_2, w_up_2, conv_w_2, conv_b_2, w_down_2,
    w_ada_2, b_ada_2, ln1_g_2, ln1_b_2, ln2_g_2, ln2_b_2,
):
    x = first_block(
        x, c, norm_mix_w, norm_ffn_w, w_ada, b_ada, w_in, conv_a_w, na_rpb, gdn_conv_w,
        gdn_a_log, gdn_dt_bias, gdn_norm_w, w_out, router_group_w, router_group_b,
        router_expert_w, router_expert_b, expert_w1, expert_w3, expert_w2, final_norm_w,
    )
    return second_block(
        x, c_2, w_in_2, b_f_2, rel_bias_2, w_br_fox_2, w_br_chunk_2, w_out_2, w_up_2, conv_w_2,
        conv_b_2, w_down_2, w_ada_2, b_ada_2, ln1_g_2, ln1_b_2, ln2_g_2, ln2_b_2,
    )


_drawn_inputs = setup_inputs


def setup_inputs(seed=0):
    import zlib

    import numpy as np

    out = dict(_drawn_inputs(seed))
    spreads = {}
    factors = {'norm_mix_w': 4.857,
     'norm_ffn_w': 15.078,
     'na_rpb': 50.373,
     'gdn_a_log': 2.99,
     'gdn_norm_w': 41.841,
     'router_group_b': 64.0,
     'router_expert_b': 64.0,
     'rel_bias_2': 5.837,
     'conv_b_2': 8.0,
     'b_ada_2': 6.537,
     'ln1_b_2': 5.416,
     'ln2_b_2': 5.681}
    for name, (base, spread) in spreads.items():
        noise = np.random.default_rng([zlib.crc32(name.encode()), seed]).standard_normal(out[name].shape)
        drawn = base * np.exp(spread * noise) if base else spread * noise
        out[name] = __import__('jax').numpy.asarray(drawn.astype(out[name].dtype))
    for name, factor in factors.items():
        out[name] = (out[name] * factor).astype(out[name].dtype)
    return out
```

```python
from contextlib import ExitStack

import numpy as np

import concourse.bass as bass
from concourse import mybir

F32 = mybir.dt.float32
I32 = mybir.dt.int32
U32 = mybir.dt.uint32
ALU = mybir.AluOpType
ACT = mybir.ActivationFunctionType
AX = mybir.AxisListType

P = 128
SEQ = 512
D = 1024
TT = SEQ // P
KD = D // P
COLS = 512
RING = 3
HD = 64
NA_H, FOX_H, CH_H = 4, 8, 8
GH = 4
LEVELS = 7
EPS, LN_EPS = 1e-6, 1e-5
NEG = -1e30
NBMAX = 2 * SEQ // P + 31

C_IDENT, C_ONES, C_FLIP = 0, 128, 256
C_LE, C_GE, C_GT, C_LT = 384, 512, 640, 768
C_CAUSAL, C_CHUNK = 896, 1024
C_LEVEL = 1152
C_WIN = C_LEVEL + 2 * LEVELS * 64
C_IOTA = C_WIN + 64
C_TOK = C_IOTA + 128
C_N = C_TOK + TT


def shape_constants():
    r = np.arange(P)[:, None]
    c = np.arange(P)[None, :]
    t = np.zeros((P, C_N), np.float32)
    t[:, C_IDENT:C_IDENT + P] = r == c
    t[:, C_ONES:C_ONES + P] = 1
    t[:, C_FLIP:C_FLIP + P] = r + c == P - 1
    t[:, C_LE:C_LE + P] = r <= c
    t[:, C_GE:C_GE + P] = r >= c
    t[:, C_GT:C_GT + P] = r > c
    t[:, C_LT:C_LT + P] = r < c
    t[:, C_CAUSAL:C_CAUSAL + P] = np.where(c <= r, 0, NEG)
    t[:, C_CHUNK:C_CHUNK + P] = np.where(c // 64 <= r // 64, 0, NEG)
    for s in range(LEVELS):
        b = 1 << s
        first = [n for n in range(P) if (n // b) % 2 == 0]
        second = [n for n in range(P) if (n // b) % 2 == 1]
        same = lambda n: (r[:, 0] // (2 * b)) == n // (2 * b)
        for d, (cols, half) in enumerate(((first, 1), (second, 0))):
            for j, n in enumerate(cols):
                at = C_LEVEL + (d * LEVELS + s) * 64 + j
                t[:, at] = same(n) & ((r[:, 0] // b) % 2 == half)
    q = r % 64
    start = np.clip(q - 8, 0, 48)
    k = np.arange(64)[None, :]
    t[:, C_WIN:C_WIN + 64] = np.where((k >= start) & (k < start + 16), 0, NEG)
    t[:, C_IOTA:C_IOTA + P] = c
    t[:, C_TOK:C_TOK + TT] = r + P * np.arange(TT)[None, :]
    return t


R_BADA, R_NMIX, R_NFFN, R_CONVA, R_GCONV, R_C, R_C2, R_END = 0, 48, 56, 64, 70, 106, 114, 122
R2_BADA, R2_CONVB, R2_END = 0, 48, 92
NCH = 44


class Link:

    def __init__(self, sem):
        self.sem, self.n = sem, 0

    def on(self, eng):
        def run(ins):
            self.n += 1
            ins.then_inc(self.sem, 1)
            eng.wait_ge(self.sem, self.n)
        return run


class Weights:

    def __init__(self, ring, arrived):
        self.ring, self.arrived = ring, arrived
        self.issued, self.used = 0, {}
        self.landed, self.full = [0] * RING, {}

    def slot(self, n):
        return self.ring[:, n % RING, :]

    def load(self, sp, n, *srcs):
        assert n == self.issued
        self.issued += 1
        if n - RING in self.used:
            sp.wait_ge(*self.used[n - RING])
        rows, width = srcs[0].shape[1], sum(src.shape[2] for src in srcs)
        dst = self.slot(n)[:, 0:rows * width].rearrange("p (k c) -> p k c", k=rows)
        at = 0
        for src in srcs:
            sp.dma_start(dst[:, :, at:at + src.shape[2]], src).then_inc(self.arrived[n % RING], 16)
            at += src.shape[2]
            self.landed[n % RING] += 16
        self.full[n] = self.landed[n % RING]

    def wait(self, pe, n):
        pe.wait_ge(self.arrived[n % RING], self.full[n])


class Kernel:
    def __init__(self, nc, ins, out):
        self.nc, self.i, self.out = nc, ins, out
        self.stage_sems = []

    def sb(self, ctx, name, shape, dt=F32):
        return ctx.enter_context(self.nc.sbuf_tensor(name, shape, dt))

    def sem(self, name):
        handle = self.nc.alloc_semaphore(name=name)
        self.stage_sems.append(handle)
        return handle

    def retire_semaphores(self):
        with self.nc.Block() as block:
            @block.gpsimd
            def _(pool):
                self.nc.clear_and_free_semaphores(self.stage_sems)
        self.stage_sems = []
        self.W.used = {}

    def cst(self, at, n=P):
        return self.const[:, at:at + n]

    def build(self):
        nc = self.nc
        with ExitStack() as root:
            self.root = root
            self.const = self.sb(root, "const", [P, C_N])
            self.X = self.sb(root, "X", [P, TT, D])
            self.HT = self.sb(root, "HT", [P, KD, SEQ])
            self.ring = self.sb(root, "ring", [P, RING, KD * COLS])
            self.cols1 = self.sb(root, "cols1", [P, P])
            self.cols2 = self.sb(root, "cols2", [P, P])
            self.cols3 = self.sb(root, "cols3", [P, 3 * NCH])
            self.mod = self.sb(root, "mod", [P, 48])
            self.modA = self.sb(root, "modA", [P, 2, KD])
            self.gate = self.sb(root, "gate", [P, D])
            self.psum = root.enter_context(nc.psum_tensor("psum", [P, 8, 512], F32))
            self.dve_link = Link(self.sem("dve_link"))
            self.act_link = Link(self.sem("act_link"))
            self.pool_link = Link(self.sem("pool_link"))
            self.W = Weights(self.ring, [self.sem(f"slot{j}_arrived") for j in range(RING)])
            self.stored = self.sem("stored")
            self.nstored = 0
            self.stage_sems = []
            self.stages()
            self.retire_semaphores()

    def stage_load(self):
        nc, i = self.nc, self.i
        self.loaded = self.sem("inputs_loaded")
        with ExitStack() as ctx:
            rows = self.sb(ctx, "rows", [P, 4, P])
            turned = self.sem("rows_turned")
            evac = self.sem("columns_ready")
            tile_rows = [R_END, R2_END, 2 * NCH, NCH]
            with nc.Block() as block:
                @block.sync
                def _(sp):
                    def vec(t, at, src, n):
                        sp.dma_start(rows[at:at + n, t, :], src.rearrange("(j p) -> j p", p=P)) \
                          .then_inc(self.loaded, 16)
                        count[0] += 16
                    count = [16]
                    sp.dma_start(self.const[:, :], i["shape_constants"]).then_inc(self.loaded, 16)
                    vec(0, R_BADA, i["b_ada"][0], 48)
                    vec(0, R_NMIX, i["norm_mix_w"][0], KD)
                    vec(0, R_NFFN, i["norm_ffn_w"][0], KD)
                    vec(0, R_CONVA, i["conv_a_w"][0].rearrange("k c -> (k c)"), 6)
                    vec(0, R_GCONV, i["gdn_conv_w"][0].rearrange("k c -> (k c)"), 36)
                    vec(0, R_C, i["c"][0], KD)
                    vec(0, R_C2, i["c_2"][0], KD)
                    vec(1, R2_BADA, i["b_ada_2"][0], 48)
                    vec(1, R2_CONVB, i["conv_b_2"][0], NCH)
                    vec(2, 0, i["conv_w_2"][0, 0:2].rearrange("k c -> (k c)"), 2 * NCH)
                    vec(3, 0, i["conv_w_2"][0, 2], NCH)
                    sp.dma_start(self.X[:, :, :], i["x"][0].rearrange("(t p) d -> p t d", p=P)) \
                      .then_inc(self.loaded, 16)
                    count[0] += 16
                    self.loaded_all = count[0]

                @block.tensor
                def _(pe):
                    pe.wait_ge(self.loaded, self.loaded_all)
                    for t, n in enumerate(tile_rows):
                        pe.transpose(self.psum[:, t, 0:n], rows[0:n, t, :],
                                     self.const[0:n, C_IDENT:C_IDENT + n]).then_inc(turned, 1)

                @block.vector
                def _(dve):
                    for t, (n, dst) in enumerate(zip(tile_rows, (
                            self.cols1[:, 0:R_END], self.cols2[:, 0:R2_END],
                            self.cols3[:, 0:2 * NCH], self.cols3[:, 2 * NCH:3 * NCH]))):
                        dve.wait_ge(turned, t + 1)
                        dve.tensor_copy(dst, self.psum[:, t, 0:n]).then_inc(evac, 1)

                @block.scalar
                def _(act):
                    act.wait_ge(evac, 1)
                    act.activation(self.cols1[:, R_C:R_END], self.cols1[:, R_C:R_END], ACT.Silu) \
                       .then_inc(evac, 1)

    def stage_mod(self, tag, w_ada, cond, b_ada):
        nc, W = self.nc, self.W
        base, n_loads = W.issued, 6 * D // COLS
        trips, per = n_loads // RING, COLS // P
        src = w_ada.rearrange("(k p) c -> p k c", p=P)
        used, copied = self.sem(f"{tag}_slots_used"), self.sem(f"{tag}_columns_copied")
        for n in range(n_loads):
            W.used[base + n] = (used, n + 1)
        slot3 = [W.slot(base + j).rearrange("p (k c) -> p k c", k=KD) for j in range(RING)]
        with nc.Block() as block:
            @block.sync
            def _(sp):
                for j in range(RING):
                    W.load(sp, base + j, src[:, :, j * COLS:(j + 1) * COLS])
                with sp.Fori(1, trips) as i:
                    for j in range(RING):
                        sp.wait_ge(used, i * RING + (j - RING + 1))
                        sp.dma_start(slot3[j], src[:, :, bass.ds(i * (RING * COLS) + j * COLS, COLS)]) \
                          .then_inc(W.arrived[(base + j) % RING], 16)
                W.issued = base + n_loads
                for j in range(RING):
                    W.landed[(base + j) % RING] += 16 * (trips - 1)

            @block.tensor
            def _(pe):
                def trip(i):
                    for j in range(RING):
                        pe.wait_ge(W.arrived[(base + j) % RING], i * 16 + W.full[base + j])
                        if not isinstance(i, int):
                            pe.wait_ge(copied, i * RING + (j - RING + 1))
                        for c in range(per):
                            for k in range(KD):
                                mm = pe.matmul(self.psum[:, j, c:c + 1], slot3[j][:, k, c * P:(c + 1) * P],
                                               cond[:, k:k + 1], start=(k == 0), stop=(k == KD - 1))
                        mm.then_inc(used, 1)
                trip(0)
                with pe.Fori(1, trips) as i:
                    trip(i)

            @block.vector
            def _(dve):
                with dve.Fori(0, trips) as i:
                    for j in range(RING):
                        cols = bass.ds(i * (RING * per) + j * per, per)
                        dve.wait_ge(used, i * RING + (j + 1))
                        dve.tensor_tensor(self.mod[:, cols], self.psum[:, j, 0:per], b_ada[:, cols],
                                          ALU.add).then_inc(copied, 1)

    def stage_gate(self, tag, at, plus=0.0):
        nc = self.nc
        with ExitStack() as ctx:
            diag = self.sb(ctx, f"{tag}_diag", [P, KD, P])
            ready, summed = self.sem(f"{tag}_diag_ready"), self.sem(f"{tag}_summed")
            with nc.Block() as block:
                @block.vector
                def _(dve):
                    for k in range(KD):
                        dve.tensor_scalar(diag[:, k, :], self.cst(C_IDENT), self.mod[:, at + k:at + k + 1],
                                          None, ALU.mult).then_inc(ready, 1)
                    for b in range(2):
                        dve.wait_ge(summed, 4 * b + 4)
                        dve.tensor_scalar(self.gate[:, b * 512:(b + 1) * 512], self.psum[:, b, :], plus,
                                          None, ALU.add)

                @block.tensor
                def _(pe):
                    for k in range(KD):
                        pe.wait_ge(ready, k + 1)
                        pe.matmul(self.psum[:, k // 4, (k % 4) * P:(k % 4 + 1) * P], self.cst(C_ONES),
                                  diag[:, k, :], start=True, stop=True).then_inc(summed, 1)

    def row_stats(self, block, tag, ctx, eps, mean):
        rstd = self.sb(ctx, f"{tag}_rstd", [P, TT])
        mu = self.sb(ctx, f"{tag}_mean", [P, TT, 2])
        var = self.sb(ctx, f"{tag}_var", [P, TT])
        junk = self.sb(ctx, f"{tag}_junk", [P, D])
        bn = self.sb(ctx, f"{tag}_bn", [P, TT, 2, 6])
        s_var, s_std = self.sem(f"{tag}_var_ready"), self.sem(f"{tag}_std_ready")

        def on_dve(dve):
            link = self.dve_link.on(dve)
            if mean:
                for t in range(TT):
                    for h in range(2):
                        link(dve.bn_stats(bn[:, t, h, :], self.X[:, t, h * 512:(h + 1) * 512]))
                    link(dve.bn_aggr(mu[:, t, :], bn[:, t, :, :].rearrange("p h s -> p (h s)")))
                dve.tensor_scalar(var[:, :], mu[:, :, 1], eps, None, ALU.add).then_inc(s_var, TT)
            else:
                dve.wait_ge(s_var, TT)
                link(dve.tensor_scalar(var[:, :], var[:, :], 1.0 / D, eps, ALU.mult, ALU.add))
                dve.sem_inc(s_std, 1)
            dve.wait_ge(s_std, 2 - (1 if mean else 0))
            link(dve.reciprocal(rstd[:, :], var[:, :]))

        def on_act(act):
            if mean:
                act.wait_ge(s_var, TT)
            else:
                link = self.act_link.on(act)
                for t in range(TT):
                    link(act.activation(junk[:, :], self.X[:, t, :], ACT.Square,
                                        accum_out=var[:, t:t + 1]))
                act.sem_inc(s_var, TT)
                act.wait_ge(s_std, 1)
            act.activation(var[:, :], var[:, :], ACT.Sqrt).then_inc(s_std, 1)

        return rstd, mu, on_dve, on_act

    def stage_norm(self, tag, eps, mean, scale, shift, save_rows=None):
        nc = self.nc
        with ExitStack() as ctx:
            XN = self.sb(ctx, f"{tag}_XN", [P, TT, D])
            normed, turned, filled = (self.sem(f"{tag}_{n}") for n in ("rows_normed", "turned", "filled"))
            with nc.Block() as block:
                rstd, mu, stats_dve, stats_act = self.row_stats(block, tag, ctx, eps, mean)

                @block.vector
                def _(dve):
                    stats_dve(dve)
                    for t in range(TT):
                        if mean:
                            ins = dve.tensor_scalar(XN[:, t, :], self.X[:, t, :], mu[:, t, 0:1],
                                                    rstd[:, t:t + 1], ALU.subtract, ALU.mult)
                        else:
                            ins = dve.tensor_scalar(XN[:, t, :], self.X[:, t, :], rstd[:, t:t + 1],
                                                    None, ALU.mult)
                        ins.then_inc(normed, 1)
                    for k in range(0, KD, 2):
                        dve.wait_ge(turned, k + 1)
                        dve.tensor_scalar(self.HT[:, k, :], self.psum[:, k, :], scale[:, k:k + 1],
                                          shift[:, k:k + 1], ALU.mult, ALU.add).then_inc(filled, 1)

                @block.tensor
                def _(pe):
                    pe.wait_ge(normed, TT)
                    for k in range(KD):
                        for t in range(TT):
                            tr = pe.transpose(self.psum[:, k, t * P:(t + 1) * P],
                                              XN[:, t, k * P:(k + 1) * P], self.cst(C_IDENT))
                        tr.then_inc(turned, 1)

                @block.scalar
                def _(act):
                    stats_act(act)
                    for k in range(1, KD, 2):
                        act.wait_ge(turned, k + 1)
                        act.activation(self.HT[:, k, :], self.psum[:, k, :], ACT.Identity,
                                       scale=scale[:, k:k + 1], bias=shift[:, k:k + 1]).then_inc(filled, 1)

                @block.sync
                def _(sp):
                    if save_rows is not None:
                        sp.wait_ge(normed, TT)
                        self.nstored += 16
                        sp.dma_start(save_rows.rearrange("(t p) d -> p t d", p=P), XN[:, :, :]) \
                          .then_inc(self.stored, 16)
                        sp.wait_ge(self.stored, self.nstored)

    def stage_scale(self, tag, gain, scale_at):
        nc = self.nc
        with nc.Block() as block:
            @block.vector
            def _(dve):
                link = self.dve_link.on(dve)
                link(dve.tensor_scalar(self.modA[:, 0, :], self.mod[:, scale_at:scale_at + KD], 1.0, None,
                                       ALU.add))
                if gain is not None:
                    link(dve.tensor_tensor(self.modA[:, 0, :], self.modA[:, 0, :], gain, ALU.mult))

    def stage_proj1(self, B):
        nc, W = self.nc, self.W
        w = self.i["w_in"][0].rearrange("(k p) c -> p k c", p=P)
        base = W.issued
        GAB_AT = 3584
        loads = [(n * COLS, COLS) for n in range(7)] + [(GAB_AT, 16)]
        items = []
        for n, names in enumerate((("cb", "cb", "cc", "cc"), ("cx", "cx", "nq", "nq"), ("nk", "nk", None, None))):
            items += [(n, what, c, c % 2) for c, what in enumerate(names) if what]
        items += [(2, "nv", t, t) for t in range(TT)]
        items += [(3 + n, "g", c, 4 * n + c) for n in range(3) for c in range(4)]
        items += [(6, "gz", t, t) for t in range(TT)] + [(7, "gab", t, t) for t in range(TT)]
        last = {it[0]: n for n, it in enumerate(items)}
        BANKS = 6
        with ExitStack() as ctx:
            CB = self.sb(ctx, "CB", [P, 2, SEQ])
            CC = self.sb(ctx, "CC", [P, 2, SEQ])
            PAD = self.sb(ctx, "PAD", [P, 4, SEQ + 2])
            CV = self.sb(ctx, "CV", [P, 2, SEQ])
            summed, copied = self.sem("proj1_summed"), self.sem("proj1_copied")
            zeroed, conved, silued = self.sem("pads_zeroed"), self.sem("conv_done"), self.sem("silu_done")
            for ld in last:
                W.used[base + ld] = (summed, last[ld] + 1)
            convs = [n for n, it in enumerate(items) if it[1] in ("cx", "g")]
            with nc.Block() as block:
                @block.sync
                def _(sp):
                    for n, (at, width) in enumerate(loads):
                        W.load(sp, base + n, w[:, :, at:at + width])

                @block.tensor
                def _(pe):
                    for n, (ld, what, c, _) in enumerate(items):
                        if n == 0 or items[n - 1][0] != ld:
                            W.wait(pe, base + ld)
                        if n >= BANKS:
                            pe.wait_ge(copied, n - BANKS + 1)
                        width = loads[ld][1]
                        slot = W.slot(base + ld)[:, 0:KD * width].rearrange("p (k c) -> p k c", k=KD)
                        bank = self.psum[:, n % BANKS, :]
                        for k in range(KD):
                            if what in ("nv", "gz", "gab"):
                                cols = slice(256, 512) if what == "nv" else slice(0, width)
                                wk = slot[:, k, cols]
                                mm = pe.matmul(bank[:, 0:wk.shape[1]], self.HT[:, k, c * P:(c + 1) * P], wk,
                                               start=(k == 0), stop=(k == KD - 1))
                            else:
                                mm = pe.matmul(bank, slot[:, k, c * P:(c + 1) * P], self.HT[:, k, :],
                                               start=(k == 0), stop=(k == KD - 1))
                        mm.then_inc(summed, 1)

                @block.scalar
                def _(act):
                    act.wait_ge(zeroed, 1)
                    def silu(m):
                        if m >= 2:
                            act.wait_ge(conved, m + 1)
                            act.activation(B.G[:, m - 2, :], CV[:, m % 2, :], ACT.Silu).then_inc(silued, 1)
                    m = 0
                    for n, (_, what, c, at) in enumerate(items):
                        act.wait_ge(summed, n + 1)
                        bank = self.psum[:, n % BANKS, :]
                        if what in ("cx", "g"):
                            if m >= 4:
                                act.wait_ge(conved, m - 3)
                            dst = PAD[:, m % 4, 1:SEQ + 1]
                        else:
                            dst = {"cb": CB, "cc": CC, "nq": B.NQ, "nk": B.NK, "nv": B.NV, "gz": B.GZ,
                                   "gab": B.GAB}[what][:, at, :]
                        act.activation(dst, bank[:, 0:dst.shape[1]], ACT.Copy,
                                       scale=HD ** -0.5 if what == "nq" else 1.0).then_inc(copied, 1)
                        if what in ("cx", "g"):
                            m += 1
                            if m >= 2:
                                silu(m - 2)
                    silu(m - 2)
                    silu(m - 1)

                @block.vector
                def _(dve):
                    link = self.dve_link.on(dve)
                    dve.memset(PAD[:, :, :], 0.0).then_inc(zeroed, 1)
                    for m, n in enumerate(convs):
                        what, at = items[n][1], items[n][3]
                        dve.wait_ge(copied, n + 1)
                        src = PAD[:, m % 4, :]
                        if what == "cx":
                            link(dve.tensor_tensor(src[:, 1:SEQ + 1], src[:, 1:SEQ + 1], CC[:, at, :], ALU.mult))
                            tap = lambda j: self.cols1[:, R_CONVA + 2 * j + at:R_CONVA + 2 * j + at + 1]
                        else:
                            tap = lambda j: self.cols1[:, R_GCONV + 12 * j + at:R_GCONV + 12 * j + at + 1]
                        if m >= 4:
                            dve.wait_ge(silued, m - 3)
                        cv = CV[:, m % 2, :]
                        link(dve.tensor_scalar(cv, src[:, 0:SEQ], tap(0), None, ALU.mult))
                        link(dve.scalar_tensor_tensor(cv, src[:, 1:SEQ + 1], tap(1), cv, ALU.mult, ALU.add))
                        ins = dve.scalar_tensor_tensor(cv, src[:, 2:SEQ + 2], tap(2), cv, ALU.mult, ALU.add)
                        if what == "cx":
                            link(ins)
                            dve.tensor_tensor(B.YT[:, at, :], CB[:, at, :], cv, ALU.mult).then_inc(conved, 1)
                        else:
                            ins.then_inc(conved, 1)

    def stage_attention(self, tag, heads, qT, kT, vals, bias, width, outT, cum=None):
        nc = self.nc
        units = [(h, t) for h in range(heads) for t in range(TT)]
        N = len(units)
        with ExitStack() as ctx:
            S = self.sb(ctx, f"{tag}_S", [P, 2, SEQ])
            PR = self.sb(ctx, f"{tag}_PR", [P, 2, SEQ])
            PT = self.sb(ctx, f"{tag}_PT", [P, 2, TT, SEQ])
            mx = self.sb(ctx, f"{tag}_max", [P, N])
            sm = self.sb(ctx, f"{tag}_sum", [P, N])
            DEC = self.sb(ctx, f"{tag}_decay", [P, 2, SEQ]) if cum else None
            names = "scored maxed exped normed turned kept valued headed rowed biased"
            scored, maxed, exped, normed, turned, kept, valued, headed, rowed, biased = (
                self.sem(f"{tag}_{n}") for n in names.split())
            score_bank = lambda u: self.psum[:, u % 2, :]
            turn_bank = lambda u: self.psum[:, 2 + u % 2, :]
            out_bank = lambda h: self.psum[:, 4 + h % 2, :]
            row_bank = lambda h: self.psum[:, 6 + h % 2, :]
            def head_out(dve, h):
                at = HD * (h % 2)
                dve.wait_ge(valued, h + 1)
                dve.tensor_copy(outT(h), out_bank(h)[at:at + HD, :]).then_inc(headed, 1)

            with nc.Block() as block:
                @block.tensor
                def _(pe):
                    def scores(u):
                        h, t = units[u]
                        if cum and t == 0:
                            if h >= 2:
                                pe.wait_ge(biased, TT * (h - 1))
                            pe.matmul(row_bank(h), cum[1](h), cum[2], start=True, stop=True).then_inc(rowed, 1)
                        if u >= 2:
                            pe.wait_ge(maxed, u - 1)
                        w = width(t)
                        mm = pe.matmul(score_bank(u)[:, 0:w], qT(h)[:, t * P:(t + 1) * P], kT(h)[:, 0:w],
                                       start=True, stop=not cum)
                        if cum:
                            mm = pe.matmul(score_bank(u)[:, w - P:w], self.cst(C_IDENT), self.cst(C_CAUSAL),
                                           start=False, stop=True)
                        mm.then_inc(scored, 1)

                    def turn(u):
                        h, t = units[u]
                        pe.wait_ge(normed, u + 1)
                        if u >= 2:
                            pe.wait_ge(kept, u - 1)
                        for j in range(width(t) // P):
                            tr = pe.transpose(turn_bank(u)[:, j * P:(j + 1) * P], PR[:, u % 2, j * P:(j + 1) * P],
                                              self.cst(C_IDENT))
                        tr.then_inc(turned, 1)

                    def values(h):
                        pe.wait_ge(kept, TT * (h + 1))
                        if h >= 2:
                            pe.wait_ge(headed, h - 1)
                        at = HD * (h % 2)
                        for j in range(TT):
                            q0 = 0 if width(0) == SEQ else j * P
                            mm = pe.matmul(out_bank(h)[at:at + HD, q0:], vals(h, j), PT[:, h % 2, j, q0:],
                                           start=(j == 0), stop=(j == TT - 1))
                        mm.then_inc(valued, 1)

                    scores(0)
                    for u in range(N):
                        if u + 1 < N:
                            scores(u + 1)
                        turn(u)
                        if u >= TT and u % TT == 0:
                            values(u // TT - 1)
                    values(heads - 1)

                @block.vector
                def _(dve):
                    link = self.dve_link.on(dve)

                    def top(u):
                        h, t = units[u]
                        w = width(t)
                        dve.wait_ge(scored, u + 1)
                        if cum:
                            dve.wait_ge(biased, u + 1)
                        if u >= 2:
                            dve.wait_ge(exped, u - 1)
                        add = DEC[:, u % 2, 0:w] if cum else bias(h, t)
                        s, b = S[:, u % 2, 0:w], score_bank(u)[:, 0:w]
                        if len(add.shape) == 3:
                            g = add.shape[1]
                            s, b = (x.rearrange("p (g k) -> p g k", g=g) for x in (s, b))
                        link(dve.tensor_tensor_reduce(s, b, add, 1.0, -3e38, ALU.add, ALU.max, mx[:, u:u + 1]))
                        dve.tensor_scalar(mx[:, u:u + 1], mx[:, u:u + 1], -1.0, None, ALU.mult).then_inc(maxed, 1)

                    def norm(u):
                        w = width(units[u][1])
                        dve.wait_ge(exped, u + 1)
                        link(dve.reciprocal(sm[:, u:u + 1], sm[:, u:u + 1]))
                        dve.tensor_scalar(PR[:, u % 2, 0:w], PR[:, u % 2, 0:w], sm[:, u:u + 1], None, ALU.mult) \
                           .then_inc(normed, 1)

                    top(0)
                    for u in range(N):
                        if u + 1 < N:
                            top(u + 1)
                        norm(u)
                        if u % TT == 0 and u >= TT:
                            head_out(dve, u // TT - 1)
                    head_out(dve, heads - 1)

                @block.scalar
                def _(act):
                    def decay(u):
                        h, t = units[u]
                        w = width(t)
                        act.wait_ge(rowed, h + 1)
                        if u >= 2:
                            act.wait_ge(maxed, u - 1)
                        act.activation(DEC[:, u % 2, 0:w], row_bank(h)[:, 0:w], ACT.Identity, scale=-1.0,
                                       bias=cum[0](t, h)).then_inc(biased, 1)

                    def exps(u):
                        w = width(units[u][1])
                        act.wait_ge(maxed, u + 1)
                        if u >= 2:
                            act.wait_ge(turned, u - 1)
                        act.activation(PR[:, u % 2, 0:w], S[:, u % 2, 0:w], ACT.Exp, bias=mx[:, u:u + 1],
                                       accum_out=sm[:, u:u + 1]).then_inc(exped, 1)

                    def keep(u):
                        h, t = units[u]
                        w = width(t)
                        act.wait_ge(turned, u + 1)
                        if h >= 2:
                            act.wait_ge(valued, h - 1)
                        act.activation(PT[:, h % 2, 0:w // P, t * P:(t + 1) * P],
                                       turn_bank(u)[:, 0:w].rearrange("p (j q) -> p j q", q=P), ACT.Copy) \
                           .then_inc(kept, 1)

                    if cum:
                        decay(0)
                        decay(1)
                    exps(0)
                    for u in range(N):
                        if u + 1 < N:
                            if cum and u + 2 < N:
                                decay(u + 2)
                            exps(u + 1)
                        keep(u)

    def stage_na(self, B):
        nc = self.nc
        NR, HEADW = 14, 127
        with ExitStack() as ctx:
            hank = self.HT[:, :, :].rearrange("p k s -> p (k s)")[:, 0:NA_H * NR * 64]
            bias = self.sb(ctx, "na_bias", [P, NA_H, NR, 64])
            laid, flipped = self.sem("na_bias_laid"), self.sem("na_bias_flipped")
            made = self.sem("na_bias_made")
            half = 7 * 64
            with nc.Block() as block:
                @block.sync
                def _(sp):
                    src = self.i["na_rpb"]
                    for part in range(2):
                        for h in range(NA_H):
                            sp.dma_start(
                                hank[part * 64:(part + 1) * 64, h * NR * 64:(h + 1) * NR * 64]
                                .rearrange("p (r c) -> p r c", r=NR),
                                bass.AP(src.tensor, (h * 15 + part) * HEADW, [[1, 64], [HEADW, NR], [1, 64]])) \
                              .then_inc(laid, 16)

                @block.tensor
                def _(pe):
                    pe.wait_ge(laid, 2 * NA_H * 16)
                    for j in range(2 * NA_H):
                        pe.matmul(self.psum[:, j, 0:half], self.cst(C_FLIP), hank[:, j * half:(j + 1) * half],
                                  start=True, stop=True).then_inc(flipped, 1)

                @block.vector
                def _(dve):
                    win = self.cst(C_WIN, 64).unsqueeze(1).to_broadcast([P, 7, 64])
                    for j in range(2 * NA_H):
                        dve.wait_ge(flipped, j + 1)
                        dve.tensor_tensor(bias[:, j // 2, (j % 2) * 7:(j % 2 + 1) * 7, :],
                                          self.psum[:, j, 0:half].rearrange("p (r c) -> p r c", r=7), win,
                                          ALU.add).then_inc(made, 1)
            rows = lambda h: slice(HD * (h % 2), HD * (h % 2 + 1))
            self.stage_attention(
                "na", NA_H, lambda h: B.NQ[rows(h), h // 2, :], lambda h: B.NK[rows(h), h // 2, :],
                lambda h, j: B.NV[:, j, h * HD:(h + 1) * HD],
                lambda h, t: bias[:, h, 6 - 2 * t:14 - 2 * t, :].rearrange("p r c -> p (r c)"),
                lambda t: SEQ, lambda h: B.YT[rows(h), 2 + h // 2, :])

    def stage_gdn_prep(self, B, ctx):
        nc, i = self.nc, self.i
        slot = lambda n: self.ring[:, n, :]
        B.LKK = slot(0)[:, 0:2048].rearrange("p (t h j) -> p t h j", t=TT, h=GH)
        B.KQ = slot(0)[:, 2048:4096].rearrange("p (t h j) -> p t h j", t=TT, h=GH)
        flat = self.HT[:, :, :].rearrange("p k s -> p (k s)")
        B.KR = flat[:, 0:2048].rearrange("p (t h c) -> p t h c", t=TT, h=GH)
        B.VR = flat[:, 2048:4096].rearrange("p (t h c) -> p t h c", t=TT, h=GH)
        SQ = slot(2).rearrange("p (c s) -> p c s", c=8)
        alog = self.sb(ctx, "a_log", [P, 8])
        dtb = self.sb(ctx, "dt_bias", [P, 8])
        B.gnw = self.sb(ctx, "gdn_norm_gain", [P, P])
        B.g = self.sb(ctx, "g", [P, TT, 8])
        B.beta = self.sb(ctx, "beta", [P, TT, 8])
        B.rqk = self.sb(ctx, "rqk", [P, TT, 8])
        B.ex = self.sb(ctx, "decays", [P, 3, TT, 8])
        B.brk = self.sb(ctx, "beta_rk", [P, TT, 8])
        B.beG = self.sb(ctx, "beta_decay", [P, TT, 8])
        B.req = self.sb(ctx, "rq_decay", [P, TT, 8])
        tmp = self.sb(ctx, "softplus_tmp", [P, 4, TT * 8])
        names = "loaded squared summed rooted minus_abs exped summed_g exped_g tiled evacuated sigmoided v_copied"
        (loaded, squared, summed, rooted, absed, exped, summed_g, exped_g, tiled, evac, sigm, vcop) = (
            self.sem("gp_" + n) for n in names.split())
        with nc.Block() as block:
            @block.sync
            def _(sp):
                for dst, src, n in ((alog, i["gdn_a_log"], 8), (dtb, i["gdn_dt_bias"], 8), (B.gnw, i["gdn_norm_w"], P)):
                    sp.dma_start(dst[:, :], bass.AP(src.tensor, 0, [[0, P], [1, n]])).then_inc(loaded, 16)

            @block.scalar
            def _(act):
                for c in range(8):
                    act.activation(SQ[:, c, :], B.G[:, c, :], ACT.Square).then_inc(squared, 1)
                act.wait_ge(rooted, 1)
                act.activation(B.rqk[:, :, :], B.rqk[:, :, :], ACT.Sqrt).then_inc(rooted, 1)
                act.activation(B.beta[:, :, :], B.GAB[:, :, 8:16], ACT.Sigmoid).then_inc(sigm, 1)
                act.wait_ge(absed, 1)
                act.activation(tmp[:, 1, :], tmp[:, 1, :], ACT.Exp, scale=-1.0).then_inc(exped, 1)
                act.wait_ge(loaded, 48)
                act.activation(alog[:, :], alog[:, :], ACT.Exp).then_inc(exped, 1)
                act.wait_ge(summed_g, 1)
                act.activation(B.ex[:, :, :, :].rearrange("p a t h -> p (a t h)"), self.psum[:, 6, 0:96], ACT.Exp) \
                   .then_inc(exped_g, 1)
                for t in range(TT):
                    act.wait_ge(tiled, t + 1)
                    act.activation(B.VR[:, t, :, :].rearrange("p h c -> p (h c)"), self.psum[:, 1, :], ACT.Copy) \
                       .then_inc(vcop, 1)

            @block.tensor
            def _(pe):
                pe.wait_ge(squared, 8)
                for t in range(TT):
                    for c in range(8):
                        mm = pe.matmul(self.psum[:, 7, t * 8 + c:t * 8 + c + 1], SQ[:, c, t * P:(t + 1) * P],
                                       self.cst(C_ONES, 1), start=True, stop=True)
                mm.then_inc(summed, 1)
                pe.wait_ge(evac, 1)
                for t in range(TT):
                    for d in range(2):
                        for kind, tri in enumerate(((C_LE, C_GE)[d], (C_GT, C_LT)[d], C_ONES)):
                            at = kind * 32 + t * 8 + d * 4
                            mm = pe.matmul(self.psum[:, 6, at:at + 4], self.cst(tri), B.g[:, t, d * 4:d * 4 + 4],
                                           start=True, stop=True)
                mm.then_inc(summed_g, 1)
                for t in range(TT):
                    cols = slice(t * P, (t + 1) * P)
                    if t:
                        pe.wait_ge(evac, 1 + t)
                        pe.wait_ge(vcop, t)
                    for h in range(GH):
                        to = slice(h * P, (h + 1) * P)
                        kt, qt = B.G[:, 4 + h, cols], B.G[:, h, cols]
                        pe.transpose(self.psum[:, 0, to], kt, self.cst(C_IDENT))
                        pe.transpose(self.psum[:, 1, to], B.G[:, 8 + h, cols], self.cst(C_IDENT))
                        pe.matmul(self.psum[:, 2, to], kt, kt, start=True, stop=True)
                        mm = pe.matmul(self.psum[:, 3, to], kt, qt, start=True, stop=True)
                    mm.then_inc(tiled, 1)

            @block.vector
            def _(dve):
                link = self.dve_link.on(dve)
                dve.wait_ge(summed, 1)
                link(dve.tensor_scalar(B.rqk[:, :, :].rearrange("p t c -> p (t c)"), self.psum[:, 7, 0:32], EPS,
                                       None, ALU.add))
                dve.sem_inc(rooted, 1)
                x, u, s2, acc = (tmp[:, n, :] for n in range(4))
                xt = x.rearrange("p (t c) -> p t c", t=TT)
                dve.wait_ge(loaded, 48)
                link(dve.tensor_tensor(xt, B.GAB[:, :, 0:8], dtb[:, :].unsqueeze(1).to_broadcast([P, TT, 8]), ALU.add))
                link(dve.tensor_scalar(u, x, -1.0, None, ALU.mult))
                link(dve.tensor_tensor(u, u, x, ALU.max))
                dve.sem_inc(absed, 1)
                dve.wait_ge(exped, 1)
                self.log1p(dve, link, u, s2, acc, acc)
                link(dve.scalar_tensor_tensor(x, x, 0.0, acc, ALU.max, ALU.add))
                dve.wait_ge(exped, 2)
                link(dve.scalar_tensor_tensor(B.g[:, :, :], xt, -1.0,
                                              alog[:, :].unsqueeze(1).to_broadcast([P, TT, 8]), ALU.mult, ALU.mult))
                dve.sem_inc(evac, 1)
                dve.wait_ge(rooted, 2)
                link(dve.reciprocal(B.rqk[:, :, :], B.rqk[:, :, :]))
                link(dve.tensor_scalar(B.rqk[:, :, 0:4], B.rqk[:, :, 0:4], 128 ** -0.5, None, ALU.mult))
                rk = lambda t: B.rqk[:, t, 4:8].unsqueeze(2).to_broadcast([P, GH, P])
                for t in range(TT):
                    dve.wait_ge(tiled, t + 1)
                    for bank, dst in ((0, B.KR), (2, B.LKK), (3, B.KQ)):
                        ins = dve.tensor_tensor(dst[:, t, :, :],
                                                self.psum[:, bank, :].rearrange("p (h j) -> p h j", h=GH), rk(t), ALU.mult)
                    ins.then_inc(evac, 1)
                dve.wait_ge(sigm, 1)
                dve.wait_ge(exped_g, 1)
                for d in range(2):
                    at = slice(4 * d, 4 * d + 4)
                    dve.tensor_tensor(B.brk[:, :, at], B.beta[:, :, at], B.rqk[:, :, 4:8], ALU.mult)
                    dve.tensor_tensor(B.req[:, :, at], B.ex[:, 0, :, at], B.rqk[:, :, 0:4], ALU.mult)
                dve.tensor_tensor(B.beG[:, :, :], B.ex[:, 0, :, :], B.beta[:, :, :], ALU.mult)

    def stage_gdn(self, B):
        nc = self.nc
        PAIRS = [(n, d) for n in range(TT) for d in range(2)]
        tile_of = lambda n, d: n if d == 0 else TT - 1 - n
        bc = lambda ap: ap.unsqueeze(2).to_broadcast([P, GH, P])
        over = lambda ap: ap.unsqueeze(1).to_broadcast([P, GH, P])

        def half(x, s, sel):
            return x.rearrange("p (g two b) -> p g two b", two=2, b=1 << s)[:, :, sel, :]

        def split(x, s):
            return x.rearrange("p (g b) -> p g b", b=1 << s)

        with ExitStack() as ctx:
            quad = [P, 2, GH, P]
            E = self.sb(ctx, "gdn_decay", quad)
            LT, IT = self.sb(ctx, "gdn_LT", quad), self.sb(ctx, "gdn_IT", quad)
            T, U = self.sb(ctx, "gdn_T", quad), self.sb(ctx, "gdn_TT", quad)
            VB, KB, KE = self.sb(ctx, "gdn_vb", quad), self.sb(ctx, "gdn_kb", quad), self.sb(ctx, "gdn_ke", quad)
            NW, VN = self.sb(ctx, "gdn_negw", quad), self.sb(ctx, "gdn_vnew", quad)
            S = self.sb(ctx, "gdn_state", quad)
            OT = self.sb(ctx, "gdn_out_tmp", [P, 2, GH, P])
            Y = [self.ring[:, 2 - d, 0:LEVELS * 512].rearrange("p (s h c) -> p s h c", s=LEVELS, h=GH) for d in range(2)]
            names = ("masked diffed decayed decay_masked products y_summed y_kept z_summed updated inited scaled "
                     "w_summed w_kept v_summed v_kept o_summed state_done out_done cleared")
            (masked, diffed, decayed, dmasked, products, y_summed, y_kept, z_summed, updated, inited, scaled,
             w_summed, w_kept, v_summed, v_kept, o_summed, state_done, out_done, cleared) = (
                self.sem("gdn_" + n) for n in names.split())
            bank = lambda d, n: self.psum[:, 4 * d + n, :]
            heads = lambda x: x.rearrange("p (h c) -> p h c", h=GH)
            idx = lambda n, s, d: (n * LEVELS + s) * 2 + d
            zeros = self.sb(ctx, "gdn_zeros", [P, 512])
            with nc.Block() as block:
                @block.sync
                def _(sp):
                    sp.wait_ge(cleared, 5)
                    lo = 2 * SEQ // P
                    rows = self.ys[lo * P:NBMAX * P, :].rearrange("(n p) d -> p n d", p=P)
                    for c in range(2):
                        self.nstored += 16
                        sp.dma_start(rows[:, :, c * 512:(c + 1) * 512],
                                     zeros[:, :].unsqueeze(1).to_broadcast([P, NBMAX - lo, 512])) \
                          .then_inc(self.stored, 16)
                    sp.wait_ge(self.stored, self.nstored)

                @block.gpsimd
                def _(pool):
                    for d in range(2):
                        pool.memset(self.ring[:, 2 - d, 0:LEVELS * 512], 0.0).then_inc(cleared, 1)
                        pool.memset(S[:, d, :, :], 0.0).then_inc(cleared, 1)
                    pool.memset(zeros[:, :], 0.0).then_inc(cleared, 1)
                    for q, (n, d) in enumerate(PAIRS):
                        t = tile_of(n, d)
                        if n:
                            pool.wait_ge(products, q - 1)
                        pool.tensor_tensor(E[:, d, :, :], over(self.cst((C_GT, C_LT)[d])),
                                           bc(B.g[:, t, 4 * d:4 * d + 4]), ALU.mult).then_inc(masked, 1)
                        if d == 1:
                            for dd in range(2):
                                qq = q - 1 + dd
                                tt = tile_of(n, dd)
                                pool.wait_ge(decayed, qq + 1)
                                pool.tensor_tensor(E[:, dd, :, :], E[:, dd, :, :],
                                                   over(self.cst((C_LE, C_GE)[dd])), ALU.mult).then_inc(dmasked, 1)
                            for dd in range(2):
                                qq = q - 1 + dd
                                tt = tile_of(n, dd)
                                hs = slice(4 * dd, 4 * dd + 4)
                                if n:
                                    pool.wait_ge(o_summed, qq - 1)
                                pool.tensor_tensor(VB[:, dd, :, :], B.VR[:, tt, :, :], bc(B.beta[:, tt, hs]), ALU.mult)
                                pool.tensor_tensor(KB[:, dd, :, :], B.KR[:, tt, :, :], bc(B.beG[:, tt, hs]), ALU.mult)
                                pool.tensor_tensor(KE[:, dd, :, :], B.KR[:, tt, :, :], bc(B.ex[:, 1, tt, hs]),
                                                   ALU.mult).then_inc(scaled, 1)

                @block.scalar
                def _(act):
                    for n in range(TT):
                        for d in range(2):
                            q = 2 * n + d
                            act.wait_ge(diffed, q + 1)
                            act.activation(E[:, d, :, :], heads(bank(d, 0)), ACT.Exp).then_inc(decayed, 1)
                        for d in range(2):
                            q = 2 * n + d
                            act.wait_ge(w_summed, q + 1)
                            act.activation(NW[:, d, :, :], heads(bank(d, 0)), ACT.Copy, scale=-1.0).then_inc(w_kept, 1)
                        for d in range(2):
                            q = 2 * n + d
                            act.wait_ge(v_summed, q + 1)
                            act.activation(VN[:, d, :, :], heads(bank(d, 2)), ACT.Copy).then_inc(v_kept, 1)

                @block.tensor
                def _(pe):
                    pe.wait_ge(cleared, 4)
                    for n in range(TT):
                        for d in range(2):
                            q = 2 * n + d
                            pe.wait_ge(masked, q + 1)
                            if n:
                                pe.wait_ge(out_done, q - 1)
                            for h in range(GH):
                                mm = pe.matmul(bank(d, 0)[:, h * P:(h + 1) * P], E[:, d, h, :],
                                               self.cst((C_LE, C_GE)[d]), start=True, stop=True)
                            mm.then_inc(diffed, 1)
                        for s in range(LEVELS):
                            for d in range(2):
                                q = 2 * n + d
                                if s == 0:
                                    pe.wait_ge(products, q + 1)
                                    pe.wait_ge(inited, q + 1)
                                else:
                                    pe.wait_ge(updated, idx(n, s - 1, d) + 1)
                                for h in range(GH):
                                    mm = pe.matmul(split(bank(d, 1)[:, h * 64:(h + 1) * 64], s), LT[:, d, h, :],
                                                   half(T[:, d, h, :], s, d), start=True, stop=True)
                                mm.then_inc(y_summed, 1)
                            for d in range(2):
                                pe.wait_ge(y_kept, idx(n, s, d) + 1)
                                for h in range(GH):
                                    pe.matmul(split(bank(d, 2)[:, h * 64:(h + 1) * 64], s), U[:, d, h, :],
                                              half(Y[d][:, s, h, :], s, d), start=True, stop=True)
                                    mm = pe.matmul(split(bank(d, 2)[:, 256 + h * 64:256 + (h + 1) * 64], s),
                                                   Y[d][:, s, h, :], half(U[:, d, h, :], s, 1 - d),
                                                   start=True, stop=True)
                                mm.then_inc(z_summed, 1)
                        for d in range(2):
                            q = 2 * n + d
                            pe.wait_ge(updated, idx(n, LEVELS - 1, d) + 1)
                            pe.wait_ge(scaled, q + 1)
                            for h in range(GH):
                                mm = pe.matmul(bank(d, 0)[:, h * P:(h + 1) * P], KB[:, d, h, :], U[:, d, h, :],
                                               start=True, stop=True)
                            mm.then_inc(w_summed, 1)
                        for d in range(2):
                            q = 2 * n + d
                            cols = slice(tile_of(n, d) * P, (tile_of(n, d) + 1) * P)
                            pe.wait_ge(w_kept, q + 1)
                            if n:
                                pe.wait_ge(state_done, q - 1)
                            for h in range(GH):
                                to = slice(h * P, (h + 1) * P)
                                pe.matmul(bank(d, 1)[:, to], B.G[:, h, cols], S[:, d, h, :], start=True, stop=True)
                                pe.matmul(bank(d, 2)[:, to], U[:, d, h, :], VB[:, d, h, :], start=True, stop=False)
                                mm = pe.matmul(bank(d, 2)[:, to], NW[:, d, h, :], S[:, d, h, :],
                                               start=False, stop=True)
                            mm.then_inc(v_summed, 1)
                        for d in range(2):
                            q = 2 * n + d
                            pe.wait_ge(v_kept, q + 1)
                            for h in range(GH):
                                to = slice(h * P, (h + 1) * P)
                                pe.matmul(bank(d, 0)[:, to], IT[:, d, h, :], VN[:, d, h, :], start=True, stop=True)
                                mm = pe.matmul(bank(d, 3)[:, to], KE[:, d, h, :], VN[:, d, h, :],
                                               start=True, stop=True)
                            mm.then_inc(o_summed, 1)

                @block.vector
                def _(dve):
                    link = self.dve_link.on(dve)
                    dve.wait_ge(cleared, 4)
                    for n in range(TT):
                        for d in range(2):
                            q, t = 2 * n + d, tile_of(n, d)
                            if n:
                                dve.wait_ge(o_summed, q - 1)
                            for X in (T, U):
                                ins = dve.tensor_copy(X[:, d, :, :], over(self.cst(C_IDENT)))
                            ins.then_inc(inited, 1)
                            dve.wait_ge(dmasked, q + 1)
                            dve.tensor_tensor(LT[:, d, :, :], E[:, d, :, :], B.LKK[:, t, :, :], ALU.mult)
                            dve.tensor_tensor(IT[:, d, :, :], E[:, d, :, :], B.KQ[:, t, :, :], ALU.mult) \
                               .then_inc(products, 1)
                        for s in range(LEVELS):
                            for d in range(2):
                                t = tile_of(n, d)
                                at = C_LEVEL + (d * LEVELS + s) * 64
                                dve.wait_ge(y_summed, idx(n, s, d) + 1)
                                for h in range(GH):
                                    ins = dve.scalar_tensor_tensor(
                                        half(Y[d][:, s, h, :], s, d), split(bank(d, 1)[:, h * 64:(h + 1) * 64], s),
                                        B.brk[:, t, 4 * d + h:4 * d + h + 1], split(self.cst(at, 64), s),
                                        ALU.mult, ALU.mult)
                                ins.then_inc(y_kept, 1)
                            for d in range(2):
                                dve.wait_ge(z_summed, idx(n, s, d) + 1)
                                for X, lo, sel in ((T, 0, d), (U, 256, 1 - d)):
                                    cols = X[:, d, :, :].rearrange("p h (g two b) -> p h g two b", two=2, b=1 << s)[
                                        :, :, :, sel, :]
                                    z = bank(d, 2)[:, lo:lo + 256].rearrange("p (h g b) -> p h g b", h=GH, b=1 << s)
                                    if (1 << s) == 1:
                                        cols, z = cols[:, :, :, 0], z[:, :, :, 0]
                                    elif (1 << s) == 64:
                                        cols, z = cols[:, :, 0, :], z[:, :, 0, :]
                                    ins = dve.tensor_tensor(cols, cols, z, ALU.subtract)
                                ins.then_inc(updated, 1)
                        for d in range(2):
                            q, t = 2 * n + d, tile_of(n, d)
                            hs = slice(4 * d, 4 * d + 4)
                            O = heads(B.OG[:, t, :])
                            first = n < TT // 2
                            dve.wait_ge(o_summed, q + 1)
                            for h in range(GH):
                                ins = dve.scalar_tensor_tensor(S[:, d, h, :], S[:, d, h, :],
                                                               B.ex[:, 2, t, 4 * d + h:4 * d + h + 1],
                                                               bank(d, 3)[:, h * P:(h + 1) * P], ALU.mult, ALU.add)
                            ins.then_inc(state_done, 1)
                            link(dve.tensor_tensor(OT[:, d, :, :], heads(bank(d, 1)), bc(B.req[:, t, hs]), ALU.mult))
                            if first:
                                link(dve.tensor_tensor(O, heads(bank(d, 0)), bc(B.rqk[:, t, 0:4]), ALU.mult))
                                dve.tensor_tensor(O, O, OT[:, d, :, :], ALU.add).then_inc(out_done, 1)
                            else:
                                link(dve.tensor_tensor(O, O, OT[:, d, :, :], ALU.add))
                                link(dve.tensor_tensor(OT[:, d, :, :], heads(bank(d, 0)), bc(B.rqk[:, t, 0:4]), ALU.mult))
                                dve.tensor_tensor(O, O, OT[:, d, :, :], ALU.add).then_inc(out_done, 1)

    def stage_gdn_out(self, B):
        nc = self.nc
        with ExitStack() as ctx:
            sq = self.sb(ctx, "go_sq", [P, TT * GH, P])
            ss = self.sb(ctx, "go_ss", [P, TT * GH])
            gated, rooted, turned, summed = (self.sem("go_" + n) for n in ("gated", "rooted", "turned", "summed"))
            O = B.OG[:, :, :].rearrange("p t (h c) -> p (t h) c", h=GH)
            Z = B.GZ[:, :, :].rearrange("p t (h c) -> p (t h) c", h=GH)
            with nc.Block() as block:
                @block.scalar
                def _(act):
                    act.activation(Z, Z, ACT.Silu).then_inc(gated, 1)
                    act.wait_ge(summed, 1)
                    act.activation(ss[:, :], ss[:, :], ACT.Sqrt).then_inc(rooted, 1)
                    for h in range(1, GH, 2):
                        act.wait_ge(turned, h + 1)
                        act.activation(B.YT[:, 4 + h, :], self.psum[:, h, :], ACT.Copy)

                @block.gpsimd
                def _(pool):
                    link = self.pool_link.on(pool)
                    pool.wait_ge(gated, 1)
                    link(pool.tensor_tensor(Z, Z, B.gnw[:, :].unsqueeze(1).to_broadcast([P, TT * GH, P]), ALU.mult))
                    pool.sem_inc(gated, 1)

                @block.vector
                def _(dve):
                    link = self.dve_link.on(dve)
                    link(dve.tensor_tensor(sq[:, :, :], O, O, ALU.mult))
                    link(dve.tensor_reduce(ss[:, :], sq[:, :, :], AX.X, ALU.add))
                    link(dve.tensor_scalar(ss[:, :], ss[:, :], 1.0 / P, EPS, ALU.mult, ALU.add))
                    dve.sem_inc(summed, 1)
                    dve.wait_ge(rooted, 1)
                    link(dve.reciprocal(ss[:, :], ss[:, :]))
                    link(dve.tensor_tensor(O, O, ss[:, :].unsqueeze(2).to_broadcast([P, TT * GH, P]), ALU.mult))
                    dve.wait_ge(gated, 2)
                    link(dve.tensor_tensor(O, O, Z, ALU.mult))
                    dve.sem_inc(summed, 1)
                    for h in range(0, GH, 2):
                        dve.wait_ge(turned, h + 1)
                        dve.tensor_copy(B.YT[:, 4 + h, :], self.psum[:, h, :])

                @block.tensor
                def _(pe):
                    pe.wait_ge(summed, 2)
                    for h in range(GH):
                        for t in range(TT):
                            tr = pe.transpose(self.psum[:, h, t * P:(t + 1) * P], B.OG[:, t, h * P:(h + 1) * P],
                                              self.cst(C_IDENT))
                        tr.then_inc(turned, 1)

    def stage_residual(self, tag, w, YT, loads_done=False, alpha=1.0):
        nc, W = self.nc, self.W
        src = w.rearrange("(k p) c -> p k c", p=P)
        base = W.issued
        with ExitStack() as ctx:
            tmp = self.sb(ctx, f"{tag}_tmp", [P, 2, COLS])
            summed, added = self.sem(f"{tag}_summed"), self.sem(f"{tag}_added")
            for n in range(2):
                W.used[base + n] = (summed, TT * (n + 1))
            with nc.Block() as block:
                @block.sync
                def _(sp):
                    for n in range(2):
                        W.load(sp, base + n, src[:, :, n * COLS:(n + 1) * COLS])

                @block.tensor
                def _(pe):
                    for n in range(2):
                        W.wait(pe, base + n)
                        slot = W.slot(base + n).rearrange("p (k c) -> p k c", k=KD)
                        for t in range(TT):
                            for k in range(KD):
                                mm = pe.matmul(self.psum[:, n * TT + t, :], YT[:, k, t * P:(t + 1) * P],
                                               slot[:, k, :], start=(k == 0), stop=(k == KD - 1))
                            mm.then_inc(summed, 1)

                @block.vector
                def _(dve):
                    link = self.dve_link.on(dve)
                    for n in range(2):
                        cols = slice(n * COLS, (n + 1) * COLS)
                        for t in range(TT):
                            u = n * TT + t
                            dve.wait_ge(summed, u + 1)
                            link(dve.tensor_tensor(tmp[:, u % 2, :], self.psum[:, u, :], self.gate[:, cols], ALU.mult))
                            dve.scalar_tensor_tensor(self.X[:, t, cols], self.X[:, t, cols], alpha, tmp[:, u % 2, :],
                                                     ALU.mult, ALU.add).then_inc(added, 1)

    def stage_route(self, R):
        nc, i = self.nc, self.i
        NE, NG, PER = 32, 4, 8
        GL, EL, G4, BE = 0, NG, 8, 32
        names = ("loaded zeroed summed ranked counted prefixed computed exped scattered listed turned cleared")
        (loaded, zeroed, summed, ranked, counted, prefixed, computed, exped, scattered, listed, turned, cleared) = (
            self.sem("rt_" + n) for n in names.split())
        with ExitStack() as ctx:
            RW = self.sb(ctx, "router_w", [P, KD, NG + NE])
            RB = self.sb(ctx, "router_b", [P, NG + NE])
            L = self.sb(ctx, "logits", [P, TT, NG + NE])
            s4 = self.sb(ctx, "rt_s4", [P, 2, TT, NG])
            s32 = self.sb(ctx, "rt_s32", [P, 2, TT, NE])
            OH = self.sb(ctx, "rt_onehot", [P, 2, TT, NE])
            A = self.sb(ctx, "rt_assigned", [P, TT, NE])
            v = self.sb(ctx, "rt_scalars", [P, 8, TT])
            nbT = self.sb(ctx, "rt_blocks_of", [NE, 4])
            ends = self.sb(ctx, "rt_ends", [P, 2, NE])
            cmp = self.sb(ctx, "rt_cmp", [P, NBMAX + 1, NE])
            bef = self.sb(ctx, "rt_bef", [P, NBMAX + 1])
            destf = self.sb(ctx, "rt_destf", [P, 2, TT])
            zero = self.sb(ctx, "rt_zero", [NBMAX + 1, P])
            lists = self.sb(ctx, "rt_lists", [NBMAX + 1, P])
            tok = R.tok_of_row
            with nc.Block() as block:
                @block.sync
                def _(sp):
                    for src, at, n in ((i["router_group_w"][0], 0, NG), (i["router_expert_w"][0], NG, NE)):
                        sp.dma_start(RW[:, :, at:at + n], src.rearrange("(k p) e -> p k e", p=P)).then_inc(loaded, 16)
                    for src, at, n in ((i["router_group_b"], 0, NG), (i["router_expert_b"], NG, NE)):
                        sp.dma_start(RB[:, at:at + n], bass.AP(src.tensor, 0, [[0, P], [1, n]])).then_inc(loaded, 16)
                    sp.wait_ge(cleared, 1)
                    sp.dma_start(tok.rearrange("(n p) a -> n (p a)", p=P), zero[:, :]).then_inc(zeroed, 16)
                    sp.wait_ge(scattered, 16 * 2 * TT)
                    sp.dma_start(lists[:, :], tok.rearrange("(n p) a -> n (p a)", p=P)).then_inc(listed, 16)

                @block.tensor
                def _(pe):
                    pe.wait_ge(loaded, 64)
                    for t in range(TT):
                        for k in range(KD):
                            mm = pe.matmul(self.psum[:, 0, t * 36:(t + 1) * 36], self.HT[:, k, t * P:(t + 1) * P],
                                           RW[:, k, :], start=(k == 0), stop=(k == KD - 1))
                    mm.then_inc(summed, 1)
                    pe.wait_ge(computed, 1)
                    for t in range(TT):
                        for s in range(t + 1):
                            pe.matmul(self.psum[:, 1, t * NE:(t + 1) * NE], self.cst(C_LT if s == t else C_ONES),
                                      A[:, s, :], start=(s == 0), stop=(s == t))
                    for t in range(TT):
                        mm = pe.matmul(self.psum[0:NE, 2, 0:1], A[:, t, :], self.cst(C_ONES, 1),
                                       start=(t == 0), stop=(t == TT - 1))
                    mm.then_inc(counted, 1)
                    pe.wait_ge(computed, 2)
                    wide = nbT[:, 3:4].to_broadcast([NE, P])
                    pe.matmul(self.psum[:, 3, 0:NE], wide, self.const[0:NE, C_LT:C_LT + NE], start=True, stop=True)
                    mm = pe.matmul(self.psum[:, 3, NE:2 * NE], wide, self.const[0:NE, C_LE:C_LE + NE],
                                   start=True, stop=True)
                    mm.then_inc(prefixed, 1)
                    pe.wait_ge(listed, 16)
                    n = NBMAX + 1
                    pe.transpose(self.psum[:, 4, 0:n], lists[:, :], self.const[0:n, C_IDENT:C_IDENT + n]) \
                      .then_inc(turned, 1)

                @block.scalar
                def _(act):
                    act.wait_ge(exped, 1)
                    act.activation(s4[:, 0, :, :], s4[:, 0, :, :], ACT.Exp).then_inc(exped, 1)
                    act.wait_ge(exped, 3)
                    act.activation(v[:, 5, :], v[:, 5, :], ACT.Exp).then_inc(exped, 1)

                @block.gpsimd
                def _(pool):
                    pool.memset(zero[:, :], 0.0).then_inc(cleared, 1)
                    pool.wait_ge(zeroed, 16)
                    pool.wait_ge(computed, 3)
                    for k in range(2):
                        for t in range(TT):
                            pool.indirect_dma_start(
                                tok, bass.IndirectOffsetOnAxis(R.dest[:, k, t:t + 1].bitcast(U32), 0),
                                self.const[:, C_TOK + t:C_TOK + t + 1], None).then_inc(scattered, 16)

                @block.vector
                def _(dve):
                    link = self.dve_link.on(dve)
                    rep = lambda ap, n: ap.unsqueeze(2).to_broadcast([P, TT, n])
                    iota = lambda n: self.cst(C_IOTA, n).unsqueeze(1).to_broadcast([P, TT, n])
                    dve.wait_ge(loaded, 64)
                    dve.wait_ge(summed, 1)
                    link(dve.tensor_tensor(L[:, :, :], self.psum[:, 0, 0:TT * 36].rearrange("p (t e) -> p t e", t=TT),
                                           RB[:, :].unsqueeze(1).to_broadcast([P, TT, 36]), ALU.add))
                    gl, el = L[:, :, 0:NG], L[:, :, NG:]

                    def first_of(x, n, top, index, scratch):
                        link(dve.tensor_reduce(top, x, AX.X, ALU.max))
                        link(dve.tensor_tensor(scratch, x, rep(top, n), ALU.is_lt))
                        link(dve.scalar_tensor_tensor(scratch, scratch, 64.0, iota(n), ALU.mult, ALU.add))
                        link(dve.tensor_reduce(index, scratch, AX.X, ALU.min))

                    first_of(gl, NG, v[:, 0, :], v[:, 1, :], s4[:, 1, :, :])
                    link(dve.tensor_tensor(s4[:, 0, :, :], gl, rep(v[:, 0, :], NG), ALU.subtract))
                    dve.sem_inc(exped, 1)
                    link(dve.tensor_tensor(s4[:, 1, :, :], iota(NG), rep(v[:, 1, :], NG), ALU.not_equal))
                    link(dve.tensor_scalar(s4[:, 1, :, :], s4[:, 1, :, :], NEG, None, ALU.mult))
                    for t in range(TT):
                        link(dve.tensor_tensor(s32[:, 0, t, :].rearrange("p (g e) -> p g e", g=NG),
                                               el[:, t, :].rearrange("p (g e) -> p g e", g=NG),
                                               s4[:, 1, t, :].unsqueeze(2).to_broadcast([P, NG, PER]), ALU.add))
                    for k in range(2):
                        first_of(s32[:, 0, :, :], NE, v[:, 2 + k, :], v[:, 4, :], s32[:, 1, :, :])
                        link(dve.tensor_tensor(OH[:, k, :, :], iota(NE), rep(v[:, 4, :], NE), ALU.is_equal))
                        if k == 0:
                            link(dve.scalar_tensor_tensor(s32[:, 0, :, :], OH[:, 0, :, :], 2 * NEG, s32[:, 0, :, :],
                                                          ALU.mult, ALU.add))
                    link(dve.tensor_tensor(A[:, :, :], OH[:, 0, :, :], OH[:, 1, :, :], ALU.add))
                    dve.sem_inc(computed, 1)
                    dve.wait_ge(exped, 2)
                    link(dve.tensor_tensor(v[:, 5, :], v[:, 3, :], v[:, 2, :], ALU.subtract))
                    dve.sem_inc(exped, 1)
                    link(dve.tensor_reduce(v[:, 6, :], s4[:, 0, :, :], AX.X, ALU.add))
                    dve.wait_ge(exped, 4)
                    link(dve.tensor_scalar(v[:, 7, :], v[:, 5, :], 1.0, None, ALU.add))
                    link(dve.tensor_tensor(v[:, 6, :], v[:, 6, :], v[:, 7, :], ALU.mult))
                    link(dve.reciprocal(R.gates[:, 0, :], v[:, 6, :]))
                    link(dve.tensor_tensor(R.gates[:, 1, :], R.gates[:, 0, :], v[:, 5, :], ALU.mult))
                    dve.wait_ge(counted, 1)
                    link(dve.tensor_copy(nbT[:, 0:1], self.psum[0:NE, 2, 0:1]))
                    link(dve.tensor_scalar(nbT[:, 3:4], nbT[:, 0:1], 0.0, None, ALU.is_gt))
                    for n in range(1, SEQ // P):
                        link(dve.tensor_scalar(nbT[:, 1:2], nbT[:, 0:1], float(n * P), None, ALU.is_gt))
                        link(dve.tensor_tensor(nbT[:, 3:4], nbT[:, 3:4], nbT[:, 1:2], ALU.add))
                    dve.sem_inc(computed, 1)
                    dve.wait_ge(prefixed, 1)
                    link(dve.tensor_copy(ends[:, :, :].rearrange("p a e -> p (a e)"), self.psum[:, 3, 0:2 * NE]))
                    link(dve.tensor_scalar(ends[:, 0, :], ends[:, 0, :], float(P), None, ALU.mult))
                    link(dve.tensor_tensor(s32[:, 0, :, :], self.psum[:, 1, 0:TT * NE].rearrange("p (t e) -> p t e", t=TT),
                                           ends[:, 0, :].unsqueeze(1).to_broadcast([P, TT, NE]), ALU.add))
                    for k in range(2):
                        link(dve.tensor_tensor(s32[:, 1, :, :], s32[:, 0, :, :], OH[:, k, :, :], ALU.mult))
                        link(dve.tensor_reduce(destf[:, k, :], s32[:, 1, :, :], AX.X, ALU.add))
                    link(dve.tensor_copy(R.dest[:, :, :], destf[:, :, :]))
                    dve.sem_inc(computed, 1)
                    link(dve.tensor_tensor(cmp[:, :, :], ends[:, 1, :].unsqueeze(1).to_broadcast([P, NBMAX + 1, NE]),
                                           self.cst(C_IOTA, NBMAX + 1).unsqueeze(2).to_broadcast([P, NBMAX + 1, NE]),
                                           ALU.is_le))
                    link(dve.tensor_reduce(bef[:, :], cmp[:, :, :], AX.X, ALU.add))
                    link(dve.tensor_scalar(R.block_expert[:, :], bef[:, :], float(NE - 1), None, ALU.min))
                    link(dve.tensor_copy(R.n_blocks[:, 0:1], ends[:, 1, NE - 1:NE]))
                    link(dve.tensor_scalar(R.n_blocks[:, 1:2], ends[:, 1, NE - 1:NE], 1.0, None, ALU.subtract))
                    dve.wait_ge(turned, 1)
                    link(dve.tensor_copy(R.rows[:, :], self.psum[:, 4, 0:NBMAX + 1]))

    def stage_experts(self, R):
        nc, i = self.nc, self.i
        w1 = i["expert_w1"][0].rearrange("e (k p) c -> p (e k) c", p=P)
        w3 = i["expert_w3"][0].rearrange("e (k p) c -> p (e k) c", p=P)
        w2 = i["expert_w2"][0].rearrange("e (k p) c -> p (e k) c", p=P)
        KF = 4
        halves = [self.ring[:, n // 2, (n % 2) * 2048:(n % 2 + 1) * 2048].rearrange("p (k c) -> p k c", k=4)
                  for n in range(6)]
        arrived = [self.sem(f"w_half{n}_arrived") for n in range(6)]
        used = [self.sem(f"w_half{n}_used") for n in range(6)]
        names = "idx_copied gathered rows_turned xt_act xt_dve silued hidden h_turned ht_kept y_act y_dve y_stored gathering"
        (idx_copied, gathered, rows_turned, xt_act, xt_dve, silued, hidden, h_turned, ht_kept, y_act, y_dve,
         y_stored, gathering) = (self.sem("ex_" + n) for n in names.split())
        bankA, bankB = self.psum[:, 0, :], self.psum[:, 1, :]
        turn = lambda k: self.psum[:, 2 + k // 4, (k % 4) * P:(k % 4 + 1) * P]
        bankH = self.psum[:, 4, :]
        bankY = lambda c: self.psum[:, 5 + c, :]
        scale, shift = self.modA[:, 0, :], self.mod[:, 3 * KD:4 * KD]
        with ExitStack() as ctx:
            XG = self.sb(ctx, "ex_rows", [P, D])
            XT = self.sb(ctx, "ex_XT", [P, KD, P])
            IDX = self.sb(ctx, "ex_idx", [P, 1], I32)
            HS = self.sb(ctx, "ex_silu", [P, 512])
            HM = self.sb(ctx, "ex_hidden", [P, 512])
            HTB = self.sb(ctx, "ex_hiddenT", [P, KF, P])
            YO = self.sb(ctx, "ex_out", [P, D])
            ys = R.ys

            def count(eng):
                return [eng.value_load(R.n_blocks[0:1, c:c + 1], min_val=SEQ * 2 // P - c, max_val=NBMAX - c)
                        for c in range(2)]

            with nc.Block() as block:
                @block.sync
                def _(sp):
                    nb, last = count(sp)

                    def up(n, first):
                        e = sp.value_load(R.block_expert[0:1, bass.ds(n, 1)], min_val=0, max_val=31)
                        for m, w in enumerate((w1, w3)):
                            for h in range(2):
                                if not first:
                                    sp.wait_ge(used[2 * m + h], n)
                                sp.dma_start(halves[2 * m + h], w[:, bass.ds(e * 8 + 4 * h, 4), :]) \
                                  .then_inc(arrived[2 * m + h], 16)

                    def down(n, first):
                        e = sp.value_load(R.block_expert[0:1, bass.ds(n, 1)], min_val=0, max_val=31)
                        for h in range(2):
                            if not first:
                                sp.wait_ge(used[4 + h], n)
                            sp.dma_start(halves[4 + h], w2[:, bass.ds(e * 4, 4), h * 512:(h + 1) * 512]) \
                              .then_inc(arrived[4 + h], 16)

                    up(0, True)
                    up(1, False)
                    down(0, True)
                    with sp.Fori(2, nb) as n:
                        up(n, False)
                        down(n - 1, False)
                    down(last, False)

                @block.gpsimd
                def _(pool):
                    nb, _ = count(pool)

                    def gather(m, first):
                        if not first:
                            pool.wait_ge(rows_turned, m)
                        pool.tensor_copy(IDX[:, :], R.rows[:, bass.ds(m, 1)]).then_inc(idx_copied, 1)
                        pool.wait_ge(idx_copied, m + 1)
                        pool.sem_inc(gathering, 1)
                        pool.indirect_dma_start(XG[:, :], None, R.xn,
                                                bass.IndirectOffsetOnAxis(IDX[:, :].bitcast(U32), 0)) \
                            .then_inc(gathered, 16)
                    gather(0, True)
                    with pool.Fori(1, nb + 1) as m:
                        gather(m, False)

                @block.tensor
                def _(pe):
                    nb, last = count(pe)

                    def rows(m):
                        pe.wait_ge(gathered, m * 16 + 16)
                        for k in range(KD):
                            tr = pe.transpose(turn(k), XG[:, k * P:(k + 1) * P], self.cst(C_IDENT))
                        tr.then_inc(rows_turned, 1)

                    def up(n, first):
                        pe.wait_ge(xt_act, n + 1)
                        pe.wait_ge(xt_dve, n + 1)
                        for m, bank in enumerate((bankA, bankB)):
                            if not first:
                                pe.wait_ge((silued, hidden)[m], n)
                            for h in range(2):
                                pe.wait_ge(arrived[2 * m + h], n * 16 + 16)
                                for k in range(4):
                                    mm = pe.matmul(bank, XT[:, 4 * h + k, :], halves[2 * m + h][:, k, :],
                                                   start=(h + k == 0), stop=(h * 4 + k == KD - 1))
                                mm.then_inc(used[2 * m + h], 1)

                    def down(n):
                        pe.wait_ge(ht_kept, n + 1)
                        pe.wait_ge(y_act, n + 1)
                        pe.wait_ge(y_dve, n + 1)
                        for h in range(2):
                            pe.wait_ge(arrived[4 + h], n * 16 + 16)
                            for k in range(KF):
                                mm = pe.matmul(bankY(h), HTB[:, k, :], halves[4 + h][:, k, :],
                                               start=(k == 0), stop=(k == KF - 1))
                            mm.then_inc(used[4 + h], 1)

                    def hid(n):
                        pe.wait_ge(hidden, n + 1)
                        for k in range(KF):
                            tr = pe.transpose(bankH[:, k * P:(k + 1) * P], HM[:, k * P:(k + 1) * P],
                                              self.cst(C_IDENT))
                        tr.then_inc(h_turned, 1)

                    rows(0)
                    up(0, True)
                    rows(1)
                    hid(0)
                    with pe.Fori(1, nb) as n:
                        up(n, False)
                        rows(n + 1)
                        down(n - 1)
                        hid(n)
                    down(last)

                @block.scalar
                def _(act):
                    nb, last = count(act)
                    act.sem_inc(y_act, 1)
                    act.sem_inc(y_stored, 16)

                    def silu(n):
                        act.wait_ge(used[1], n + 1)
                        if not isinstance(n, int):
                            act.wait_ge(hidden, n)
                        act.activation(HS[:, :], bankA, ACT.Silu).then_inc(silued, 1)

                    def xt(m):
                        act.wait_ge(rows_turned, m + 1)
                        for k in range(KD // 2, KD):
                            ins = act.activation(XT[:, k, :], turn(k), ACT.Identity, scale=scale[:, k:k + 1],
                                                 bias=shift[:, k:k + 1])
                        ins.then_inc(xt_act, 1)

                    def out(n):
                        act.wait_ge(used[4], n + 1)
                        act.wait_ge(y_stored, n * 16 + 16)
                        act.activation(YO[:, 0:512], bankY(0), ACT.Copy).then_inc(y_act, 1)
                        act.wait_ge(y_act, n + 2)
                        act.wait_ge(y_dve, n + 2)
                        act.dma_start(ys[bass.ds(n * P, P), :], YO[:, :]).then_inc(y_stored, 16)

                    xt(0)
                    silu(0)
                    xt(1)
                    with act.Fori(1, nb) as n:
                        silu(n)
                        xt(n + 1)
                        out(n - 1)
                    out(last)
                    act.wait_ge(y_stored, nb * 16 + 16)
                    act.sem_inc(y_act, 1)

                @block.vector
                def _(dve):
                    nb, last = count(dve)
                    dve.sem_inc(y_dve, 1)

                    def gate(n):
                        dve.wait_ge(silued, n + 1)
                        dve.wait_ge(used[3], n + 1)
                        if not isinstance(n, int):
                            dve.wait_ge(h_turned, n)
                        dve.tensor_tensor(HM[:, :], HS[:, :], bankB, ALU.mult).then_inc(hidden, 1)

                    def xt(m):
                        dve.wait_ge(rows_turned, m + 1)
                        for k in range(KD // 2):
                            ins = dve.tensor_scalar(XT[:, k, :], turn(k), scale[:, k:k + 1], shift[:, k:k + 1],
                                                    ALU.mult, ALU.add)
                        ins.then_inc(xt_dve, 1)

                    def out(n):
                        dve.wait_ge(used[5], n + 1)
                        dve.wait_ge(y_stored, n * 16 + 16)
                        dve.tensor_copy(YO[:, 512:D], bankY(1)).then_inc(y_dve, 1)

                    def keep(n):
                        dve.wait_ge(h_turned, n + 1)
                        dve.tensor_copy(HTB[:, :, :].rearrange("p k s -> p (k s)"), bankH).then_inc(ht_kept, 1)

                    xt(0)
                    gate(0)
                    xt(1)
                    keep(0)
                    with dve.Fori(1, nb) as n:
                        gate(n)
                        xt(n + 1)
                        out(n - 1)
                        keep(n)
                    out(last)

    def stage_combine(self, R):
        nc = self.nc
        with ExitStack() as ctx:
            YG = self.sb(ctx, "cb_rows", [P, 4, D])
            fetched = [self.sem(f"cb_fetched{n}") for n in range(4)]
            added = self.sem("cb_added")
            with nc.Block() as block:
                @block.gpsimd
                def _(pool):
                    for t in range(TT):
                        if t >= 2:
                            pool.wait_ge(added, t - 1)
                        for k in range(2):
                            n = 2 * (t % 2) + k
                            pool.indirect_dma_start(YG[:, n, :], None, R.ys, bass.IndirectOffsetOnAxis(
                                R.dest[:, k, t:t + 1].bitcast(U32), 0)).then_inc(fetched[n], 16)

                @block.vector
                def _(dve):
                    link = self.dve_link.on(dve)
                    for t in range(TT):
                        for k in range(2):
                            dve.wait_ge(fetched[2 * (t % 2) + k], 16 * (t // 2 + 1))
                        a, b = YG[:, 2 * (t % 2), :], YG[:, 2 * (t % 2) + 1, :]
                        link(dve.tensor_scalar(a, a, R.gates[:, 0, t:t + 1], None, ALU.mult))
                        link(dve.scalar_tensor_tensor(a, b, R.gates[:, 1, t:t + 1], a, ALU.mult, ALU.add))
                        link(dve.tensor_tensor(a, a, self.gate[:, :], ALU.mult))
                        dve.tensor_tensor(self.X[:, t, :], self.X[:, t, :], a, ALU.add).then_inc(added, 1)

    def stage_row_norm(self, tag, eps, mean, gain, bias=None, out=None):
        nc = self.nc
        with ExitStack() as ctx:
            GB = self.sb(ctx, f"{tag}_gain", [P, 2, D])
            loaded, normed = self.sem(f"{tag}_loaded"), self.sem(f"{tag}_normed")
            with nc.Block() as block:
                rstd, mu, stats_dve, stats_act = self.row_stats(block, tag, ctx, eps, mean)
                n_vec = 1 if bias is None else 2

                @block.sync
                def _(sp):
                    for n, src in enumerate((gain, bias)[:n_vec]):
                        sp.dma_start(GB[:, n, :], bass.AP(src.tensor, 0, [[0, P], [1, D]])).then_inc(loaded, 16)
                    if out is not None:
                        for t in range(TT):
                            sp.wait_ge(normed, t + 1)
                            self.nstored += 16
                            sp.dma_start(out[t * P:(t + 1) * P, :], self.X[:, t, :]).then_inc(self.stored, 16)
                        sp.wait_ge(self.stored, self.nstored)

                @block.scalar
                def _(act):
                    stats_act(act)

                @block.vector
                def _(dve):
                    link = self.dve_link.on(dve)
                    stats_dve(dve)
                    dve.wait_ge(loaded, 16 * n_vec)
                    for t in range(TT):
                        x = self.X[:, t, :]
                        if mean:
                            link(dve.tensor_scalar(x, x, mu[:, t, 0:1], rstd[:, t:t + 1], ALU.subtract, ALU.mult))
                            link(dve.tensor_tensor(x, x, GB[:, 0, :], ALU.mult))
                            dve.tensor_tensor(x, x, GB[:, 1, :], ALU.add).then_inc(normed, 1)
                        else:
                            dve.scalar_tensor_tensor(x, x, rstd[:, t:t + 1], GB[:, 0, :], ALU.mult, ALU.mult) \
                               .then_inc(normed, 1)

    def stage_branch_proj(self, tag, B, at, with_f):
        nc, i, W = self.nc, self.i, self.W
        w = i["w_in_2"][0].rearrange("(k p) c -> p k c", p=P)
        base = W.issued
        loads = [(at + n * COLS, COLS) for n in range(3)] + ([(at + 3 * COLS, 8)] if with_f else [])
        items = [(n, "qk"[n], c) for n in range(2) for c in range(4)] + [(2, "v", t) for t in range(TT)]
        if with_f:
            items += [(3, "f", t) for t in range(TT)]
        BANKS = 6
        with ExitStack() as ctx:
            summed, copied = self.sem(f"{tag}_summed"), self.sem(f"{tag}_copied")
            for n in range(len(loads)):
                W.used[base + n] = (summed, TT * (n + 1))
            with nc.Block() as block:
                @block.sync
                def _(sp):
                    for n, (col, width) in enumerate(loads):
                        W.load(sp, base + n, w[:, :, col:col + width])

                @block.tensor
                def _(pe):
                    for n, (ld, what, c) in enumerate(items):
                        if n % 4 == 0:
                            W.wait(pe, base + ld)
                        if n >= BANKS:
                            pe.wait_ge(copied, n - BANKS + 1)
                        width = loads[ld][1]
                        slot = W.slot(base + ld)[:, 0:KD * width].rearrange("p (k c) -> p k c", k=KD)
                        bank = self.psum[:, n % BANKS, 0:width]
                        for k in range(KD):
                            if what in "vf":
                                mm = pe.matmul(bank, self.HT[:, k, c * P:(c + 1) * P], slot[:, k, :],
                                               start=(k == 0), stop=(k == KD - 1))
                            else:
                                mm = pe.matmul(bank, slot[:, k, c * P:(c + 1) * P], self.HT[:, k, :],
                                               start=(k == 0), stop=(k == KD - 1))
                        mm.then_inc(summed, 1)

                @block.scalar
                def _(act):
                    for n, (_, what, c) in enumerate(items):
                        act.wait_ge(summed, n + 1)
                        dst = (B.Q if what == "q" else B.K if what == "k" else B.V if what == "v" else B.F)[:, c, :]
                        act.activation(dst, self.psum[:, n % BANKS, 0:dst.shape[1]], ACT.Copy,
                                       scale=HD ** -0.5 if what == "q" else 1.0).then_inc(copied, 1)

    def log1p(self, dve, link, u, s2, acc, out):
        link(dve.tensor_scalar(acc, u, 2.0, None, ALU.add))
        link(dve.reciprocal(acc, acc))
        link(dve.tensor_tensor(u, u, acc, ALU.mult))
        link(dve.tensor_tensor(s2, u, u, ALU.mult))
        link(dve.tensor_scalar(acc, s2, 1.0 / 17, 1.0 / 15, ALU.mult, ALU.add))
        for n in (13, 11, 9, 7, 5, 3, 1):
            link(dve.tensor_tensor(acc, acc, s2, ALU.mult))
            link(dve.tensor_scalar(acc, acc, 1.0 / n, None, ALU.add))
        link(dve.scalar_tensor_tensor(out, u, 2.0, acc, ALU.mult, ALU.mult))

    def stage_forget(self, B):
        nc, i = self.nc, self.i
        H = FOX_H
        with ExitStack() as ctx:
            bf = self.sb(ctx, "fox_bf", [P, H])
            tmp = self.sb(ctx, "fox_tmp", [P, 4, TT * H])
            logf = self.sb(ctx, "fox_logf", [P, TT, H])
            loaded, absed, exped, ready, summed = (self.sem("fg_" + n) for n in
                                                   ("loaded", "absed", "exped", "ready", "summed"))
            with nc.Block() as block:
                @block.sync
                def _(sp):
                    sp.dma_start(bf[:, :], bass.AP(i["b_f_2"].tensor, 0, [[0, P], [1, H]])).then_inc(loaded, 16)

                @block.scalar
                def _(act):
                    act.wait_ge(absed, 1)
                    act.activation(tmp[:, 1, :], tmp[:, 1, :], ACT.Exp, scale=-1.0).then_inc(exped, 1)

                @block.vector
                def _(dve):
                    link = self.dve_link.on(dve)
                    x, u, s2, acc = (tmp[:, n, :] for n in range(4))
                    dve.wait_ge(loaded, 16)
                    link(dve.tensor_tensor(x.rearrange("p (t h) -> p t h", t=TT), B.F[:, :, :],
                                           bf[:, :].unsqueeze(1).to_broadcast([P, TT, H]), ALU.add))
                    link(dve.tensor_scalar(u, x, -1.0, None, ALU.mult))
                    link(dve.tensor_tensor(u, u, x, ALU.max))
                    dve.sem_inc(absed, 1)
                    dve.wait_ge(exped, 1)
                    self.log1p(dve, link, u, s2, acc, acc)
                    link(dve.scalar_tensor_tensor(logf[:, :, :].rearrange("p t h -> p (t h)"), x, 0.0, acc,
                                                  ALU.min, ALU.subtract))
                    dve.sem_inc(ready, 1)
                    dve.wait_ge(summed, 1)
                    dve.tensor_copy(B.cum[:, :, :].rearrange("p t h -> p (t h)"), self.psum[:, 0, 0:TT * H])
                    dve.tensor_copy(B.cumT[:, :], self.psum[0:H, 1, :])

                @block.tensor
                def _(pe):
                    pe.wait_ge(ready, 1)
                    for t in range(TT):
                        for s in range(t + 1):
                            tri = self.cst(C_LE if s == t else C_ONES)
                            pe.matmul(self.psum[:, 0, t * H:(t + 1) * H], tri, logf[:, s, :],
                                      start=(s == 0), stop=(s == t))
                            mm = pe.matmul(self.psum[0:H, 1, t * P:(t + 1) * P], logf[:, s, :], tri,
                                           start=(s == 0), stop=(s == t))
                    mm.then_inc(summed, 1)

    def stage_chunk_bias(self, CB):
        nc = self.nc
        hank = self.ring[:, 0, :].rearrange("p (h j) -> p h j", h=CH_H)
        laid, flipped = self.sem("cb_laid"), self.sem("cb_flipped")
        with nc.Block() as block:
            @block.sync
            def _(sp):
                sp.dma_start(hank, bass.AP(self.i["rel_bias_2"].tensor, 0, [[1, P], [640, CH_H], [1, SEQ]])) \
                  .then_inc(laid, 16)

            @block.tensor
            def _(pe):
                pe.wait_ge(laid, 16)
                for h in range(CH_H):
                    pe.matmul(self.psum[:, h, :], self.cst(C_FLIP), hank[:, h, :], start=True, stop=True) \
                      .then_inc(flipped, 1)

            @block.vector
            def _(dve):
                for h in range(CH_H):
                    dve.wait_ge(flipped, h + 1)
                    dve.tensor_copy(CB[:, h, 0:SEQ - P], self.psum[:, h, 0:SEQ - P])
                    dve.tensor_tensor(CB[:, h, SEQ - P:], self.psum[:, h, SEQ - P:], self.cst(C_CHUNK), ALU.add)

    def stage_merge(self, B, M):
        nc, i, W = self.nc, self.i, self.W
        w = i["w_in_2"][0].rearrange("(k p) c -> p k c", p=P)
        base = W.issued
        GATE_AT = 3 * COLS + 8 + 3 * COLS
        srcs = []
        for b, name in enumerate(("w_br_fox_2", "w_br_chunk_2")):
            srcs.append(i[name][0].rearrange("(k p) c -> p k c", p=P))
            srcs += [w[:, :, GATE_AT + b * D + h * COLS:GATE_AT + b * D + (h + 1) * COLS] for h in range(2)]
        with ExitStack() as ctx:
            SG = self.sb(ctx, "mg_gate", [P, 2, SEQ])
            tmp = self.sb(ctx, "mg_tmp", [P, 2, SEQ])
            summed, sigm, merged = self.sem("mg_summed"), self.sem("mg_sigmoid"), self.sem("mg_merged")
            for b in range(2):
                W.used[base + 3 * b] = (summed, 8 * b + 8)
                for h in range(2):
                    W.used[base + 3 * b + 1 + h] = (summed, 8 * b + 4 * h + 4)
            with nc.Block() as block:
                @block.sync
                def _(sp):
                    for n, src in enumerate(srcs):
                        W.load(sp, base + n, src)

                @block.tensor
                def _(pe):
                    for u in range(16):
                        b, c = u // 8, u % 8
                        if c == 0:
                            W.wait(pe, base + 3 * b)
                        if c % 4 == 0:
                            W.wait(pe, base + 3 * b + 1 + c // 4)
                        if u >= 4:
                            pe.wait_ge(merged, u - 3)
                        wg = W.slot(base + 3 * b + 1 + c // 4).rearrange("p (k c) -> p k c", k=KD)
                        wb = W.slot(base + 3 * b).rearrange("p (k c) -> p k c", k=4)
                        src = (B.OA, B.OC)[b]
                        for k in range(KD):
                            pe.matmul(self.psum[:, 2 * (u % 4), :], wg[:, k, (c % 4) * P:(c % 4 + 1) * P],
                                      self.HT[:, k, :], start=(k == 0), stop=(k == KD - 1))
                        for k in range(4):
                            mm = pe.matmul(self.psum[:, 2 * (u % 4) + 1, :], wb[:, k, c * P:(c + 1) * P],
                                           src[:, k, :], start=(k == 0), stop=(k == 3))
                        mm.then_inc(summed, 1)

                @block.scalar
                def _(act):
                    for u in range(16):
                        act.wait_ge(summed, u + 1)
                        if u >= 2:
                            act.wait_ge(merged, u - 1)
                        act.activation(SG[:, u % 2, :], self.psum[:, 2 * (u % 4), :], ACT.Sigmoid).then_inc(sigm, 1)

                @block.vector
                def _(dve):
                    link = self.dve_link.on(dve)
                    for u in range(16):
                        c = u % 8
                        dve.wait_ge(sigm, u + 1)
                        if u < 8:
                            dve.tensor_tensor(M[:, c, :], SG[:, u % 2, :], self.psum[:, 2 * (u % 4) + 1, :],
                                              ALU.mult).then_inc(merged, 1)
                        else:
                            link(dve.tensor_tensor(tmp[:, u % 2, :], SG[:, u % 2, :],
                                                   self.psum[:, 2 * (u % 4) + 1, :], ALU.mult))
                            dve.tensor_tensor(M[:, c, :], M[:, c, :], tmp[:, u % 2, :], ALU.add).then_inc(merged, 1)

    def stage_up(self, YF):
        nc, W = self.nc, self.W
        NF = NCH // 2
        w = self.i["w_up_2"][0].rearrange("(k p) c -> p k c", p=P)
        base, n_loads = W.issued, NF // 2
        summed, copied, conved, silued, made, zeroed = (
            self.sem("up_" + n) for n in ("summed", "copied", "conved", "silued", "made", "zeroed"))
        with ExitStack() as ctx:
            PAD = self.sb(ctx, "up_pad", [P, 4, SEQ + 2])
            CV = self.sb(ctx, "up_conv", [P, 4, SEQ])
            for n in range(n_loads):
                W.used[base + n] = (summed, 4 * (n + 1))
            with nc.Block() as block:
                @block.sync
                def _(sp):
                    for n in range(n_loads):
                        W.load(sp, base + n, *(w[:, :, side + n * 256:side + (n + 1) * 256] for side in (0, NF * P)))

                @block.tensor
                def _(pe):
                    for m in range(NCH):
                        pair, side = m // 2, m % 2
                        n = pair // 2
                        if m % 4 == 0:
                            W.wait(pe, base + n)
                        if m >= 6:
                            pe.wait_ge(copied, m - 5)
                        at = side * 256 + (pair % 2) * P
                        slot = W.slot(base + n).rearrange("p (k c) -> p k c", k=KD)
                        for k in range(KD):
                            mm = pe.matmul(self.psum[:, m % 6, :], slot[:, k, at:at + P], self.HT[:, k, :],
                                           start=(k == 0), stop=(k == KD - 1))
                        mm.then_inc(summed, 1)

                @block.scalar
                def _(act):
                    act.wait_ge(zeroed, 1)

                    def silu(pair):
                        m = 2 * pair
                        act.wait_ge(conved, m + 1)
                        act.activation(CV[:, m % 4, :], CV[:, m % 4, :], ACT.Silu).then_inc(silued, 1)
                    for m in range(NCH):
                        act.wait_ge(summed, m + 1)
                        if m >= 4:
                            act.wait_ge(conved, m - 3)
                        act.activation(PAD[:, m % 4, 2:], self.psum[:, m % 6, :], ACT.Copy).then_inc(copied, 1)
                        if m % 2 == 1 and m >= 3:
                            silu(m // 2 - 1)
                    silu(NF - 1)

                @block.vector
                def _(dve):
                    link = self.dve_link.on(dve)
                    dve.memset(PAD[:, :, :], 0.0).then_inc(zeroed, 1)

                    def product(pair):
                        m = 2 * pair
                        dve.wait_ge(silued, pair + 1)
                        dve.tensor_tensor(YF[:, pair, :], CV[:, m % 4, :], CV[:, (m + 1) % 4, :], ALU.mult) \
                           .then_inc(made, 1)
                    for m in range(NCH):
                        ch = m // 2 + NF * (m % 2)
                        tap = lambda j: self.cols3[:, j * NCH + ch:j * NCH + ch + 1]
                        x, cv = PAD[:, m % 4, :], CV[:, m % 4, :]
                        dve.wait_ge(copied, m + 1)
                        if m >= 4:
                            dve.wait_ge(made, m // 2 - 1)
                        link(dve.tensor_scalar(cv, x[:, 0:SEQ], tap(0), self.cols2[:, R2_CONVB + ch:R2_CONVB + ch + 1],
                                               ALU.mult, ALU.add))
                        link(dve.scalar_tensor_tensor(cv, x[:, 1:SEQ + 1], tap(1), cv, ALU.mult, ALU.add))
                        link(dve.scalar_tensor_tensor(cv, x[:, 2:SEQ + 2], tap(2), cv, ALU.mult, ALU.add))
                        dve.sem_inc(conved, 1)
                        if m % 2 == 1 and m >= 3:
                            product(m // 2 - 1)
                    product(NF - 1)

    def stage_down(self, YF, alpha):
        nc, W = self.nc, self.W
        NF = NCH // 2
        w = self.i["w_down_2"][0].rearrange("(k p) c -> p k c", p=P)
        base = W.issued
        parts = [(k, min(4, NF - k)) for k in range(0, NF, 4)]
        summed, used = self.sem("down_summed"), self.sem("down_used")
        with ExitStack() as ctx:
            tmp = self.sb(ctx, "down_tmp", [P, 2, COLS])
            for n in range(len(parts)):
                W.used[base + n] = (used, n + 1)
            with nc.Block() as block:
                @block.sync
                def _(sp):
                    for n, (k0, nk) in enumerate(parts):
                        W.load(sp, base + n, w[:, k0:k0 + nk, :])

                @block.tensor
                def _(pe):
                    for n, (k0, nk) in enumerate(parts):
                        W.wait(pe, base + n)
                        slot = W.slot(base + n)[:, 0:nk * D].rearrange("p (k c) -> p k c", k=nk)
                        for u in range(2 * TT):
                            t, c = u % TT, u // TT
                            for k in range(nk):
                                mm = pe.matmul(self.psum[:, u, :], YF[:, k0 + k, t * P:(t + 1) * P],
                                               slot[:, k, c * COLS:(c + 1) * COLS],
                                               start=(k0 + k == 0), stop=(k0 + k == NF - 1))
                            if n == len(parts) - 1:
                                mm.then_inc(summed, 1)
                        if n < len(parts) - 1:
                            mm.then_inc(used, 1)

                @block.vector
                def _(dve):
                    link = self.dve_link.on(dve)
                    for u in range(2 * TT):
                        t, c = u % TT, u // TT
                        cols = slice(c * COLS, (c + 1) * COLS)
                        dve.wait_ge(summed, u + 1)
                        link(dve.tensor_tensor(tmp[:, u % 2, :], self.psum[:, u, :], self.gate[:, cols], ALU.mult))
                        link(dve.scalar_tensor_tensor(self.X[:, t, cols], self.X[:, t, cols], alpha, tmp[:, u % 2, :],
                                                      ALU.mult, ALU.add))

    def stages(self):
        nc = self.nc
        self.ys = nc.dram_tensor("expert_rows", (NBMAX * P, D), F32).ap()

        class B:
            pass
        self.stage_load()
        self.stage_mod("mod1", self.i["w_ada"][0], self.cols1[:, R_C:R_C2], self.cols1[:, R_BADA:R_NMIX])
        self.stage_scale("mix", self.cols1[:, R_NMIX:R_NFFN], KD)
        self.stage_norm("norm_mix", EPS, False, self.modA[:, 0, :], self.mod[:, 0:KD])
        with ExitStack() as ctx:
            B.YT = self.sb(ctx, "YT", [P, KD, SEQ])
            B.GZ = self.sb(ctx, "GZ", [P, TT, 512])
            B.GAB = self.sb(ctx, "GAB", [P, TT, 16])
            B.G = self.sb(ctx, "G", [P, 12, SEQ])
            B.OG = self.sb(ctx, "OG", [P, TT, 512])
            with ExitStack() as ctx2:
                B.NQ = self.sb(ctx2, "NQ", [P, 2, SEQ])
                B.NK = self.sb(ctx2, "NK", [P, 2, SEQ])
                B.NV = self.sb(ctx2, "NV", [P, TT, 256])
                self.stage_proj1(B)
                self.stage_na(B)
            with ExitStack() as ctx2:
                self.stage_gdn_prep(B, ctx2)
                self.stage_gdn(B)
                self.stage_gdn_out(B)
            self.stage_gate("gate1", 2 * KD)
            self.stage_residual("mix_out", self.i["w_out"][0], B.YT)
        self.retire_semaphores()

        class R:
            pass
        R.xn = nc.dram_tensor("normed_rows", (SEQ, D), F32).ap()
        R.ys = self.ys
        R.tok_of_row = nc.dram_tensor("token_of_row", ((NBMAX + 1) * P, 1), F32).ap()
        self.stage_scale("ffn", self.cols1[:, R_NFFN:R_CONVA], 4 * KD)
        self.stage_norm("norm_ffn", EPS, False, self.modA[:, 0, :], self.mod[:, 3 * KD:4 * KD], save_rows=R.xn)
        with ExitStack() as ctx:
            R.gates = self.sb(ctx, "gates", [P, 2, TT])
            R.dest = self.sb(ctx, "dest", [P, 2, TT], I32)
            R.rows = self.sb(ctx, "block_rows", [P, NBMAX + 1], I32)
            R.block_expert = self.sb(ctx, "block_expert", [P, NBMAX + 1], I32)
            R.n_blocks = self.sb(ctx, "n_blocks", [P, 2], I32)
            self.stage_route(R)
            self.stage_experts(R)
            self.stage_gate("gate2", 5 * KD)
            self.stage_combine(R)
        self.stage_row_norm("final_norm", EPS, False, self.i["final_norm_w"])
        self.retire_semaphores()

        ALPHA = 2.0 ** 0.25
        self.stage_mod("mod2", self.i["w_ada_2"][0], self.cols1[:, R_C2:R_END], self.cols2[:, R2_BADA:R2_CONVB])
        self.stage_scale("branches", None, KD)
        self.stage_norm("norm_branches", LN_EPS, True, self.modA[:, 0, :], self.mod[:, 0:KD])
        with ExitStack() as ctx:
            B.OA = self.sb(ctx, "OA", [P, 4, SEQ])
            B.OC = self.sb(ctx, "OC", [P, 4, SEQ])
            rows = lambda h: slice(HD * (h % 2), HD * (h % 2 + 1))
            causal = lambda t: (t + 1) * P
            with ExitStack() as ctx2:
                B.Q, B.K, B.V = (self.sb(ctx2, n, [P, 4, SEQ]) for n in ("bq", "bk", "bv"))
                B.F = self.sb(ctx2, "bf", [P, TT, FOX_H])
                B.cum = self.sb(ctx2, "cum", [P, TT, FOX_H])
                B.cumT = self.sb(ctx2, "cumT", [FOX_H, SEQ])
                q = lambda h: B.Q[rows(h), h // 2, :]
                k = lambda h: B.K[rows(h), h // 2, :]
                v = lambda h, j: B.V[:, j, h * HD:(h + 1) * HD]
                self.stage_branch_proj("fox_proj", B, 0, True)
                self.stage_forget(B)
                pick = lambda h: self.const[0:FOX_H, C_IDENT + h:C_IDENT + h + 1].to_broadcast([FOX_H, P])
                self.stage_attention("fox", FOX_H, q, k, v, None, causal, lambda h: B.OA[rows(h), h // 2, :],
                                     cum=(lambda t, h: B.cum[:, t, h:h + 1], pick, B.cumT[:, :]))
                self.retire_semaphores()
                self.stage_branch_proj("chunk_proj", B, 3 * COLS + 8, False)
                CB = self.sb(ctx2, "chunk_bias", [P, CH_H, SEQ])
                self.stage_chunk_bias(CB)
                self.stage_attention("chunk", CH_H, q, k, v, lambda h, t: CB[:, h, SEQ - P - t * P:], causal,
                                     lambda h: B.OC[rows(h), h // 2, :])
            M = self.sb(ctx, "merged", [P, KD, SEQ])
            self.stage_merge(B, M)
            self.stage_gate("gate3", 2 * KD, 1.0)
            self.stage_residual("branch_out", self.i["w_out_2"][0], M, alpha=ALPHA)
        self.stage_row_norm("ln1", LN_EPS, True, self.i["ln1_g_2"], self.i["ln1_b_2"])
        self.stage_scale("ffn2", None, 4 * KD)
        self.stage_norm("norm_ffn2", LN_EPS, True, self.modA[:, 0, :], self.mod[:, 3 * KD:4 * KD])
        with ExitStack() as ctx:
            YF = self.sb(ctx, "YF", [P, NCH // 2, SEQ])
            self.stage_up(YF)
            self.stage_gate("gate4", 5 * KD, 1.0)
            self.stage_down(YF, ALPHA)
        self.stage_row_norm("ln2", LN_EPS, True, self.i["ln2_g_2"], self.i["ln2_b_2"], out=self.out[0])


def lay_out(inputs):
    a = {k: np.ascontiguousarray(v) for k, v in inputs.items()}
    a["na_rpb"] = np.pad(a["na_rpb"][0], ((0, 0), (0, 0), (48, 48)))
    a["rel_bias_2"] = np.pad(a["rel_bias_2"][0][:, ::-1], ((0, 0), (383, 0)), mode="edge")
    a["shape_constants"] = shape_constants()
    return a


def kernel(**inputs):
    import concourse.bacc as bacc
    from concourse.bass_utils import run_bass_kernel_spmd

    nc = bacc.Bacc("TRN2", target_bir_lowering=False, num_devices=1)
    arrays, args = {}, {}
    for name, a in lay_out(inputs).items():
        arrays[f"in_{name}"] = a
        args[name] = nc.dram_tensor(f"in_{name}", a.shape, mybir.dt.from_np(a.dtype), kind="ExternalInput").ap()
    out = nc.dram_tensor("out", (1, SEQ, D), F32, kind="ExternalOutput").ap()
    Kernel(nc, args, out).build()
    r = run_bass_kernel_spmd(nc, [arrays], core_ids=[0])
    return r.results[0]["out"]
```

```python
from contextlib import ExitStack

import numpy as np

import concourse.bass as bass
from concourse import mybir

F32 = mybir.dt.float32
F32R = mybir.dt.float32r
I32 = mybir.dt.int32
U32 = mybir.dt.uint32
ALU = mybir.AluOpType
ACT = mybir.ActivationFunctionType
AX = mybir.AxisListType

P = 128
SEQ = 512
D = 1024
TT = SEQ // P
KD = D // P
COLS = 512
RING = 3
HD = 64
AHEAD = 3
NA_H, FOX_H, CH_H = 4, 8, 8
GH = 4
LEVELS = 7
EPS, LN_EPS = 1e-6, 1e-5
NEG = -1e30
MCOLS = 256
MCHUNKS = 6 * D // MCOLS
MGROUP = 8
MSLOTS = 3
MACC = 4
NBMAX = 2 * SEQ // P + 31

C_IDENT, C_ONES, C_FLIP = 0, 128, 256
C_LE, C_GE, C_GT, C_LT = 384, 512, 640, 768
C_CAUSAL, C_CHUNK = 896, 1024
C_LEVEL = 1152
C_WIN = C_LEVEL + 2 * LEVELS * 64
C_IOTA = C_WIN + 64
C_TOK = C_IOTA + 128
C_N = C_TOK + TT


def shape_constants():
    r = np.arange(P)[:, None]
    c = np.arange(P)[None, :]
    t = np.zeros((P, C_N), np.float32)
    t[:, C_IDENT:C_IDENT + P] = r == c
    t[:, C_ONES:C_ONES + P] = 1
    t[:, C_FLIP:C_FLIP + P] = r + c == P - 1
    t[:, C_LE:C_LE + P] = r <= c
    t[:, C_GE:C_GE + P] = r >= c
    t[:, C_GT:C_GT + P] = r > c
    t[:, C_LT:C_LT + P] = r < c
    t[:, C_CAUSAL:C_CAUSAL + P] = np.where(c <= r, 0, NEG)
    t[:, C_CHUNK:C_CHUNK + P] = np.where(c // 64 <= r // 64, 0, NEG)
    for s in range(LEVELS):
        b = 1 << s
        first = [n for n in range(P) if (n // b) % 2 == 0]
        second = [n for n in range(P) if (n // b) % 2 == 1]
        same = lambda n: (r[:, 0] // (2 * b)) == n // (2 * b)
        for d, (cols, half) in enumerate(((first, 1), (second, 0))):
            for j, n in enumerate(cols):
                at = C_LEVEL + (d * LEVELS + s) * 64 + j
                t[:, at] = same(n) & ((r[:, 0] // b) % 2 == half)
    q = r % 64
    start = np.clip(q - 8, 0, 48)
    k = np.arange(64)[None, :]
    t[:, C_WIN:C_WIN + 64] = np.where((k >= start) & (k < start + 16), 0, NEG)
    t[:, C_IOTA:C_IOTA + P] = c
    t[:, C_TOK:C_TOK + TT] = r + P * np.arange(TT)[None, :]
    return t


R_BADA, R_NMIX, R_NFFN, R_CONVA, R_GCONV, R_C, R_C2, R_END = 0, 48, 56, 64, 70, 106, 114, 122
R2_BADA, R2_CONVB, R2_END = 0, 48, 92
NCH = 44


class Link:

    def __init__(self, sem):
        self.sem, self.n = sem, 0

    def on(self, eng):
        def run(ins):
            self.n += 1
            ins.then_inc(self.sem, 1)
            eng.wait_ge(self.sem, self.n)
        return run


class Weights:

    def __init__(self, ring, arrived):
        self.ring, self.arrived = ring, arrived
        self.plan, self.issued, self.begun, self.done = [], 0, 0, 0
        self.used, self.landed, self.full = {}, [0] * RING, {}

    def slot(self, n):
        return self.ring[:, n % RING, :]

    def begin(self, used):
        base = self.done = self.begun
        self.begun += len(used)
        self.used = {**{n: u for n, u in self.used.items() if n >= base - RING},
                     **{base + j: u for j, u in enumerate(used)}}
        return base

    def stream(self, sp):
        while self.issued < len(self.plan):
            n = self.issued
            if n - RING >= self.done:
                if n - RING not in self.used:
                    return
                sp.wait_ge(*self.used[n - RING])
            self.issued += 1
            srcs = self.plan[n]
            rows, width = srcs[0].shape[1], sum(src.shape[2] for src in srcs)
            dst = self.slot(n)[:, 0:rows * width].rearrange("p (k c) -> p k c", k=rows)
            at = 0
            for src in srcs:
                sp.dma_start(dst[:, :, at:at + src.shape[2]], src).then_inc(self.arrived[n % RING], 16)
                at += src.shape[2]
                self.landed[n % RING] += 16
            self.full[n] = self.landed[n % RING]

    def wait(self, pe, n):
        pe.wait_ge(self.arrived[n % RING], self.full[n])


class SplitWeights:

    def __init__(self, k, ctx, tag, rows, used):
        self.W, self.rows, self.used = k.W, rows, used
        self.rounded, self.ready = k.sem(f"{tag}_w_rounded"), k.sem(f"{tag}_w_ready")
        self.hi, self.lo = (k.sb(ctx, f"{tag}_w_{n}", [P, 2, KD * COLS // 2], F32R) for n in ("hi", "lo"))
        self.base = k.W.begin([(self.ready, 2 * n + 2) for n in range(len(rows))])

    def parts(self, p):
        rows, width = self.rows[p // 2]
        return [x[:, p % 2, 0:rows * width].rearrange("p (k c) -> p k c", k=rows) for x in (self.hi, self.lo)]

    def source(self, p):
        rows, width = self.rows[p // 2]
        slot = self.W.slot(self.base + p // 2)[:, 0:2 * rows * width].rearrange("p (k c) -> p k c", k=rows)
        return slot[:, :, (p % 2) * width:(p % 2 + 1) * width]

    def round(self, act, p):
        if p < 2 * len(self.rows):
            if p % 2 == 0:
                self.W.wait(act, self.base + p // 2)
            if p >= 2:
                act.wait_ge(*self.used[p - 2])
            act.activation(self.parts(p)[0], self.source(p), ACT.Copy).then_inc(self.rounded, 1)

    def rest(self, dve, p):
        if p < 2 * len(self.rows):
            hi, lo = self.parts(p)
            dve.wait_ge(self.rounded, p + 1)
            dve.tensor_tensor(lo, self.source(p), hi.bitcast(F32), ALU.subtract).then_inc(self.ready, 1)

    def wait(self, pe, p):
        pe.wait_ge(self.ready, p + 1)


def matmul3(pe, out, left, right, start, stop):
    pe.matmul(out, left[0], right[0], start=start, stop=False)
    pe.matmul(out, left[0], right[1], start=False, stop=False)
    return pe.matmul(out, left[1], right[0], start=False, stop=stop)


class Kernel:
    def __init__(self, nc, ins, out):
        self.nc, self.i, self.out = nc, ins, out
        self.stage_sems = []

    def sb(self, ctx, name, shape, dt=F32):
        return ctx.enter_context(self.nc.sbuf_tensor(name, shape, dt))

    def sem(self, name):
        handle = self.nc.alloc_semaphore(name=name)
        self.stage_sems.append(handle)
        return handle

    def retire_semaphores(self):
        with self.nc.Block() as block:
            @block.gpsimd
            def _(pool):
                self.nc.clear_and_free_semaphores(self.stage_sems)
        self.stage_sems = []
        self.W.used, self.W.done = {}, self.W.begun

    def cst(self, at, n=P):
        return self.const[:, at:at + n]

    def build(self):
        nc = self.nc
        with ExitStack() as root:
            self.root = root
            self.const = self.sb(root, "const", [P, C_N])
            self.X = self.sb(root, "X", [P, TT, D])
            self.ring = self.sb(root, "ring", [P, RING, KD * COLS])
            self.cols1 = self.sb(root, "cols1", [P, P])
            self.cols2 = self.sb(root, "cols2", [P, P])
            self.cols3 = self.sb(root, "cols3", [P, 3 * NCH])
            self.mods = self.sb(root, "mods", [P, 2, 48])
            self.mod = self.mods[:, 0, :]
            self.modA = self.sb(root, "modA", [P, 2, KD])
            self.gate = self.sb(root, "gate", [P, D])
            self.HT_life = ExitStack()
            self.HT = self.sb(self.HT_life, "HT", [P, KD, SEQ])
            self.psum = root.enter_context(nc.psum_tensor("psum", [P, 8, 512], F32))
            self.dve_link = Link(self.sem("dve_link"))
            self.act_link = Link(self.sem("act_link"))
            self.pool_link = Link(self.sem("pool_link"))
            self.W = Weights(self.ring, [self.sem(f"slot{j}_arrived") for j in range(RING)])
            self.stored = self.sem("stored")
            self.nstored = 0
            self.stage_sems = []
            self.stages()
            self.retire_semaphores()

    def stage_load(self):
        nc, i = self.nc, self.i
        self.loaded, self.x_loaded = self.sem("inputs_loaded"), self.sem("x_loaded")
        with ExitStack() as ctx:
            rows = self.sb(ctx, "rows", [P, 4, P])
            turned = self.sem("rows_turned")
            evac = self.sem("columns_ready")
            tile_rows = [R_END, R2_END, 2 * NCH, NCH]
            with nc.Block() as block:
                @block.sync
                def _(sp):
                    def vec(t, at, src, n):
                        sp.dma_start(rows[at:at + n, t, :], src.rearrange("(j p) -> j p", p=P)) \
                          .then_inc(self.loaded, 16)
                        count[0] += 16
                    count = [16]
                    sp.dma_start(self.const[:, :], i["shape_constants"]).then_inc(self.loaded, 16)
                    vec(0, R_BADA, i["b_ada"][0], 48)
                    vec(0, R_NMIX, i["norm_mix_w"][0], KD)
                    vec(0, R_NFFN, i["norm_ffn_w"][0], KD)
                    vec(0, R_CONVA, i["conv_a_w"][0].rearrange("k c -> (k c)"), 6)
                    vec(0, R_GCONV, i["gdn_conv_w"][0].rearrange("k c -> (k c)"), 36)
                    vec(0, R_C, i["c"][0], KD)
                    vec(0, R_C2, i["c_2"][0], KD)
                    vec(1, R2_BADA, i["b_ada_2"][0], 48)
                    vec(1, R2_CONVB, i["conv_b_2"][0], NCH)
                    vec(2, 0, i["conv_w_2"][0, 0:2].rearrange("k c -> (k c)"), 2 * NCH)
                    vec(3, 0, i["conv_w_2"][0, 2], NCH)
                    self.loaded_all = count[0]
                    for j in range(MSLOTS):
                        self.mod_load(sp, j)
                    sp.dma_start(self.X[:, :, :], i["x"][0].rearrange("(t p) d -> p t d", p=P)) \
                      .then_inc(self.x_loaded, 16)

                @block.tensor
                def _(pe):
                    pe.wait_ge(self.loaded, self.loaded_all)
                    for t, n in enumerate(tile_rows):
                        pe.transpose(self.psum[:, t, 0:n], rows[0:n, t, :],
                                     self.const[0:n, C_IDENT:C_IDENT + n]).then_inc(turned, 1)

                @block.vector
                def _(dve):
                    for t, (n, dst) in enumerate(zip(tile_rows, (
                            self.cols1[:, 0:R_END], self.cols2[:, 0:R2_END],
                            self.cols3[:, 0:2 * NCH], self.cols3[:, 2 * NCH:3 * NCH]))):
                        dve.wait_ge(turned, t + 1)
                        dve.tensor_copy(dst, self.psum[:, t, 0:n]).then_inc(evac, 1)

                @block.scalar
                def _(act):
                    act.wait_ge(evac, 1)
                    act.activation(self.cols1[:, R_C:R_END], self.cols1[:, R_C:R_END], ACT.Silu) \
                       .then_inc(evac, 1)

    def mod_begin(self, ctx, slots):
        self.mod_slots = slots
        self.macc = self.sb(ctx, "mod_acc", [P, MACC, MCOLS])
        self.m_arrived = [[self.sem(f"mod_slot{j}_arrived_{q}") for j in range(MSLOTS)] for q in ("sp", "pool")]
        self.m_acc, self.m_turned, self.m_kept = (self.sem(f"mod_{n}") for n in ("accumulated", "turned", "kept"))

    def mod_arrived(self, j):
        late = int(j >= MGROUP)
        before = len([n for n in range(MGROUP * late, j) if n % MSLOTS == j % MSLOTS])
        return self.m_arrived[late][j % MSLOTS], 16 * (before + 1)

    def mod_load(self, eng, j):
        if j >= MSLOTS:
            eng.wait_ge(self.m_acc, j - MSLOTS + 1)
        w = self.i[("w_ada", "w_ada_2")[j // MCHUNKS]][0].rearrange("(k p) c -> p k c", p=P)
        at = (j % MCHUNKS) * MCOLS
        eng.dma_start(self.mod_slots[j % MSLOTS], w[:, :, at:at + MCOLS]).then_inc(self.mod_arrived(j)[0], 16)

    def mod_accumulate(self, dve, j):
        link = self.dve_link.on(dve)
        w, acc = self.mod_slots[j % MSLOTS], self.macc[:, j % MACC, :]
        cond = self.cols1[:, R_C + KD * (j // MCHUNKS):]
        dve.wait_ge(*self.mod_arrived(j))
        if j >= MACC:
            dve.wait_ge(self.m_turned, j - MACC + 1)
        link(dve.tensor_scalar(acc, w[:, 0, :], cond[:, 0:1], None, ALU.mult))
        for k in range(1, KD):
            ins = dve.scalar_tensor_tensor(acc, w[:, k, :], cond[:, k:k + 1], acc, ALU.mult, ALU.add)
            if k < KD - 1:
                link(ins)
        ins.then_inc(self.m_acc, 1)

    def mod_turn(self, pe, j, c):
        g = j // MGROUP
        if c == 0:
            pe.wait_ge(self.m_acc, j + 1)
            if g >= 2 and j % MGROUP == 0:
                pe.wait_ge(self.m_kept, g - 1)
        col = (j % MGROUP) * (MCOLS // P) + c
        mm = pe.matmul(self.psum[:, 6 + g % 2, col:col + 1], self.macc[:, j % MACC, c * P:(c + 1) * P],
                       self.cst(C_ONES, 1), start=True, stop=True)
        if c == MCOLS // P - 1:
            mm.then_inc(self.m_turned, 1)

    def mod_keep(self, dve, g):
        n = MGROUP * MCOLS // P
        block, at = divmod(g * n, 6 * KD)
        b_ada = (self.cols1[:, R_BADA:R_NMIX], self.cols2[:, R2_BADA:R2_CONVB])[block]
        dve.wait_ge(self.m_turned, MGROUP * (g + 1))
        dve.tensor_tensor(self.mods[:, block, at:at + n], self.psum[:, 6 + g % 2, 0:n], b_ada[:, at:at + n],
                          ALU.add).then_inc(self.m_kept, 1)

    def stage_mod_first(self):
        with self.nc.Block() as block:
            @block.sync
            def _(sp):
                for j in range(MSLOTS, MGROUP):
                    self.mod_load(sp, j)
                self.W.stream(sp)

            @block.vector
            def _(dve):
                for j in range(MGROUP):
                    self.mod_accumulate(dve, j)
                self.mod_keep(dve, 0)

            @block.tensor
            def _(pe):
                for j in range(MGROUP):
                    for c in range(MCOLS // P):
                        self.mod_turn(pe, j, c)

            @block.scalar
            def _(act):
                act.wait_ge(self.x_loaded, 16)

    def stage_gate(self, tag, at, plus=0.0):
        nc = self.nc
        with ExitStack() as ctx:
            diag = self.sb(ctx, f"{tag}_diag", [P, KD, P])
            ready, summed = self.sem(f"{tag}_diag_ready"), self.sem(f"{tag}_summed")
            with nc.Block() as block:
                @block.vector
                def _(dve):
                    for k in range(KD):
                        dve.tensor_scalar(diag[:, k, :], self.cst(C_IDENT), self.mod[:, at + k:at + k + 1],
                                          None, ALU.mult).then_inc(ready, 1)
                    for b in range(2):
                        dve.wait_ge(summed, 4 * b + 4)
                        dve.tensor_scalar(self.gate[:, b * 512:(b + 1) * 512], self.psum[:, b, :], plus,
                                          None, ALU.add)

                @block.tensor
                def _(pe):
                    for k in range(KD):
                        pe.wait_ge(ready, k + 1)
                        pe.matmul(self.psum[:, k // 4, (k % 4) * P:(k % 4 + 1) * P], self.cst(C_ONES),
                                  diag[:, k, :], start=True, stop=True).then_inc(summed, 1)

    def row_stats(self, block, tag, ctx, eps, mean):
        rstd = self.sb(ctx, f"{tag}_rstd", [P, TT])
        mu = self.sb(ctx, f"{tag}_mean", [P, TT, 2])
        var = self.sb(ctx, f"{tag}_var", [P, TT])
        junk = self.sb(ctx, f"{tag}_junk", [P, D])
        bn = self.sb(ctx, f"{tag}_bn", [P, TT, 2, 6])
        s_var, s_std = self.sem(f"{tag}_var_ready"), self.sem(f"{tag}_std_ready")

        def on_dve(dve):
            link = self.dve_link.on(dve)
            if mean:
                for t in range(TT):
                    for h in range(2):
                        link(dve.bn_stats(bn[:, t, h, :], self.X[:, t, h * 512:(h + 1) * 512]))
                    link(dve.bn_aggr(mu[:, t, :], bn[:, t, :, :].rearrange("p h s -> p (h s)")))
                dve.tensor_scalar(var[:, :], mu[:, :, 1], eps, None, ALU.add).then_inc(s_var, TT)
            else:
                dve.wait_ge(s_var, TT)
                link(dve.tensor_scalar(var[:, :], var[:, :], 1.0 / D, eps, ALU.mult, ALU.add))
                dve.sem_inc(s_std, 1)
            dve.wait_ge(s_std, 2 - (1 if mean else 0))
            link(dve.reciprocal(rstd[:, :], var[:, :]))

        def on_act(act):
            if mean:
                act.wait_ge(s_var, TT)
            else:
                link = self.act_link.on(act)
                for t in range(TT):
                    link(act.activation(junk[:, :], self.X[:, t, :], ACT.Square,
                                        accum_out=var[:, t:t + 1]))
                act.sem_inc(s_var, TT)
                act.wait_ge(s_std, 1)
            act.activation(var[:, :], var[:, :], ACT.Sqrt).then_inc(s_std, 1)

        return rstd, mu, on_dve, on_act

    def stage_norm(self, tag, eps, mean, scale, shift, save_rows=None, split=None):
        nc = self.nc
        with ExitStack() as ctx:
            XN = self.sb(ctx, f"{tag}_XN", [P, TT, D])
            normed, turned, filled = (self.sem(f"{tag}_{n}") for n in ("rows_normed", "turned", "filled"))
            rounded = self.sem(f"{tag}_rounded")
            with nc.Block() as block:
                rstd, mu, stats_dve, stats_act = self.row_stats(block, tag, ctx, eps, mean)

                @block.vector
                def _(dve):
                    stats_dve(dve)
                    for t in range(TT):
                        if mean:
                            ins = dve.tensor_scalar(XN[:, t, :], self.X[:, t, :], mu[:, t, 0:1],
                                                    rstd[:, t:t + 1], ALU.subtract, ALU.mult)
                        else:
                            ins = dve.tensor_scalar(XN[:, t, :], self.X[:, t, :], rstd[:, t:t + 1],
                                                    None, ALU.mult)
                        ins.then_inc(normed, 1)
                    for k in range(0, KD, 2):
                        dve.wait_ge(turned, k + 1)
                        dve.tensor_scalar(self.HT[:, k, :], self.psum[:, k, :], scale[:, k:k + 1],
                                          shift[:, k:k + 1], ALU.mult, ALU.add).then_inc(filled, 1)
                    for k in range(KD if split else 0):
                        dve.wait_ge(rounded, k + 1)
                        dve.tensor_tensor(split[1][:, k, :], self.HT[:, k, :], split[0][:, k, :].bitcast(F32),
                                          ALU.subtract)

                @block.tensor
                def _(pe):
                    pe.wait_ge(normed, TT)
                    for k in range(KD):
                        for t in range(TT):
                            tr = pe.transpose(self.psum[:, k, t * P:(t + 1) * P],
                                              XN[:, t, k * P:(k + 1) * P], self.cst(C_IDENT))
                        tr.then_inc(turned, 1)

                @block.scalar
                def _(act):
                    stats_act(act)
                    for k in range(1, KD, 2):
                        act.wait_ge(turned, k + 1)
                        act.activation(self.HT[:, k, :], self.psum[:, k, :], ACT.Identity,
                                       scale=scale[:, k:k + 1], bias=shift[:, k:k + 1]).then_inc(filled, 1)
                    if split:
                        act.wait_ge(filled, KD)
                        for k in range(KD):
                            act.activation(split[0][:, k, :], self.HT[:, k, :], ACT.Copy).then_inc(rounded, 1)

                @block.sync
                def _(sp):
                    self.W.stream(sp)
                    if save_rows is not None:
                        sp.wait_ge(normed, TT)
                        self.nstored += 16
                        sp.dma_start(save_rows.rearrange("(t p) d -> p t d", p=P), XN[:, :, :]) \
                          .then_inc(self.stored, 16)
                        sp.wait_ge(self.stored, self.nstored)

    def stage_scale(self, tag, gain, scale_at):
        nc = self.nc
        with nc.Block() as block:
            @block.vector
            def _(dve):
                link = self.dve_link.on(dve)
                link(dve.tensor_scalar(self.modA[:, 0, :], self.mod[:, scale_at:scale_at + KD], 1.0, None,
                                       ALU.add))
                if gain is not None:
                    link(dve.tensor_tensor(self.modA[:, 0, :], self.modA[:, 0, :], gain, ALU.mult))

    def stage_proj1(self, B):
        nc, W = self.nc, self.W
        widths = [COLS] * 7 + [16]
        items = []
        for n, names in enumerate((("cb", "cb", "cc", "cc"), ("cx", "cx", "nq", "nq"), ("nk", "nk", None, None))):
            items += [(n, what, c, c % 2) for c, what in enumerate(names) if what]
        items += [(2, "nv", t, t) for t in range(TT)]
        items += [(3 + n, "g", c, 4 * n + c) for n in range(3) for c in range(4)]
        items += [(6, "gz", t, t) for t in range(TT)] + [(7, "gab", t, t) for t in range(TT)]
        last = {it[0]: n for n, it in enumerate(items)}
        BANKS = 6
        with ExitStack() as ctx:
            CB = self.sb(ctx, "CB", [P, 2, SEQ])
            CC = self.sb(ctx, "CC", [P, 2, SEQ])
            PAD = self.sb(ctx, "PAD", [P, 4, SEQ + 2])
            CV = self.sb(ctx, "CV", [P, 2, SEQ])
            summed, copied = self.sem("proj1_summed"), self.sem("proj1_copied")
            zeroed, conved, silued = self.sem("pads_zeroed"), self.sem("conv_done"), self.sem("silu_done")
            base = W.begin([(summed, last[ld] + 1) for ld in range(len(widths))])
            MOD_LAG = 2
            late = 2 * MCHUNKS - MGROUP
            long_items = len(items) - TT
            chunks_of = lambda n: range(MGROUP + min(late, late * max(n, 0) // long_items),
                                        MGROUP + min(late, late * max(n + 1, 0) // long_items))
            with nc.Block() as block:
                @block.sync
                def _(sp):
                    W.stream(sp)

                @block.gpsimd
                def _(pool):
                    for j in range(MGROUP, 2 * MCHUNKS):
                        self.mod_load(pool, j)

                @block.tensor
                def _(pe):
                    for n, (ld, what, c, _) in enumerate(items):
                        turns = [(j, cc) for j in chunks_of(n - MOD_LAG) for cc in range(MCOLS // P)]
                        if n == 0 or items[n - 1][0] != ld:
                            W.wait(pe, base + ld)
                        if n >= BANKS:
                            pe.wait_ge(copied, n - BANKS + 1)
                        width = widths[ld]
                        slot = W.slot(base + ld)[:, 0:KD * width].rearrange("p (k c) -> p k c", k=KD)
                        bank = self.psum[:, n % BANKS, :]
                        for k in range(KD):
                            if turns and k:
                                self.mod_turn(pe, *turns.pop(0))
                            if what in ("nv", "gz", "gab"):
                                cols = slice(256, 512) if what == "nv" else slice(0, width)
                                wk = slot[:, k, cols]
                                mm = pe.matmul(bank[:, 0:wk.shape[1]], self.HT[:, k, c * P:(c + 1) * P], wk,
                                               start=(k == 0), stop=(k == KD - 1))
                            else:
                                mm = pe.matmul(bank, slot[:, k, c * P:(c + 1) * P], self.HT[:, k, :],
                                               start=(k == 0), stop=(k == KD - 1))
                        mm.then_inc(summed, 1)

                @block.scalar
                def _(act):
                    act.wait_ge(zeroed, 1)
                    def silu(m):
                        if m >= 2:
                            act.wait_ge(conved, m + 1)
                            act.activation(B.G[:, m - 2, :], CV[:, m % 2, :], ACT.Silu).then_inc(silued, 1)
                    m = 0
                    for n, (_, what, c, at) in enumerate(items):
                        act.wait_ge(summed, n + 1)
                        bank = self.psum[:, n % BANKS, :]
                        if what in ("cx", "g"):
                            if m >= 4:
                                act.wait_ge(conved, m - 3)
                            dst = PAD[:, m % 4, 1:SEQ + 1]
                        else:
                            dst = {"cb": CB, "cc": CC, "nq": B.NQ, "nk": B.NK, "nv": B.NV, "gz": B.GZ,
                                   "gab": B.GAB}[what][:, at, :]
                        act.activation(dst, bank[:, 0:dst.shape[1]], ACT.Copy,
                                       scale=HD ** -0.5 if what == "nq" else 1.0).then_inc(copied, 1)
                        if what in ("cx", "g"):
                            m += 1
                            if m >= 2:
                                silu(m - 2)
                    silu(m - 2)
                    silu(m - 1)

                @block.vector
                def _(dve):
                    link = self.dve_link.on(dve)
                    dve.memset(PAD[:, :, :], 0.0).then_inc(zeroed, 1)
                    m = -1
                    for n, (_, what, _, at) in enumerate(items):
                        for j in chunks_of(n):
                            self.mod_accumulate(dve, j)
                        for j in chunks_of(n - 2 * MOD_LAG):
                            if j % MGROUP == MGROUP - 1:
                                self.mod_keep(dve, j // MGROUP)
                        if what not in ("cx", "g"):
                            continue
                        m += 1
                        dve.wait_ge(copied, n + 1)
                        src = PAD[:, m % 4, :]
                        if what == "cx":
                            link(dve.tensor_tensor(src[:, 1:SEQ + 1], src[:, 1:SEQ + 1], CC[:, at, :], ALU.mult))
                            tap = lambda j: self.cols1[:, R_CONVA + 2 * j + at:R_CONVA + 2 * j + at + 1]
                        else:
                            tap = lambda j: self.cols1[:, R_GCONV + 12 * j + at:R_GCONV + 12 * j + at + 1]
                        if m >= 4:
                            dve.wait_ge(silued, m - 3)
                        cv = CV[:, m % 2, :]
                        link(dve.tensor_scalar(cv, src[:, 0:SEQ], tap(0), None, ALU.mult))
                        link(dve.scalar_tensor_tensor(cv, src[:, 1:SEQ + 1], tap(1), cv, ALU.mult, ALU.add))
                        ins = dve.scalar_tensor_tensor(cv, src[:, 2:SEQ + 2], tap(2), cv, ALU.mult, ALU.add)
                        if what == "cx":
                            link(ins)
                            dve.tensor_tensor(B.YT[:, at, :], CB[:, at, :], cv, ALU.mult).then_inc(conved, 1)
                        else:
                            ins.then_inc(conved, 1)

    def stage_attention(self, tag, heads, qT, kT, vals, bias, width, outT, cum=None):
        nc = self.nc
        units = [(h, t) for h in range(heads) for t in range(TT)]
        N = len(units)
        with ExitStack() as ctx:
            S = self.sb(ctx, f"{tag}_S", [P, AHEAD, SEQ])
            PR = self.sb(ctx, f"{tag}_PR", [P, AHEAD, SEQ])
            PT = self.sb(ctx, f"{tag}_PT", [P, 2, TT, SEQ])
            mx = self.sb(ctx, f"{tag}_max", [P, N])
            sm = self.sb(ctx, f"{tag}_sum", [P, N])
            DEC = self.sb(ctx, f"{tag}_decay", [P, AHEAD, SEQ]) if cum else None
            names = "scored maxed exped normed turned kept valued headed rowed biased"
            scored, maxed, exped, normed, turned, kept, valued, headed, rowed, biased = (
                self.sem(f"{tag}_{n}") for n in names.split())
            score_bank = lambda u: self.psum[:, (0, 1, 6)[u % AHEAD], :]
            turn_bank = lambda u: self.psum[:, 2 + u % 2, :]
            out_bank = lambda h: self.psum[:, 4 + h % 2, :]
            row_bank = self.psum[:, 7, :]
            def head_out(dve, h):
                at = HD * (h % 2)
                dve.wait_ge(valued, h + 1)
                dve.tensor_copy(outT(h), out_bank(h)[at:at + HD, :]).then_inc(headed, 1)

            with nc.Block() as block:
                @block.sync
                def _(sp):
                    self.W.stream(sp)

                @block.tensor
                def _(pe):
                    def scores(u):
                        h, t = units[u]
                        if cum and t == 0:
                            if h >= 1:
                                pe.wait_ge(biased, TT * h)
                            pe.matmul(row_bank, cum[1](h), cum[2], start=True, stop=True).then_inc(rowed, 1)
                        if u >= AHEAD:
                            pe.wait_ge(maxed, u - AHEAD + 1)
                        w = width(t)
                        mm = pe.matmul(score_bank(u)[:, 0:w], qT(h)[:, t * P:(t + 1) * P], kT(h)[:, 0:w],
                                       start=True, stop=not cum)
                        if cum:
                            mm = pe.matmul(score_bank(u)[:, w - P:w], self.cst(C_IDENT), self.cst(C_CAUSAL),
                                           start=False, stop=True)
                        mm.then_inc(scored, 1)

                    def turn(u):
                        h, t = units[u]
                        pe.wait_ge(normed, u + 1)
                        if u >= 2:
                            pe.wait_ge(kept, u - 1)
                        for j in range(width(t) // P):
                            tr = pe.transpose(turn_bank(u)[:, j * P:(j + 1) * P], PR[:, u % AHEAD, j * P:(j + 1) * P],
                                              self.cst(C_IDENT))
                        tr.then_inc(turned, 1)

                    def values(h):
                        pe.wait_ge(kept, TT * (h + 1))
                        if h >= 2:
                            pe.wait_ge(headed, h - 1)
                        at = HD * (h % 2)
                        for j in range(TT):
                            q0 = 0 if width(0) == SEQ else j * P
                            mm = pe.matmul(out_bank(h)[at:at + HD, q0:], vals(h, j), PT[:, h % 2, j, q0:],
                                           start=(j == 0), stop=(j == TT - 1))
                        mm.then_inc(valued, 1)

                    for u in range(AHEAD - 1):
                        scores(u)
                    for u in range(N):
                        if u + AHEAD - 1 < N:
                            scores(u + AHEAD - 1)
                        turn(u)
                        if u >= TT and u % TT == 0:
                            values(u // TT - 1)
                    values(heads - 1)

                @block.vector
                def _(dve):
                    link = self.dve_link.on(dve)

                    def top(u):
                        h, t = units[u]
                        w = width(t)
                        dve.wait_ge(scored, u + 1)
                        if cum:
                            dve.wait_ge(biased, u + 1)
                        if u >= AHEAD:
                            dve.wait_ge(exped, u - AHEAD + 1)
                        add = DEC[:, u % AHEAD, 0:w] if cum else bias(h, t)
                        s, b = S[:, u % AHEAD, 0:w], score_bank(u)[:, 0:w]
                        if len(add.shape) == 3:
                            g = add.shape[1]
                            s, b = (x.rearrange("p (g k) -> p g k", g=g) for x in (s, b))
                        link(dve.tensor_tensor_reduce(s, b, add, 1.0, -3e38, ALU.add, ALU.max, mx[:, u:u + 1]))
                        dve.tensor_scalar(mx[:, u:u + 1], mx[:, u:u + 1], -1.0, None, ALU.mult).then_inc(maxed, 1)

                    def norm(u):
                        w = width(units[u][1])
                        dve.wait_ge(exped, u + 1)
                        link(dve.reciprocal(sm[:, u:u + 1], sm[:, u:u + 1]))
                        dve.tensor_scalar(PR[:, u % AHEAD, 0:w], PR[:, u % AHEAD, 0:w], sm[:, u:u + 1], None, ALU.mult) \
                           .then_inc(normed, 1)

                    for u in range(AHEAD - 1):
                        top(u)
                    for u in range(N):
                        norm(u)
                        if u + AHEAD - 1 < N:
                            top(u + AHEAD - 1)
                        if u % TT == 0 and u >= TT:
                            head_out(dve, u // TT - 1)
                    head_out(dve, heads - 1)

                @block.scalar
                def _(act):
                    def decay(u):
                        h, t = units[u]
                        w = width(t)
                        act.wait_ge(rowed, h + 1)
                        if u >= AHEAD:
                            act.wait_ge(maxed, u - AHEAD + 1)
                        act.activation(DEC[:, u % AHEAD, 0:w], row_bank[:, 0:w], ACT.Identity, scale=-1.0,
                                       bias=cum[0](t, h)).then_inc(biased, 1)

                    def exps(u):
                        w = width(units[u][1])
                        act.wait_ge(maxed, u + 1)
                        if u >= AHEAD:
                            act.wait_ge(turned, u - AHEAD + 1)
                        act.activation(PR[:, u % AHEAD, 0:w], S[:, u % AHEAD, 0:w], ACT.Exp, bias=mx[:, u:u + 1],
                                       accum_out=sm[:, u:u + 1]).then_inc(exped, 1)

                    def keep(u):
                        h, t = units[u]
                        w = width(t)
                        act.wait_ge(turned, u + 1)
                        if h >= 2:
                            act.wait_ge(valued, h - 1)
                        act.activation(PT[:, h % 2, 0:w // P, t * P:(t + 1) * P],
                                       turn_bank(u)[:, 0:w].rearrange("p (j q) -> p j q", q=P), ACT.Copy) \
                           .then_inc(kept, 1)

                    if cum:
                        for u in range(AHEAD):
                            decay(u)
                    for u in range(AHEAD - 1):
                        exps(u)
                    for u in range(N):
                        if cum and u + AHEAD < N:
                            decay(u + AHEAD)
                        if u + AHEAD - 1 < N:
                            exps(u + AHEAD - 1)
                        keep(u)

    def stage_na(self, B):
        nc = self.nc
        NR, HEADW = 14, 127
        with ExitStack() as ctx:
            hank = self.HT[:, :, :].rearrange("p k s -> p (k s)")[:, 0:NA_H * NR * 64]
            bias = self.sb(ctx, "na_bias", [P, NA_H, NR, 64])
            laid, flipped = self.sem("na_bias_laid"), self.sem("na_bias_flipped")
            made = self.sem("na_bias_made")
            half = 7 * 64
            with nc.Block() as block:
                @block.sync
                def _(sp):
                    src = self.i["na_rpb"]
                    for part in range(2):
                        for h in range(NA_H):
                            sp.dma_start(
                                hank[part * 64:(part + 1) * 64, h * NR * 64:(h + 1) * NR * 64]
                                .rearrange("p (r c) -> p r c", r=NR),
                                bass.AP(src.tensor, (h * 15 + part) * HEADW, [[1, 64], [HEADW, NR], [1, 64]])) \
                              .then_inc(laid, 16)

                @block.tensor
                def _(pe):
                    pe.wait_ge(laid, 2 * NA_H * 16)
                    for j in range(2 * NA_H):
                        pe.matmul(self.psum[:, j, 0:half], self.cst(C_FLIP), hank[:, j * half:(j + 1) * half],
                                  start=True, stop=True).then_inc(flipped, 1)

                @block.vector
                def _(dve):
                    win = self.cst(C_WIN, 64).unsqueeze(1).to_broadcast([P, 7, 64])
                    for j in range(2 * NA_H):
                        dve.wait_ge(flipped, j + 1)
                        dve.tensor_tensor(bias[:, j // 2, (j % 2) * 7:(j % 2 + 1) * 7, :],
                                          self.psum[:, j, 0:half].rearrange("p (r c) -> p r c", r=7), win,
                                          ALU.add).then_inc(made, 1)
            rows = lambda h: slice(HD * (h % 2), HD * (h % 2 + 1))
            self.stage_attention(
                "na", NA_H, lambda h: B.NQ[rows(h), h // 2, :], lambda h: B.NK[rows(h), h // 2, :],
                lambda h, j: B.NV[:, j, h * HD:(h + 1) * HD],
                lambda h, t: bias[:, h, 6 - 2 * t:14 - 2 * t, :].rearrange("p r c -> p (r c)"),
                lambda t: SEQ, lambda h: B.YT[rows(h), 2 + h // 2, :])

    def stage_gdn_prep(self, B, ctx):
        nc, i = self.nc, self.i
        slot = lambda n: self.ring[:, n, :]
        B.LKK = slot(0)[:, 0:2048].rearrange("p (t h j) -> p t h j", t=TT, h=GH)
        B.KQ = slot(0)[:, 2048:4096].rearrange("p (t h j) -> p t h j", t=TT, h=GH)
        flat = self.HT[:, :, :].rearrange("p k s -> p (k s)")
        B.KR = flat[:, 0:2048].rearrange("p (t h c) -> p t h c", t=TT, h=GH)
        B.VR = flat[:, 2048:4096].rearrange("p (t h c) -> p t h c", t=TT, h=GH)
        SQ = slot(2).rearrange("p (c s) -> p c s", c=8)
        alog = self.sb(ctx, "a_log", [P, 8])
        dtb = self.sb(ctx, "dt_bias", [P, 8])
        B.gnw = self.sb(ctx, "gdn_norm_gain", [P, P])
        B.g = self.sb(ctx, "g", [P, TT, 8])
        B.beta = self.sb(ctx, "beta", [P, TT, 8])
        B.rqk = self.sb(ctx, "rqk", [P, TT, 8])
        B.ex = self.sb(ctx, "decays", [P, 3, TT, 8])
        B.brk = self.sb(ctx, "beta_rk", [P, TT, 8])
        B.nbG = self.sb(ctx, "minus_beta_decay_rk", [P, TT, 8])
        B.req = self.sb(ctx, "rq_decay", [P, TT, 8])
        tmp = self.sb(ctx, "softplus_tmp", [P, 4, TT * 8])
        names = "loaded squared summed rooted minus_abs exped summed_g exped_g tiled evacuated sigmoided v_copied"
        (loaded, squared, summed, rooted, absed, exped, summed_g, exped_g, tiled, evac, sigm, vcop) = (
            self.sem("gp_" + n) for n in names.split())
        with nc.Block() as block:
            @block.sync
            def _(sp):
                for dst, src, n in ((alog, i["gdn_a_log"], 8), (dtb, i["gdn_dt_bias"], 8), (B.gnw, i["gdn_norm_w"], P)):
                    sp.dma_start(dst[:, :], bass.AP(src.tensor, 0, [[0, P], [1, n]])).then_inc(loaded, 16)

            @block.scalar
            def _(act):
                for c in range(8):
                    act.activation(SQ[:, c, :], B.G[:, c, :], ACT.Square).then_inc(squared, 1)
                act.wait_ge(rooted, 1)
                act.activation(B.rqk[:, :, :], B.rqk[:, :, :], ACT.Sqrt).then_inc(rooted, 1)
                act.activation(B.beta[:, :, :], B.GAB[:, :, 8:16], ACT.Sigmoid).then_inc(sigm, 1)
                act.wait_ge(absed, 1)
                act.activation(tmp[:, 1, :], tmp[:, 1, :], ACT.Exp, scale=-1.0).then_inc(exped, 1)
                act.wait_ge(loaded, 48)
                act.activation(alog[:, :], alog[:, :], ACT.Exp).then_inc(exped, 1)
                act.wait_ge(summed_g, 1)
                act.activation(B.ex[:, :, :, :].rearrange("p a t h -> p (a t h)"), self.psum[:, 6, 0:96], ACT.Exp) \
                   .then_inc(exped_g, 1)
                for t in range(TT):
                    act.wait_ge(tiled, t + 1)
                    act.activation(B.VR[:, t, :, :].rearrange("p h c -> p (h c)"), self.psum[:, 1, :], ACT.Copy) \
                       .then_inc(vcop, 1)

            @block.tensor
            def _(pe):
                pe.wait_ge(squared, 8)
                for t in range(TT):
                    for c in range(8):
                        mm = pe.matmul(self.psum[:, 7, t * 8 + c:t * 8 + c + 1], SQ[:, c, t * P:(t + 1) * P],
                                       self.cst(C_ONES, 1), start=True, stop=True)
                mm.then_inc(summed, 1)
                pe.wait_ge(evac, 1)
                for t in range(TT):
                    for d in range(2):
                        for kind, tri in enumerate(((C_LE, C_GE)[d], (C_GT, C_LT)[d], C_ONES)):
                            at = kind * 32 + t * 8 + d * 4
                            mm = pe.matmul(self.psum[:, 6, at:at + 4], self.cst(tri), B.g[:, t, d * 4:d * 4 + 4],
                                           start=True, stop=True)
                mm.then_inc(summed_g, 1)
                for t in range(TT):
                    cols = slice(t * P, (t + 1) * P)
                    if t:
                        pe.wait_ge(evac, 1 + t)
                        pe.wait_ge(vcop, t)
                    for h in range(GH):
                        to = slice(h * P, (h + 1) * P)
                        kt, qt = B.G[:, 4 + h, cols], B.G[:, h, cols]
                        pe.transpose(self.psum[:, 0, to], kt, self.cst(C_IDENT))
                        pe.transpose(self.psum[:, 1, to], B.G[:, 8 + h, cols], self.cst(C_IDENT))
                        pe.matmul(self.psum[:, 2, to], kt, kt, start=True, stop=True)
                        mm = pe.matmul(self.psum[:, 3, to], kt, qt, start=True, stop=True)
                    mm.then_inc(tiled, 1)

            @block.vector
            def _(dve):
                link = self.dve_link.on(dve)
                dve.wait_ge(summed, 1)
                link(dve.tensor_scalar(B.rqk[:, :, :].rearrange("p t c -> p (t c)"), self.psum[:, 7, 0:32], EPS,
                                       None, ALU.add))
                dve.sem_inc(rooted, 1)
                x, u, s2, acc = (tmp[:, n, :] for n in range(4))
                xt = x.rearrange("p (t c) -> p t c", t=TT)
                dve.wait_ge(loaded, 48)
                link(dve.tensor_tensor(xt, B.GAB[:, :, 0:8], dtb[:, :].unsqueeze(1).to_broadcast([P, TT, 8]), ALU.add))
                link(dve.tensor_scalar(u, x, -1.0, None, ALU.mult))
                link(dve.tensor_tensor(u, u, x, ALU.max))
                dve.sem_inc(absed, 1)
                dve.wait_ge(exped, 1)
                self.log1p(dve, link, u, s2, acc, acc)
                link(dve.scalar_tensor_tensor(x, x, 0.0, acc, ALU.max, ALU.add))
                dve.wait_ge(exped, 2)
                link(dve.scalar_tensor_tensor(B.g[:, :, :], xt, -1.0,
                                              alog[:, :].unsqueeze(1).to_broadcast([P, TT, 8]), ALU.mult, ALU.mult))
                dve.sem_inc(evac, 1)
                dve.wait_ge(rooted, 2)
                link(dve.reciprocal(B.rqk[:, :, :], B.rqk[:, :, :]))
                link(dve.tensor_scalar(B.rqk[:, :, 0:4], B.rqk[:, :, 0:4], 128 ** -0.5, None, ALU.mult))
                rk = lambda t: B.rqk[:, t, 4:8].unsqueeze(2).to_broadcast([P, GH, P])
                for t in range(TT):
                    dve.wait_ge(tiled, t + 1)
                    for bank, dst in ((0, B.KR), (2, B.LKK), (3, B.KQ)):
                        ins = dve.tensor_tensor(dst[:, t, :, :],
                                                self.psum[:, bank, :].rearrange("p (h j) -> p h j", h=GH), rk(t), ALU.mult)
                    ins.then_inc(evac, 1)
                dve.wait_ge(sigm, 1)
                dve.wait_ge(exped_g, 1)
                for d in range(2):
                    at = slice(4 * d, 4 * d + 4)
                    dve.tensor_tensor(B.brk[:, :, at], B.beta[:, :, at], B.rqk[:, :, 4:8], ALU.mult)
                    dve.tensor_tensor(B.req[:, :, at], B.ex[:, 0, :, at], B.rqk[:, :, 0:4], ALU.mult)
                link(dve.tensor_scalar(B.nbG[:, :, :], B.ex[:, 0, :, :], -1.0, None, ALU.mult))
                dve.tensor_tensor(B.nbG[:, :, :], B.nbG[:, :, :], B.brk[:, :, :], ALU.mult)

    def stage_gdn(self, B):
        nc = self.nc
        PAIRS = [(n, d) for n in range(TT) for d in range(2)]
        tile_of = lambda n, d: n if d == 0 else TT - 1 - n
        bc = lambda ap: ap.unsqueeze(2).to_broadcast([P, GH, P])
        over = lambda ap: ap.unsqueeze(1).to_broadcast([P, GH, P])

        def half(x, s, sel):
            return x.rearrange("p (g two b) -> p g two b", two=2, b=1 << s)[:, :, sel, :]

        def split(x, s):
            return x.rearrange("p (g b) -> p g b", b=1 << s)

        with ExitStack() as ctx:
            quad = [P, 2, GH, P]
            E = self.sb(ctx, "gdn_decay", quad)
            LT, IT = self.sb(ctx, "gdn_LT", [P, 2] + quad[1:]), self.sb(ctx, "gdn_IT", [P, 2] + quad[1:])
            T, U = self.sb(ctx, "gdn_T", quad), self.sb(ctx, "gdn_TT", quad)
            VB, KE = self.sb(ctx, "gdn_vb", quad), self.sb(ctx, "gdn_ke", quad)
            R, VN = self.sb(ctx, "gdn_rest", quad), self.sb(ctx, "gdn_vnew", quad)
            S = self.sb(ctx, "gdn_state", quad)
            OT = self.sb(ctx, "gdn_out_tmp", [P, 2, GH, P])
            Y = [self.ring[:, 2 - d, 0:LEVELS * 512].rearrange("p (s h c) -> p s h c", s=LEVELS, h=GH) for d in range(2)]
            names = ("masked diffed decayed decay_masked products y_summed y_kept z_summed updated inited scaled "
                     "ks_summed r_ready v_summed v_kept o_summed state_done out_done cleared")
            (masked, diffed, decayed, dmasked, products, y_summed, y_kept, z_summed, updated, inited, scaled,
             ks_summed, r_ready, v_summed, v_kept, o_summed, state_done, out_done, cleared) = (
                self.sem("gdn_" + n) for n in names.split())
            bank = lambda d, n: self.psum[:, 4 * d + n, :]
            heads = lambda x: x.rearrange("p (h c) -> p h c", h=GH)
            idx = lambda n, s, d: (n * LEVELS + s) * 2 + d
            zeros = self.sb(ctx, "gdn_zeros", [P, 512])
            with nc.Block() as block:
                @block.sync
                def _(sp):
                    sp.wait_ge(cleared, 5)
                    lo = 2 * SEQ // P
                    rows = self.ys[lo * P:NBMAX * P, :].rearrange("(n p) d -> p n d", p=P)
                    for c in range(2):
                        self.nstored += 16
                        sp.dma_start(rows[:, :, c * 512:(c + 1) * 512],
                                     zeros[:, :].unsqueeze(1).to_broadcast([P, NBMAX - lo, 512])) \
                          .then_inc(self.stored, 16)
                    sp.wait_ge(self.stored, self.nstored)

                @block.gpsimd
                def _(pool):
                    for d in range(2):
                        pool.memset(self.ring[:, 2 - d, 0:LEVELS * 512], 0.0).then_inc(cleared, 1)
                        pool.memset(S[:, d, :, :], 0.0).then_inc(cleared, 1)
                    pool.memset(zeros[:, :], 0.0).then_inc(cleared, 1)

                    def mask(q):
                        n, d = PAIRS[q]
                        if n:
                            pool.wait_ge(products, q - 1)
                        pool.tensor_tensor(E[:, d, :, :], over(self.cst((C_LE, C_GE)[d])),
                                           bc(B.g[:, tile_of(n, d), 4 * d:4 * d + 4]), ALU.mult).then_inc(masked, 1)

                    def mask_decay(q):
                        d = PAIRS[q][1]
                        pool.wait_ge(decayed, q + 1)
                        pool.tensor_tensor(E[:, d, :, :], E[:, d, :, :], over(self.cst((C_LE, C_GE)[d])),
                                           ALU.mult).then_inc(dmasked, 1)

                    def scale(q):
                        n, d = PAIRS[q]
                        t, hs = tile_of(n, d), slice(4 * d, 4 * d + 4)
                        if n:
                            pool.wait_ge(o_summed, q - 1)
                        pool.tensor_tensor(VB[:, d, :, :], B.VR[:, t, :, :], bc(B.beta[:, t, hs]), ALU.mult)
                        pool.tensor_tensor(KE[:, d, :, :], B.KR[:, t, :, :], bc(B.ex[:, 1, t, hs]),
                                           ALU.mult).then_inc(scaled, 1)

                    def both(step, n):
                        for d in range(2 if n < TT else 0):
                            step(2 * n + d)
                    both(mask, 0)
                    both(mask_decay, 0)
                    for n in range(TT):
                        both(scale, n)
                        both(mask, n + 1)
                        both(mask_decay, n + 1)

                @block.scalar
                def _(act):
                    def decay(n):
                        for d in range(2 if n < TT else 0):
                            act.wait_ge(diffed, 2 * n + d + 1)
                            act.activation(E[:, d, :, :], heads(bank(d, 0)), ACT.Exp).then_inc(decayed, 1)
                    decay(0)
                    for n in range(TT):
                        decay(n + 1)
                        for d in range(2):
                            act.wait_ge(v_summed, 2 * n + d + 1)
                            act.activation(VN[:, d, :, :], heads(bank(d, 2)), ACT.Copy).then_inc(v_kept, 1)

                @block.tensor
                def _(pe):
                    def differences(n):
                        for d in range(2 if n < TT else 0):
                            q = 2 * n + d
                            pe.wait_ge(masked, q + 1)
                            if n:
                                pe.wait_ge(r_ready, q - 1)
                            pe.matmul(bank(d, 0), self.cst((C_GT, C_LT)[d]), E[:, d, :, :].rearrange("p h i -> p (h i)"),
                                      start=True, stop=True).then_inc(diffed, 1)

                    def keys_state(n):
                        for d in range(2):
                            q = 2 * n + d
                            cols = slice(tile_of(n, d) * P, (tile_of(n, d) + 1) * P)
                            pe.wait_ge(decayed, q + 1)
                            if n:
                                pe.wait_ge(out_done, q - 1)
                                pe.wait_ge(state_done, q - 1)
                            for h in range(GH):
                                mm = pe.matmul(bank(d, 0)[:, h * P:(h + 1) * P], B.G[:, GH + h, cols], S[:, d, h, :],
                                               start=True, stop=True)
                            mm.then_inc(ks_summed, 1)

                    pe.wait_ge(cleared, 4)
                    differences(0)
                    for n in range(TT):
                        for s in range(LEVELS):
                            for d in range(2):
                                q = 2 * n + d
                                if s == 0:
                                    pe.wait_ge(products, q + 1)
                                    pe.wait_ge(inited, q + 1)
                                else:
                                    pe.wait_ge(updated, idx(n, s - 1, d) + 1)
                                for h in range(GH):
                                    mm = pe.matmul(split(bank(d, 1)[:, h * 64:(h + 1) * 64], s), LT[:, n % 2, d, h, :],
                                                   half(T[:, d, h, :], s, d), start=True, stop=True)
                                mm.then_inc(y_summed, 1)
                            for d in range(2):
                                pe.wait_ge(y_kept, idx(n, s, d) + 1)
                                for h in range(GH):
                                    if 0 < s < LEVELS - 1:
                                        pe.matmul(split(bank(d, 2)[:, h * 64:(h + 1) * 64], s), U[:, d, h, :],
                                                  half(Y[d][:, s, h, :], s, d), start=True, stop=True)
                                    mm = pe.matmul(split(bank(d, 2)[:, 256 + h * 64:256 + (h + 1) * 64], s),
                                                   Y[d][:, s, h, :], half(U[:, d, h, :], s, 1 - d),
                                                   start=True, stop=True)
                                mm.then_inc(z_summed, 1)
                            if s == 1:
                                keys_state(n)
                            if s == 3:
                                differences(n + 1)
                        for d in range(2):
                            q = 2 * n + d
                            cols = slice(tile_of(n, d) * P, (tile_of(n, d) + 1) * P)
                            for h in range(GH):
                                pe.matmul(bank(d, 1)[:, h * P:(h + 1) * P], B.G[:, h, cols], S[:, d, h, :],
                                          start=True, stop=True)
                            pe.wait_ge(updated, idx(n, LEVELS - 1, d) + 1)
                            pe.wait_ge(r_ready, q + 1)
                            for h in range(GH):
                                mm = pe.matmul(bank(d, 2)[:, h * P:(h + 1) * P], U[:, d, h, :], R[:, d, h, :],
                                               start=True, stop=True)
                            mm.then_inc(v_summed, 1)
                        for d in range(2):
                            q = 2 * n + d
                            pe.wait_ge(v_kept, q + 1)
                            if n + 1 < TT:
                                pe.wait_ge(decayed, q + 3)
                            for h in range(GH):
                                to = slice(h * P, (h + 1) * P)
                                pe.matmul(bank(d, 0)[:, to], IT[:, n % 2, d, h, :], VN[:, d, h, :], start=True, stop=True)
                                mm = pe.matmul(bank(d, 3)[:, to], KE[:, d, h, :], VN[:, d, h, :],
                                               start=True, stop=True)
                            mm.then_inc(o_summed, 1)

                @block.vector
                def _(dve):
                    link = self.dve_link.on(dve)

                    def init(n, d):
                        if n < TT:
                            for X in (T, U):
                                ins = dve.tensor_copy(X[:, d, :, :], over(self.cst(C_IDENT)))
                            ins.then_inc(inited, 1)

                    def product(n):
                        for d in range(2 if n < TT else 0):
                            t = tile_of(n, d)
                            dve.wait_ge(dmasked, 2 * n + d + 1)
                            dve.tensor_tensor(LT[:, n % 2, d, :, :], E[:, d, :, :], B.LKK[:, t, :, :], ALU.mult)
                            dve.tensor_tensor(IT[:, n % 2, d, :, :], E[:, d, :, :], B.KQ[:, t, :, :], ALU.mult) \
                               .then_inc(products, 1)

                    def rest(n):
                        for d in range(2):
                            q, t = 2 * n + d, tile_of(n, d)
                            dve.wait_ge(ks_summed, q + 1)
                            dve.wait_ge(scaled, q + 1)
                            for h in range(GH):
                                ins = dve.scalar_tensor_tensor(
                                    R[:, d, h, :], bank(d, 0)[:, h * P:(h + 1) * P],
                                    B.nbG[:, t, 4 * d + h:4 * d + h + 1], VB[:, d, h, :], ALU.mult, ALU.add)
                            ins.then_inc(r_ready, 1)

                    def output(n):
                        for d in range(2):
                            t = tile_of(n, d)
                            O = heads(B.OG[:, t, :])
                            if n < TT // 2:
                                link(dve.tensor_tensor(O, heads(bank(d, 0)), bc(B.rqk[:, t, 0:4]), ALU.mult))
                                dve.tensor_tensor(O, O, OT[:, d, :, :], ALU.add).then_inc(out_done, 1)
                            else:
                                link(dve.tensor_tensor(O, O, OT[:, d, :, :], ALU.add))
                                link(dve.tensor_tensor(OT[:, d, :, :], heads(bank(d, 0)), bc(B.rqk[:, t, 0:4]),
                                                       ALU.mult))
                                dve.tensor_tensor(O, O, OT[:, d, :, :], ALU.add).then_inc(out_done, 1)

                    dve.wait_ge(cleared, 4)
                    for d in range(2):
                        init(0, d)
                    product(0)
                    for n in range(TT):
                        for s in range(LEVELS):
                            for d in range(2):
                                t = tile_of(n, d)
                                at = C_LEVEL + (d * LEVELS + s) * 64
                                dve.wait_ge(y_summed, idx(n, s, d) + 1)
                                for h in range(GH):
                                    ins = dve.scalar_tensor_tensor(
                                        half(Y[d][:, s, h, :], s, d), split(bank(d, 1)[:, h * 64:(h + 1) * 64], s),
                                        B.brk[:, t, 4 * d + h:4 * d + h + 1], split(self.cst(at, 64), s),
                                        ALU.mult, ALU.mult)
                                ins.then_inc(y_kept, 1)
                            for d in range(2):
                                dve.wait_ge(z_summed, idx(n, s, d) + 1)
                                for X, lo, sel in ((T, 0, d), (U, 256, 1 - d)):
                                    if X is T and s == LEVELS - 1:
                                        continue
                                    by_half = lambda x: x.rearrange("p h (g two b) -> p h g two b", two=2, b=1 << s)[
                                        :, :, :, sel, :]
                                    cols = by_half(X[:, d, :, :])
                                    z = bank(d, 2)[:, lo:lo + 256].rearrange("p (h g b) -> p h g b", h=GH, b=1 << s)
                                    if X is T and s == 0:
                                        z = by_half(Y[d][:, 0, :, :])
                                    if s == 0:
                                        cols, z = cols[:, :, :, 0], z[:, :, :, 0]
                                    elif s == LEVELS - 1:
                                        cols, z = cols[:, :, 0, :], z[:, :, 0, :]
                                    ins = dve.tensor_tensor(cols, cols, z, ALU.subtract)
                                ins.then_inc(updated, 1)
                            if s == 0 and n:
                                output(n - 1)
                            if s == 1:
                                rest(n)
                            if s == 4:
                                product(n + 1)
                        for d in range(2):
                            q, t = 2 * n + d, tile_of(n, d)
                            dve.wait_ge(v_summed, q + 1)
                            link(dve.tensor_tensor(OT[:, d, :, :], heads(bank(d, 1)), bc(B.req[:, t, 4 * d:4 * d + 4]),
                                                   ALU.mult))
                            init(n + 1, d)
                        for d in range(2):
                            q, t = 2 * n + d, tile_of(n, d)
                            dve.wait_ge(o_summed, q + 1)
                            for h in range(GH):
                                ins = dve.scalar_tensor_tensor(S[:, d, h, :], S[:, d, h, :],
                                                               B.ex[:, 2, t, 4 * d + h:4 * d + h + 1],
                                                               bank(d, 3)[:, h * P:(h + 1) * P], ALU.mult, ALU.add)
                            ins.then_inc(state_done, 1)
                    output(TT - 1)

    def stage_gdn_out(self, B):
        nc = self.nc
        with ExitStack() as ctx:
            sq = self.sb(ctx, "go_sq", [P, TT * GH, P])
            ss = self.sb(ctx, "go_ss", [P, TT * GH])
            gated, rooted, turned, summed = (self.sem("go_" + n) for n in ("gated", "rooted", "turned", "summed"))
            O = B.OG[:, :, :].rearrange("p t (h c) -> p (t h) c", h=GH)
            Z = B.GZ[:, :, :].rearrange("p t (h c) -> p (t h) c", h=GH)
            with nc.Block() as block:
                @block.sync
                def _(sp):
                    self.W.stream(sp)

                @block.scalar
                def _(act):
                    act.activation(Z, Z, ACT.Silu).then_inc(gated, 1)
                    act.wait_ge(summed, 1)
                    act.activation(ss[:, :], ss[:, :], ACT.Sqrt).then_inc(rooted, 1)
                    for h in range(1, GH, 2):
                        act.wait_ge(turned, h + 1)
                        act.activation(B.YT[:, 4 + h, :], self.psum[:, h, :], ACT.Copy)

                @block.gpsimd
                def _(pool):
                    link = self.pool_link.on(pool)
                    pool.wait_ge(gated, 1)
                    link(pool.tensor_tensor(Z, Z, B.gnw[:, :].unsqueeze(1).to_broadcast([P, TT * GH, P]), ALU.mult))
                    pool.sem_inc(gated, 1)

                @block.vector
                def _(dve):
                    link = self.dve_link.on(dve)
                    link(dve.tensor_tensor(sq[:, :, :], O, O, ALU.mult))
                    link(dve.tensor_reduce(ss[:, :], sq[:, :, :], AX.X, ALU.add))
                    link(dve.tensor_scalar(ss[:, :], ss[:, :], 1.0 / P, EPS, ALU.mult, ALU.add))
                    dve.sem_inc(summed, 1)
                    dve.wait_ge(rooted, 1)
                    link(dve.reciprocal(ss[:, :], ss[:, :]))
                    link(dve.tensor_tensor(O, O, ss[:, :].unsqueeze(2).to_broadcast([P, TT * GH, P]), ALU.mult))
                    dve.wait_ge(gated, 2)
                    link(dve.tensor_tensor(O, O, Z, ALU.mult))
                    dve.sem_inc(summed, 1)
                    for h in range(0, GH, 2):
                        dve.wait_ge(turned, h + 1)
                        dve.tensor_copy(B.YT[:, 4 + h, :], self.psum[:, h, :])

                @block.tensor
                def _(pe):
                    pe.wait_ge(summed, 2)
                    for h in range(GH):
                        for t in range(TT):
                            tr = pe.transpose(self.psum[:, h, t * P:(t + 1) * P], B.OG[:, t, h * P:(h + 1) * P],
                                              self.cst(C_IDENT))
                        tr.then_inc(turned, 1)

    def stage_residual(self, tag, YT, alpha=1.0):
        nc, W = self.nc, self.W
        with ExitStack() as ctx:
            tmp = self.sb(ctx, f"{tag}_tmp", [P, 2, COLS])
            summed, added = self.sem(f"{tag}_summed"), self.sem(f"{tag}_added")
            base = W.begin([(summed, TT * (n + 1)) for n in range(2)])
            with nc.Block() as block:
                @block.sync
                def _(sp):
                    W.stream(sp)

                @block.tensor
                def _(pe):
                    for n in range(2):
                        W.wait(pe, base + n)
                        slot = W.slot(base + n).rearrange("p (k c) -> p k c", k=KD)
                        for t in range(TT):
                            for k in range(KD):
                                mm = pe.matmul(self.psum[:, n * TT + t, :], YT[:, k, t * P:(t + 1) * P],
                                               slot[:, k, :], start=(k == 0), stop=(k == KD - 1))
                            mm.then_inc(summed, 1)

                @block.vector
                def _(dve):
                    link = self.dve_link.on(dve)
                    for n in range(2):
                        cols = slice(n * COLS, (n + 1) * COLS)
                        for t in range(TT):
                            u = n * TT + t
                            dve.wait_ge(summed, u + 1)
                            link(dve.tensor_tensor(tmp[:, u % 2, :], self.psum[:, u, :], self.gate[:, cols], ALU.mult))
                            dve.scalar_tensor_tensor(self.X[:, t, cols], self.X[:, t, cols], alpha, tmp[:, u % 2, :],
                                                     ALU.mult, ALU.add).then_inc(added, 1)

    def stage_route(self, R):
        nc, i = self.nc, self.i
        NE, NG, PER = 32, 4, 8
        GL, EL, G4, BE = 0, NG, 8, 32
        names = ("loaded zeroed summed ranked counted prefixed computed exped scattered listed turned cleared")
        (loaded, zeroed, summed, ranked, counted, prefixed, computed, exped, scattered, listed, turned, cleared) = (
            self.sem("rt_" + n) for n in names.split())
        with ExitStack() as ctx:
            RW = self.sb(ctx, "router_w", [P, KD, NG + NE])
            RB = self.sb(ctx, "router_b", [P, NG + NE])
            L = self.sb(ctx, "logits", [P, TT, NG + NE])
            s4 = self.sb(ctx, "rt_s4", [P, 2, TT, NG])
            s32 = self.sb(ctx, "rt_s32", [P, 2, TT, NE])
            OH = self.sb(ctx, "rt_onehot", [P, 2, TT, NE])
            A = self.sb(ctx, "rt_assigned", [P, TT, NE])
            v = self.sb(ctx, "rt_scalars", [P, 8, TT])
            nbT = self.sb(ctx, "rt_blocks_of", [NE, 4])
            ends = self.sb(ctx, "rt_ends", [P, 2, NE])
            cmp = self.sb(ctx, "rt_cmp", [P, NBMAX + 1, NE])
            bef = self.sb(ctx, "rt_bef", [P, NBMAX + 1])
            destf = self.sb(ctx, "rt_destf", [P, 2, TT])
            zero = self.sb(ctx, "rt_zero", [NBMAX + 1, P])
            lists = self.sb(ctx, "rt_lists", [NBMAX + 1, P])
            tok = R.tok_of_row
            with nc.Block() as block:
                @block.sync
                def _(sp):
                    for src, at, n in ((i["router_group_w"][0], 0, NG), (i["router_expert_w"][0], NG, NE)):
                        sp.dma_start(RW[:, :, at:at + n], src.rearrange("(k p) e -> p k e", p=P)).then_inc(loaded, 16)
                    for src, at, n in ((i["router_group_b"], 0, NG), (i["router_expert_b"], NG, NE)):
                        sp.dma_start(RB[:, at:at + n], bass.AP(src.tensor, 0, [[0, P], [1, n]])).then_inc(loaded, 16)
                    sp.wait_ge(cleared, 1)
                    sp.dma_start(tok.rearrange("(n p) a -> n (p a)", p=P), zero[:, :]).then_inc(zeroed, 16)
                    sp.wait_ge(scattered, 16 * 2 * TT)
                    sp.dma_start(lists[:, :], tok.rearrange("(n p) a -> n (p a)", p=P)).then_inc(listed, 16)

                @block.tensor
                def _(pe):
                    pe.wait_ge(loaded, 64)
                    for t in range(TT):
                        for k in range(KD):
                            mm = pe.matmul(self.psum[:, 0, t * 36:(t + 1) * 36], self.HT[:, k, t * P:(t + 1) * P],
                                           RW[:, k, :], start=(k == 0), stop=(k == KD - 1))
                    mm.then_inc(summed, 1)
                    pe.wait_ge(computed, 1)
                    for t in range(TT):
                        for s in range(t + 1):
                            pe.matmul(self.psum[:, 1, t * NE:(t + 1) * NE], self.cst(C_LT if s == t else C_ONES),
                                      A[:, s, :], start=(s == 0), stop=(s == t))
                    for t in range(TT):
                        mm = pe.matmul(self.psum[0:NE, 2, 0:1], A[:, t, :], self.cst(C_ONES, 1),
                                       start=(t == 0), stop=(t == TT - 1))
                    mm.then_inc(counted, 1)
                    pe.wait_ge(computed, 2)
                    wide = nbT[:, 3:4].to_broadcast([NE, P])
                    pe.matmul(self.psum[:, 3, 0:NE], wide, self.const[0:NE, C_LT:C_LT + NE], start=True, stop=True)
                    mm = pe.matmul(self.psum[:, 3, NE:2 * NE], wide, self.const[0:NE, C_LE:C_LE + NE],
                                   start=True, stop=True)
                    mm.then_inc(prefixed, 1)
                    pe.wait_ge(listed, 16)
                    n = NBMAX + 1
                    pe.transpose(self.psum[:, 4, 0:n], lists[:, :], self.const[0:n, C_IDENT:C_IDENT + n]) \
                      .then_inc(turned, 1)

                @block.scalar
                def _(act):
                    act.wait_ge(exped, 1)
                    act.activation(s4[:, 0, :, :], s4[:, 0, :, :], ACT.Exp).then_inc(exped, 1)
                    act.wait_ge(exped, 3)
                    act.activation(v[:, 5, :], v[:, 5, :], ACT.Exp).then_inc(exped, 1)

                @block.gpsimd
                def _(pool):
                    pool.memset(zero[:, :], 0.0).then_inc(cleared, 1)
                    pool.wait_ge(zeroed, 16)
                    pool.wait_ge(computed, 3)
                    for k in range(2):
                        for t in range(TT):
                            pool.indirect_dma_start(
                                tok, bass.IndirectOffsetOnAxis(R.dest[:, k, t:t + 1].bitcast(U32), 0),
                                self.const[:, C_TOK + t:C_TOK + t + 1], None).then_inc(scattered, 16)

                @block.vector
                def _(dve):
                    link = self.dve_link.on(dve)
                    rep = lambda ap, n: ap.unsqueeze(2).to_broadcast([P, TT, n])
                    iota = lambda n: self.cst(C_IOTA, n).unsqueeze(1).to_broadcast([P, TT, n])
                    dve.wait_ge(loaded, 64)
                    dve.wait_ge(summed, 1)
                    link(dve.tensor_tensor(L[:, :, :], self.psum[:, 0, 0:TT * 36].rearrange("p (t e) -> p t e", t=TT),
                                           RB[:, :].unsqueeze(1).to_broadcast([P, TT, 36]), ALU.add))
                    gl, el = L[:, :, 0:NG], L[:, :, NG:]

                    def first_of(x, n, top, index, scratch):
                        link(dve.tensor_reduce(top, x, AX.X, ALU.max))
                        link(dve.tensor_tensor(scratch, x, rep(top, n), ALU.is_lt))
                        link(dve.scalar_tensor_tensor(scratch, scratch, 64.0, iota(n), ALU.mult, ALU.add))
                        link(dve.tensor_reduce(index, scratch, AX.X, ALU.min))

                    first_of(gl, NG, v[:, 0, :], v[:, 1, :], s4[:, 1, :, :])
                    link(dve.tensor_tensor(s4[:, 0, :, :], gl, rep(v[:, 0, :], NG), ALU.subtract))
                    dve.sem_inc(exped, 1)
                    link(dve.tensor_tensor(s4[:, 1, :, :], iota(NG), rep(v[:, 1, :], NG), ALU.not_equal))
                    link(dve.tensor_scalar(s4[:, 1, :, :], s4[:, 1, :, :], NEG, None, ALU.mult))
                    for t in range(TT):
                        link(dve.tensor_tensor(s32[:, 0, t, :].rearrange("p (g e) -> p g e", g=NG),
                                               el[:, t, :].rearrange("p (g e) -> p g e", g=NG),
                                               s4[:, 1, t, :].unsqueeze(2).to_broadcast([P, NG, PER]), ALU.add))
                    for k in range(2):
                        first_of(s32[:, 0, :, :], NE, v[:, 2 + k, :], v[:, 4, :], s32[:, 1, :, :])
                        link(dve.tensor_tensor(OH[:, k, :, :], iota(NE), rep(v[:, 4, :], NE), ALU.is_equal))
                        if k == 0:
                            link(dve.scalar_tensor_tensor(s32[:, 0, :, :], OH[:, 0, :, :], 2 * NEG, s32[:, 0, :, :],
                                                          ALU.mult, ALU.add))
                    link(dve.tensor_tensor(A[:, :, :], OH[:, 0, :, :], OH[:, 1, :, :], ALU.add))
                    dve.sem_inc(computed, 1)
                    dve.wait_ge(exped, 2)
                    link(dve.tensor_tensor(v[:, 5, :], v[:, 3, :], v[:, 2, :], ALU.subtract))
                    dve.sem_inc(exped, 1)
                    link(dve.tensor_reduce(v[:, 6, :], s4[:, 0, :, :], AX.X, ALU.add))
                    dve.wait_ge(exped, 4)
                    link(dve.tensor_scalar(v[:, 7, :], v[:, 5, :], 1.0, None, ALU.add))
                    link(dve.tensor_tensor(v[:, 6, :], v[:, 6, :], v[:, 7, :], ALU.mult))
                    link(dve.reciprocal(R.gates[:, 0, :], v[:, 6, :]))
                    link(dve.tensor_tensor(R.gates[:, 1, :], R.gates[:, 0, :], v[:, 5, :], ALU.mult))
                    dve.wait_ge(counted, 1)
                    link(dve.tensor_copy(nbT[:, 0:1], self.psum[0:NE, 2, 0:1]))
                    link(dve.tensor_scalar(nbT[:, 3:4], nbT[:, 0:1], 0.0, None, ALU.is_gt))
                    for n in range(1, SEQ // P):
                        link(dve.tensor_scalar(nbT[:, 1:2], nbT[:, 0:1], float(n * P), None, ALU.is_gt))
                        link(dve.tensor_tensor(nbT[:, 3:4], nbT[:, 3:4], nbT[:, 1:2], ALU.add))
                    dve.sem_inc(computed, 1)
                    dve.wait_ge(prefixed, 1)
                    link(dve.tensor_copy(ends[:, :, :].rearrange("p a e -> p (a e)"), self.psum[:, 3, 0:2 * NE]))
                    link(dve.tensor_scalar(ends[:, 0, :], ends[:, 0, :], float(P), None, ALU.mult))
                    link(dve.tensor_tensor(s32[:, 0, :, :], self.psum[:, 1, 0:TT * NE].rearrange("p (t e) -> p t e", t=TT),
                                           ends[:, 0, :].unsqueeze(1).to_broadcast([P, TT, NE]), ALU.add))
                    for k in range(2):
                        link(dve.tensor_tensor(s32[:, 1, :, :], s32[:, 0, :, :], OH[:, k, :, :], ALU.mult))
                        link(dve.tensor_reduce(destf[:, k, :], s32[:, 1, :, :], AX.X, ALU.add))
                    link(dve.tensor_copy(R.dest[:, :, :], destf[:, :, :]))
                    dve.sem_inc(computed, 1)
                    link(dve.tensor_tensor(cmp[:, :, :], ends[:, 1, :].unsqueeze(1).to_broadcast([P, NBMAX + 1, NE]),
                                           self.cst(C_IOTA, NBMAX + 1).unsqueeze(2).to_broadcast([P, NBMAX + 1, NE]),
                                           ALU.is_le))
                    link(dve.tensor_reduce(bef[:, :], cmp[:, :, :], AX.X, ALU.add))
                    link(dve.tensor_scalar(R.block_expert[:, :], bef[:, :], float(NE - 1), None, ALU.min))
                    link(dve.tensor_copy(R.n_blocks[:, 0:1], ends[:, 1, NE - 1:NE]))
                    link(dve.tensor_scalar(R.n_blocks[:, 1:2], ends[:, 1, NE - 1:NE], 1.0, None, ALU.subtract))
                    dve.wait_ge(turned, 1)
                    link(dve.tensor_copy(R.rows[:, :], self.psum[:, 4, 0:NBMAX + 1]))

    def stage_experts(self, R):
        nc, i = self.nc, self.i
        w1 = i["expert_w1"][0].rearrange("e (k p) c -> p (e k) c", p=P)
        w3 = i["expert_w3"][0].rearrange("e (k p) c -> p (e k) c", p=P)
        w2 = i["expert_w2"][0].rearrange("e (k p) c -> p (e k) c", p=P)
        KF = 4
        halves = [self.ring[:, n // 2, (n % 2) * 2048:(n % 2 + 1) * 2048].rearrange("p (k c) -> p k c", k=4)
                  for n in range(6)]
        arrived = [self.sem(f"w_half{n}_arrived") for n in range(6)]
        used = [self.sem(f"w_half{n}_used") for n in range(6)]
        names = "idx_copied gathered rows_turned xt_act xt_dve silued hidden h_turned ht_kept y_act y_dve y_stored gathering"
        (idx_copied, gathered, rows_turned, xt_act, xt_dve, silued, hidden, h_turned, ht_kept, y_act, y_dve,
         y_stored, gathering) = (self.sem("ex_" + n) for n in names.split())
        bankA, bankB = self.psum[:, 0, :], self.psum[:, 1, :]
        turn = lambda k: self.psum[:, 2 + k // 4, (k % 4) * P:(k % 4 + 1) * P]
        bankH = self.psum[:, 4, :]
        bankY = lambda c: self.psum[:, 5 + c, :]
        scale, shift = self.modA[:, 0, :], self.mod[:, 3 * KD:4 * KD]
        with ExitStack() as ctx:
            XG = self.sb(ctx, "ex_rows", [P, D])
            XT = self.sb(ctx, "ex_XT", [P, KD, P])
            IDX = self.sb(ctx, "ex_idx", [P, 1], I32)
            HS = self.sb(ctx, "ex_silu", [P, 512])
            HM = self.sb(ctx, "ex_hidden", [P, 512])
            HTB = self.sb(ctx, "ex_hiddenT", [P, KF, P])
            YO = self.sb(ctx, "ex_out", [P, D])
            ys = R.ys

            def count(eng):
                return [eng.value_load(R.n_blocks[0:1, c:c + 1], min_val=SEQ * 2 // P - c, max_val=NBMAX - c)
                        for c in range(2)]

            with nc.Block() as block:
                @block.sync
                def _(sp):
                    nb, last = count(sp)

                    def up(n, first):
                        e = sp.value_load(R.block_expert[0:1, bass.ds(n, 1)], min_val=0, max_val=31)
                        for m, w in enumerate((w1, w3)):
                            for h in range(2):
                                if not first:
                                    sp.wait_ge(used[2 * m + h], n)
                                sp.dma_start(halves[2 * m + h], w[:, bass.ds(e * 8 + 4 * h, 4), :]) \
                                  .then_inc(arrived[2 * m + h], 16)

                    def down(n, first):
                        e = sp.value_load(R.block_expert[0:1, bass.ds(n, 1)], min_val=0, max_val=31)
                        for h in range(2):
                            if not first:
                                sp.wait_ge(used[4 + h], n)
                            sp.dma_start(halves[4 + h], w2[:, bass.ds(e * 4, 4), h * 512:(h + 1) * 512]) \
                              .then_inc(arrived[4 + h], 16)

                    up(0, True)
                    up(1, False)
                    down(0, True)
                    with sp.Fori(2, nb) as n:
                        up(n, False)
                        down(n - 1, False)
                    down(last, False)

                @block.gpsimd
                def _(pool):
                    nb, _ = count(pool)

                    def gather(m, first):
                        if not first:
                            pool.wait_ge(rows_turned, m)
                        pool.tensor_copy(IDX[:, :], R.rows[:, bass.ds(m, 1)]).then_inc(idx_copied, 1)
                        pool.wait_ge(idx_copied, m + 1)
                        pool.sem_inc(gathering, 1)
                        pool.indirect_dma_start(XG[:, :], None, R.xn,
                                                bass.IndirectOffsetOnAxis(IDX[:, :].bitcast(U32), 0)) \
                            .then_inc(gathered, 16)
                    gather(0, True)
                    with pool.Fori(1, nb + 1) as m:
                        gather(m, False)

                @block.tensor
                def _(pe):
                    nb, last = count(pe)

                    def rows(m):
                        pe.wait_ge(gathered, m * 16 + 16)
                        for k in range(KD):
                            tr = pe.transpose(turn(k), XG[:, k * P:(k + 1) * P], self.cst(C_IDENT))
                        tr.then_inc(rows_turned, 1)

                    def up(n, first):
                        pe.wait_ge(xt_act, n + 1)
                        pe.wait_ge(xt_dve, n + 1)
                        for m, bank in enumerate((bankA, bankB)):
                            if not first:
                                pe.wait_ge((silued, hidden)[m], n)
                            for h in range(2):
                                pe.wait_ge(arrived[2 * m + h], n * 16 + 16)
                                for k in range(4):
                                    mm = pe.matmul(bank, XT[:, 4 * h + k, :], halves[2 * m + h][:, k, :],
                                                   start=(h + k == 0), stop=(h * 4 + k == KD - 1))
                                mm.then_inc(used[2 * m + h], 1)

                    def down(n):
                        pe.wait_ge(ht_kept, n + 1)
                        pe.wait_ge(y_act, n + 1)
                        pe.wait_ge(y_dve, n + 1)
                        for h in range(2):
                            pe.wait_ge(arrived[4 + h], n * 16 + 16)
                            for k in range(KF):
                                mm = pe.matmul(bankY(h), HTB[:, k, :], halves[4 + h][:, k, :],
                                               start=(k == 0), stop=(k == KF - 1))
                            mm.then_inc(used[4 + h], 1)

                    def hid(n):
                        pe.wait_ge(hidden, n + 1)
                        for k in range(KF):
                            tr = pe.transpose(bankH[:, k * P:(k + 1) * P], HM[:, k * P:(k + 1) * P],
                                              self.cst(C_IDENT))
                        tr.then_inc(h_turned, 1)

                    rows(0)
                    up(0, True)
                    rows(1)
                    hid(0)
                    with pe.Fori(1, nb) as n:
                        up(n, False)
                        rows(n + 1)
                        down(n - 1)
                        hid(n)
                    down(last)

                @block.scalar
                def _(act):
                    nb, last = count(act)
                    act.sem_inc(y_act, 1)
                    act.sem_inc(y_stored, 16)

                    def silu(n):
                        act.wait_ge(used[1], n + 1)
                        if not isinstance(n, int):
                            act.wait_ge(hidden, n)
                        act.activation(HS[:, :], bankA, ACT.Silu).then_inc(silued, 1)

                    def xt(m):
                        act.wait_ge(rows_turned, m + 1)
                        for k in range(KD // 2, KD):
                            ins = act.activation(XT[:, k, :], turn(k), ACT.Identity, scale=scale[:, k:k + 1],
                                                 bias=shift[:, k:k + 1])
                        ins.then_inc(xt_act, 1)

                    def out(n):
                        act.wait_ge(used[4], n + 1)
                        act.wait_ge(y_stored, n * 16 + 16)
                        act.activation(YO[:, 0:512], bankY(0), ACT.Copy).then_inc(y_act, 1)
                        act.wait_ge(y_act, n + 2)
                        act.wait_ge(y_dve, n + 2)
                        act.dma_start(ys[bass.ds(n * P, P), :], YO[:, :]).then_inc(y_stored, 16)

                    xt(0)
                    silu(0)
                    xt(1)
                    with act.Fori(1, nb) as n:
                        silu(n)
                        xt(n + 1)
                        out(n - 1)
                    out(last)
                    act.wait_ge(y_stored, nb * 16 + 16)
                    act.sem_inc(y_act, 1)

                @block.vector
                def _(dve):
                    nb, last = count(dve)
                    dve.sem_inc(y_dve, 1)

                    def gate(n):
                        dve.wait_ge(silued, n + 1)
                        dve.wait_ge(used[3], n + 1)
                        if not isinstance(n, int):
                            dve.wait_ge(h_turned, n)
                        dve.tensor_tensor(HM[:, :], HS[:, :], bankB, ALU.mult).then_inc(hidden, 1)

                    def xt(m):
                        dve.wait_ge(rows_turned, m + 1)
                        for k in range(KD // 2):
                            ins = dve.tensor_scalar(XT[:, k, :], turn(k), scale[:, k:k + 1], shift[:, k:k + 1],
                                                    ALU.mult, ALU.add)
                        ins.then_inc(xt_dve, 1)

                    def out(n):
                        dve.wait_ge(used[5], n + 1)
                        dve.wait_ge(y_stored, n * 16 + 16)
                        dve.tensor_copy(YO[:, 512:D], bankY(1)).then_inc(y_dve, 1)

                    def keep(n):
                        dve.wait_ge(h_turned, n + 1)
                        dve.tensor_copy(HTB[:, :, :].rearrange("p k s -> p (k s)"), bankH).then_inc(ht_kept, 1)

                    xt(0)
                    gate(0)
                    xt(1)
                    keep(0)
                    with dve.Fori(1, nb) as n:
                        gate(n)
                        xt(n + 1)
                        out(n - 1)
                        keep(n)
                    out(last)

    def stage_combine(self, R):
        nc = self.nc
        with ExitStack() as ctx:
            YG = self.sb(ctx, "cb_rows", [P, 4, D])
            fetched = [self.sem(f"cb_fetched{n}") for n in range(4)]
            added = self.sem("cb_added")
            with nc.Block() as block:
                @block.gpsimd
                def _(pool):
                    for t in range(TT):
                        if t >= 2:
                            pool.wait_ge(added, t - 1)
                        for k in range(2):
                            n = 2 * (t % 2) + k
                            pool.indirect_dma_start(YG[:, n, :], None, R.ys, bass.IndirectOffsetOnAxis(
                                R.dest[:, k, t:t + 1].bitcast(U32), 0)).then_inc(fetched[n], 16)

                @block.vector
                def _(dve):
                    link = self.dve_link.on(dve)
                    for t in range(TT):
                        for k in range(2):
                            dve.wait_ge(fetched[2 * (t % 2) + k], 16 * (t // 2 + 1))
                        a, b = YG[:, 2 * (t % 2), :], YG[:, 2 * (t % 2) + 1, :]
                        link(dve.tensor_scalar(a, a, R.gates[:, 0, t:t + 1], None, ALU.mult))
                        link(dve.scalar_tensor_tensor(a, b, R.gates[:, 1, t:t + 1], a, ALU.mult, ALU.add))
                        link(dve.tensor_tensor(a, a, self.gate[:, :], ALU.mult))
                        dve.tensor_tensor(self.X[:, t, :], self.X[:, t, :], a, ALU.add).then_inc(added, 1)

    def stage_row_norm(self, tag, eps, mean, gain, bias=None, out=None):
        nc = self.nc
        with ExitStack() as ctx:
            GB = self.sb(ctx, f"{tag}_gain", [P, 2, D])
            loaded, normed = self.sem(f"{tag}_loaded"), self.sem(f"{tag}_normed")
            with nc.Block() as block:
                rstd, mu, stats_dve, stats_act = self.row_stats(block, tag, ctx, eps, mean)
                n_vec = 1 if bias is None else 2

                @block.sync
                def _(sp):
                    for n, src in enumerate((gain, bias)[:n_vec]):
                        sp.dma_start(GB[:, n, :], bass.AP(src.tensor, 0, [[0, P], [1, D]])).then_inc(loaded, 16)
                    self.W.stream(sp)
                    if out is not None:
                        for t in range(TT):
                            sp.wait_ge(normed, t + 1)
                            self.nstored += 16
                            sp.dma_start(out[t * P:(t + 1) * P, :], self.X[:, t, :]).then_inc(self.stored, 16)
                        sp.wait_ge(self.stored, self.nstored)

                @block.scalar
                def _(act):
                    stats_act(act)

                @block.vector
                def _(dve):
                    link = self.dve_link.on(dve)
                    stats_dve(dve)
                    dve.wait_ge(loaded, 16 * n_vec)
                    for t in range(TT):
                        x = self.X[:, t, :]
                        if mean:
                            link(dve.tensor_scalar(x, x, mu[:, t, 0:1], rstd[:, t:t + 1], ALU.subtract, ALU.mult))
                            link(dve.tensor_tensor(x, x, GB[:, 0, :], ALU.mult))
                            dve.tensor_tensor(x, x, GB[:, 1, :], ALU.add).then_inc(normed, 1)
                        else:
                            dve.scalar_tensor_tensor(x, x, rstd[:, t:t + 1], GB[:, 0, :], ALU.mult, ALU.mult) \
                               .then_inc(normed, 1)

    def stage_branch_proj(self, tag, B, with_f):
        nc, i, W = self.nc, self.i, self.W
        widths = [COLS] * 3 + [8] * with_f
        items = [(n, "qk"[n], c) for n in range(2) for c in range(4)] + [(2, "v", t) for t in range(TT)]
        if with_f:
            items += [(3, "f", t) for t in range(TT)]
        BANKS = 6
        with ExitStack() as ctx:
            summed, copied = self.sem(f"{tag}_summed"), self.sem(f"{tag}_copied")
            base = W.begin([(summed, TT * (n + 1)) for n in range(len(widths))])
            with nc.Block() as block:
                @block.sync
                def _(sp):
                    W.stream(sp)

                @block.tensor
                def _(pe):
                    for n, (ld, what, c) in enumerate(items):
                        if n % 4 == 0:
                            W.wait(pe, base + ld)
                        if n >= BANKS:
                            pe.wait_ge(copied, n - BANKS + 1)
                        width = widths[ld]
                        slot = W.slot(base + ld)[:, 0:KD * width].rearrange("p (k c) -> p k c", k=KD)
                        bank = self.psum[:, n % BANKS, 0:width]
                        for k in range(KD):
                            if what in "vf":
                                mm = pe.matmul(bank, self.HT[:, k, c * P:(c + 1) * P], slot[:, k, :],
                                               start=(k == 0), stop=(k == KD - 1))
                            else:
                                mm = pe.matmul(bank, slot[:, k, c * P:(c + 1) * P], self.HT[:, k, :],
                                               start=(k == 0), stop=(k == KD - 1))
                        mm.then_inc(summed, 1)

                @block.scalar
                def _(act):
                    for n, (_, what, c) in enumerate(items):
                        act.wait_ge(summed, n + 1)
                        dst = (B.Q if what == "q" else B.K if what == "k" else B.V if what == "v" else B.F)[:, c, :]
                        act.activation(dst, self.psum[:, n % BANKS, 0:dst.shape[1]], ACT.Copy,
                                       scale=HD ** -0.5 if what == "q" else 1.0).then_inc(copied, 1)

    def log1p(self, dve, link, u, s2, acc, out):
        link(dve.tensor_scalar(acc, u, 2.0, None, ALU.add))
        link(dve.reciprocal(acc, acc))
        link(dve.tensor_tensor(u, u, acc, ALU.mult))
        link(dve.tensor_tensor(s2, u, u, ALU.mult))
        link(dve.tensor_scalar(acc, s2, 1.0 / 17, 1.0 / 15, ALU.mult, ALU.add))
        for n in (13, 11, 9, 7, 5, 3, 1):
            link(dve.tensor_tensor(acc, acc, s2, ALU.mult))
            link(dve.tensor_scalar(acc, acc, 1.0 / n, None, ALU.add))
        link(dve.scalar_tensor_tensor(out, u, 2.0, acc, ALU.mult, ALU.mult))

    def stage_forget(self, B):
        nc, i = self.nc, self.i
        H = FOX_H
        with ExitStack() as ctx:
            bf = self.sb(ctx, "fox_bf", [P, H])
            tmp = self.sb(ctx, "fox_tmp", [P, 4, TT * H])
            logf = self.sb(ctx, "fox_logf", [P, TT, H])
            loaded, absed, exped, ready, summed = (self.sem("fg_" + n) for n in
                                                   ("loaded", "absed", "exped", "ready", "summed"))
            with nc.Block() as block:
                @block.sync
                def _(sp):
                    sp.dma_start(bf[:, :], bass.AP(i["b_f_2"].tensor, 0, [[0, P], [1, H]])).then_inc(loaded, 16)

                @block.scalar
                def _(act):
                    act.wait_ge(absed, 1)
                    act.activation(tmp[:, 1, :], tmp[:, 1, :], ACT.Exp, scale=-1.0).then_inc(exped, 1)

                @block.vector
                def _(dve):
                    link = self.dve_link.on(dve)
                    x, u, s2, acc = (tmp[:, n, :] for n in range(4))
                    dve.wait_ge(loaded, 16)
                    link(dve.tensor_tensor(x.rearrange("p (t h) -> p t h", t=TT), B.F[:, :, :],
                                           bf[:, :].unsqueeze(1).to_broadcast([P, TT, H]), ALU.add))
                    link(dve.tensor_scalar(u, x, -1.0, None, ALU.mult))
                    link(dve.tensor_tensor(u, u, x, ALU.max))
                    dve.sem_inc(absed, 1)
                    dve.wait_ge(exped, 1)
                    self.log1p(dve, link, u, s2, acc, acc)
                    link(dve.scalar_tensor_tensor(logf[:, :, :].rearrange("p t h -> p (t h)"), x, 0.0, acc,
                                                  ALU.min, ALU.subtract))
                    dve.sem_inc(ready, 1)
                    dve.wait_ge(summed, 1)
                    dve.tensor_copy(B.cum[:, :, :].rearrange("p t h -> p (t h)"), self.psum[:, 0, 0:TT * H])
                    dve.tensor_copy(B.cumT[:, :], self.psum[0:H, 1, :])

                @block.tensor
                def _(pe):
                    pe.wait_ge(ready, 1)
                    for t in range(TT):
                        for s in range(t + 1):
                            tri = self.cst(C_LE if s == t else C_ONES)
                            pe.matmul(self.psum[:, 0, t * H:(t + 1) * H], tri, logf[:, s, :],
                                      start=(s == 0), stop=(s == t))
                            mm = pe.matmul(self.psum[0:H, 1, t * P:(t + 1) * P], logf[:, s, :], tri,
                                           start=(s == 0), stop=(s == t))
                    mm.then_inc(summed, 1)

    def stage_chunk_bias(self, CB, hank):
        nc = self.nc
        laid, flipped = self.sem("cb_laid"), self.sem("cb_flipped")
        with nc.Block() as block:
            @block.sync
            def _(sp):
                sp.dma_start(hank[:, :, :], bass.AP(self.i["rel_bias_2"].tensor, 0, [[1, P], [640, CH_H], [1, SEQ]])) \
                  .then_inc(laid, 16)

            @block.tensor
            def _(pe):
                pe.wait_ge(laid, 16)
                for h in range(CH_H):
                    pe.matmul(self.psum[:, h, :], self.cst(C_FLIP), hank[:, h, :], start=True, stop=True) \
                      .then_inc(flipped, 1)

            @block.vector
            def _(dve):
                for h in range(CH_H):
                    dve.wait_ge(flipped, h + 1)
                    dve.tensor_copy(CB[:, h, 0:SEQ - P], self.psum[:, h, 0:SEQ - P])
                    dve.tensor_tensor(CB[:, h, SEQ - P:], self.psum[:, h, SEQ - P:], self.cst(C_CHUNK), ALU.add)

    def stage_merge(self, B, M):
        nc, i, W = self.nc, self.i, self.W
        with ExitStack() as ctx:
            SG = self.sb(ctx, "mg_gate", [P, 2, SEQ])
            tmp = self.sb(ctx, "mg_tmp", [P, 2, SEQ])
            summed, sigm, merged = self.sem("mg_summed"), self.sem("mg_sigmoid"), self.sem("mg_merged")
            base = W.begin([(summed, 8 * b + n) for b in range(2) for n in (8, 4, 8)])
            with nc.Block() as block:
                @block.sync
                def _(sp):
                    W.stream(sp)

                @block.tensor
                def _(pe):
                    for u in range(16):
                        b, c = u // 8, u % 8
                        if c == 0:
                            W.wait(pe, base + 3 * b)
                        if c % 4 == 0:
                            W.wait(pe, base + 3 * b + 1 + c // 4)
                        if u >= 4:
                            pe.wait_ge(merged, u - 3)
                        wg = W.slot(base + 3 * b + 1 + c // 4).rearrange("p (k c) -> p k c", k=KD)
                        wb = W.slot(base + 3 * b).rearrange("p (k c) -> p k c", k=4)
                        src = (B.OA, B.OC)[b]
                        for k in range(KD):
                            pe.matmul(self.psum[:, 2 * (u % 4), :], wg[:, k, (c % 4) * P:(c % 4 + 1) * P],
                                      self.HT[:, k, :], start=(k == 0), stop=(k == KD - 1))
                        for k in range(4):
                            mm = pe.matmul(self.psum[:, 2 * (u % 4) + 1, :], wb[:, k, c * P:(c + 1) * P],
                                           src[:, k, :], start=(k == 0), stop=(k == 3))
                        mm.then_inc(summed, 1)

                @block.scalar
                def _(act):
                    for u in range(16):
                        act.wait_ge(summed, u + 1)
                        if u >= 2:
                            act.wait_ge(merged, u - 1)
                        act.activation(SG[:, u % 2, :], self.psum[:, 2 * (u % 4), :], ACT.Sigmoid).then_inc(sigm, 1)

                @block.vector
                def _(dve):
                    link = self.dve_link.on(dve)
                    for u in range(16):
                        c = u % 8
                        dve.wait_ge(sigm, u + 1)
                        if u < 8:
                            dve.tensor_tensor(M[:, c, :], SG[:, u % 2, :], self.psum[:, 2 * (u % 4) + 1, :],
                                              ALU.mult).then_inc(merged, 1)
                        else:
                            link(dve.tensor_tensor(tmp[:, u % 2, :], SG[:, u % 2, :],
                                                   self.psum[:, 2 * (u % 4) + 1, :], ALU.mult))
                            dve.tensor_tensor(M[:, c, :], M[:, c, :], tmp[:, u % 2, :], ALU.add).then_inc(merged, 1)

    def stage_up(self, YF, H):
        nc, W = self.nc, self.W
        NF = NCH // 2
        n_loads = NF // 2
        summed, copied, conved, silued, made, zeroed = (
            self.sem("up_" + n) for n in ("summed", "copied", "conved", "silued", "made", "zeroed"))
        with ExitStack() as ctx:
            PAD = self.sb(ctx, "up_pad", [P, 4, SEQ + 2])
            CV = self.sb(ctx, "up_conv", [P, 4, SEQ])
            WS = SplitWeights(self, ctx, "up", [(KD, 2 * P)] * n_loads, [(summed, 2 * p + 2) for p in range(NF)])
            with nc.Block() as block:
                @block.sync
                def _(sp):
                    W.stream(sp)

                @block.tensor
                def _(pe):
                    for m in range(NCH):
                        pair, side = m // 2, m % 2
                        if side == 0:
                            WS.wait(pe, pair)
                        if m >= 6:
                            pe.wait_ge(copied, m - 5)
                        w = WS.parts(pair)
                        for k in range(KD):
                            mm = matmul3(pe, self.psum[:, m % 6, :], [x[:, k, side * P:(side + 1) * P] for x in w],
                                         [x[:, k, :] for x in H], k == 0, k == KD - 1)
                        mm.then_inc(summed, 1)

                @block.scalar
                def _(act):
                    WS.round(act, 0)
                    WS.round(act, 1)
                    act.wait_ge(zeroed, 1)

                    def silu(pair):
                        m = 2 * pair
                        act.wait_ge(conved, m + 1)
                        act.activation(CV[:, m % 4, :], CV[:, m % 4, :], ACT.Silu).then_inc(silued, 1)
                    for m in range(NCH):
                        act.wait_ge(summed, m + 1)
                        if m >= 4:
                            act.wait_ge(conved, m - 3)
                        act.activation(PAD[:, m % 4, 2:], self.psum[:, m % 6, :], ACT.Copy).then_inc(copied, 1)
                        if m % 2 == 1:
                            WS.round(act, m // 2 + 2)
                        if m % 2 == 1 and m >= 3:
                            silu(m // 2 - 1)
                    silu(NF - 1)

                @block.vector
                def _(dve):
                    link = self.dve_link.on(dve)
                    WS.rest(dve, 0)
                    dve.memset(PAD[:, :, :], 0.0).then_inc(zeroed, 1)
                    WS.rest(dve, 1)

                    def product(pair):
                        m = 2 * pair
                        dve.wait_ge(silued, pair + 1)
                        dve.tensor_tensor(YF[:, pair, :], CV[:, m % 4, :], CV[:, (m + 1) % 4, :], ALU.mult) \
                           .then_inc(made, 1)
                    for m in range(NCH):
                        ch = m // 2 + NF * (m % 2)
                        tap = lambda j: self.cols3[:, j * NCH + ch:j * NCH + ch + 1]
                        x, cv = PAD[:, m % 4, :], CV[:, m % 4, :]
                        dve.wait_ge(copied, m + 1)
                        if m % 2 == 1:
                            WS.rest(dve, m // 2 + 2)
                        if m >= 4:
                            dve.wait_ge(made, m // 2 - 1)
                        link(dve.tensor_scalar(cv, x[:, 0:SEQ], tap(0), self.cols2[:, R2_CONVB + ch:R2_CONVB + ch + 1],
                                               ALU.mult, ALU.add))
                        link(dve.scalar_tensor_tensor(cv, x[:, 1:SEQ + 1], tap(1), cv, ALU.mult, ALU.add))
                        link(dve.scalar_tensor_tensor(cv, x[:, 2:SEQ + 2], tap(2), cv, ALU.mult, ALU.add))
                        dve.sem_inc(conved, 1)
                        if m % 2 == 1 and m >= 3:
                            product(m // 2 - 1)
                    product(NF - 1)

    def stage_down(self, YF, alpha):
        nc, W = self.nc, self.W
        NF = NCH // 2
        parts = [(k, min(4, NF - k)) for k in range(0, NF, 4)]
        summed, used = self.sem("down_summed"), self.sem("down_used")
        with ExitStack() as ctx:
            tmp = self.sb(ctx, "down_tmp", [P, 2, COLS])
            WS = SplitWeights(self, ctx, "down", [(nk, COLS) for _, nk in parts],
                              [(used, p + 1) for p in range(2 * len(parts))])
            YH, YL = (self.sb(ctx, f"down_in_{n}", [P, 2, 4, SEQ], F32R) for n in ("hi", "lo"))
            y_rounded, y_ready = self.sem("down_in_rounded"), self.sem("down_in_ready")
            with nc.Block() as block:
                @block.sync
                def _(sp):
                    W.stream(sp)

                @block.tensor
                def _(pe):
                    for n, (k0, nk) in enumerate(parts):
                        y = YH[:, n % 2, :, :], YL[:, n % 2, :, :]
                        for c in range(2):
                            w = WS.parts(2 * n + c)
                            if c == 0:
                                pe.wait_ge(y_ready, n + 1)
                            WS.wait(pe, 2 * n + c)
                            for t in range(TT):
                                for k in range(nk):
                                    mm = matmul3(pe, self.psum[:, c * TT + t, :], [x[:, k, t * P:(t + 1) * P] for x in y],
                                                 [x[:, k, :] for x in w], k0 + k == 0, k0 + k == NF - 1)
                                if n == len(parts) - 1:
                                    mm.then_inc(summed, 1)
                            if n < len(parts) - 1:
                                mm.then_inc(used, 1)

                @block.scalar
                def _(act):
                    for n, (k0, nk) in enumerate(parts):
                        WS.round(act, 2 * n)
                        if n >= 2:
                            act.wait_ge(used, 2 * n - 2)
                        act.activation(YH[:, n % 2, 0:nk, :], YF[:, k0:k0 + nk, :], ACT.Copy).then_inc(y_rounded, 1)
                        WS.round(act, 2 * n + 1)

                @block.vector
                def _(dve):
                    link = self.dve_link.on(dve)
                    for n, (k0, nk) in enumerate(parts):
                        WS.rest(dve, 2 * n)
                        dve.wait_ge(y_rounded, n + 1)
                        dve.tensor_tensor(YL[:, n % 2, 0:nk, :], YF[:, k0:k0 + nk, :],
                                          YH[:, n % 2, 0:nk, :].bitcast(F32), ALU.subtract).then_inc(y_ready, 1)
                        WS.rest(dve, 2 * n + 1)
                    for u in range(2 * TT):
                        t, c = u % TT, u // TT
                        cols = slice(c * COLS, (c + 1) * COLS)
                        dve.wait_ge(summed, u + 1)
                        link(dve.tensor_tensor(tmp[:, u % 2, :], self.psum[:, u, :], self.gate[:, cols], ALU.mult))
                        link(dve.scalar_tensor_tensor(self.X[:, t, cols], self.X[:, t, cols], alpha, tmp[:, u % 2, :],
                                                      ALU.mult, ALU.add))

    def stages(self):
        nc = self.nc
        self.ys = nc.dram_tensor("expert_rows", (NBMAX * P, D), F32).ap()

        class B:
            pass
        rows = lambda ap: ap.rearrange("(k p) c -> p k c", p=P)
        w_in, w_in_2, w_up = (rows(self.i[n][0]) for n in ("w_in", "w_in_2", "w_up_2"))
        cols = lambda w, at, n, width=COLS: [(w[:, :, at + j * width:at + (j + 1) * width],) for j in range(n)]
        self.W.plan += cols(w_in, 0, 7) + cols(w_in, 7 * COLS, 1, 16)
        with ExitStack() as ctx:
            B.YT = self.sb(ctx, "YT", [P, KD, SEQ])
            B.GZ = self.sb(ctx, "GZ", [P, TT, 512])
            B.GAB = self.sb(ctx, "GAB", [P, TT, 16])
            B.G = self.sb(ctx, "G", [P, 12, SEQ])
            B.OG = self.sb(ctx, "OG", [P, TT, 512])
            with ExitStack() as ctx2:
                B.NQ = self.sb(ctx2, "NQ", [P, 2, SEQ])
                B.NK = self.sb(ctx2, "NK", [P, 2, SEQ])
                B.NV = self.sb(ctx2, "NV", [P, TT, 256])
                with ExitStack() as ctx3:
                    MS = self.sb(ctx3, "mod_weights", [P, 2, KD, MCOLS])
                    spare = B.OG[:, :, :].rearrange("p t c -> p (t c)").rearrange("p (k c) -> p k c", k=KD)
                    self.mod_begin(ctx3, [MS[:, 0, :, :], MS[:, 1, :, :], spare])
                    self.stage_load()
                    self.stage_mod_first()
                    self.stage_scale("mix", self.cols1[:, R_NMIX:R_NFFN], KD)
                    self.stage_norm("norm_mix", EPS, False, self.modA[:, 0, :], self.mod[:, 0:KD])
                    self.stage_proj1(B)
                self.stage_na(B)
            with ExitStack() as ctx2:
                self.stage_gdn_prep(B, ctx2)
                self.stage_gdn(B)
                self.W.plan += cols(rows(self.i["w_out"][0]), 0, 2)
                self.stage_gdn_out(B)
            self.stage_gate("gate1", 2 * KD)
            self.stage_residual("mix_out", B.YT)
        self.retire_semaphores()

        class R:
            pass
        R.xn = nc.dram_tensor("normed_rows", (SEQ, D), F32).ap()
        R.ys = self.ys
        R.tok_of_row = nc.dram_tensor("token_of_row", ((NBMAX + 1) * P, 1), F32).ap()
        self.stage_scale("ffn", self.cols1[:, R_NFFN:R_CONVA], 4 * KD)
        self.stage_norm("norm_ffn", EPS, False, self.modA[:, 0, :], self.mod[:, 3 * KD:4 * KD], save_rows=R.xn)
        with ExitStack() as ctx:
            R.gates = self.sb(ctx, "gates", [P, 2, TT])
            R.dest = self.sb(ctx, "dest", [P, 2, TT], I32)
            R.rows = self.sb(ctx, "block_rows", [P, NBMAX + 1], I32)
            R.block_expert = self.sb(ctx, "block_expert", [P, NBMAX + 1], I32)
            R.n_blocks = self.sb(ctx, "n_blocks", [P, 2], I32)
            self.stage_route(R)
            self.stage_experts(R)
            self.stage_gate("gate2", 5 * KD)
            self.stage_combine(R)
        FORGET_AT, CHUNK_AT = 3 * COLS, 3 * COLS + FOX_H
        GATE_AT, NF = CHUNK_AT + 3 * COLS, NCH // 2
        self.W.plan += cols(w_in_2, 0, 3) + cols(w_in_2, FORGET_AT, 1, FOX_H) + cols(w_in_2, CHUNK_AT, 3)
        for b, name in enumerate(("w_br_fox_2", "w_br_chunk_2")):
            self.W.plan += [(rows(self.i[name][0]),)] + cols(w_in_2, GATE_AT + b * D, 2)
        self.W.plan += cols(rows(self.i["w_out_2"][0]), 0, 2)
        self.W.plan += [tuple(w_up[:, :, a:a + P] for at in (at2, at2 + P) for a in (at, NF * P + at))
                        for at2 in range(0, NF * P, 2 * P)]
        self.W.plan += [(rows(self.i["w_down_2"][0])[:, k:min(k + 4, NF), :],) for k in range(0, NF, 4)]
        self.stage_row_norm("final_norm", EPS, False, self.i["final_norm_w"])
        self.retire_semaphores()

        ALPHA = 2.0 ** 0.25
        self.mod = self.mods[:, 1, :]
        self.stage_scale("branches", None, KD)
        self.stage_norm("norm_branches", LN_EPS, True, self.modA[:, 0, :], self.mod[:, 0:KD])
        with ExitStack() as ctx:
            B.OA = self.sb(ctx, "OA", [P, 4, SEQ])
            B.OC = self.sb(ctx, "OC", [P, 4, SEQ])
            rows = lambda h: slice(HD * (h % 2), HD * (h % 2 + 1))
            causal = lambda t: (t + 1) * P
            with ExitStack() as ctx2:
                B.Q, B.K, B.V = (self.sb(ctx2, n, [P, 4, SEQ]) for n in ("bq", "bk", "bv"))
                B.F = self.sb(ctx2, "bf", [P, TT, FOX_H])
                B.cum = self.sb(ctx2, "cum", [P, TT, FOX_H])
                B.cumT = self.sb(ctx2, "cumT", [FOX_H, SEQ])
                q = lambda h: B.Q[rows(h), h // 2, :]
                k = lambda h: B.K[rows(h), h // 2, :]
                v = lambda h, j: B.V[:, j, h * HD:(h + 1) * HD]
                self.stage_branch_proj("fox_proj", B, True)
                self.stage_forget(B)
                pick = lambda h: self.const[0:FOX_H, C_IDENT + h:C_IDENT + h + 1].to_broadcast([FOX_H, P])
                self.stage_attention("fox", FOX_H, q, k, v, None, causal, lambda h: B.OA[rows(h), h // 2, :],
                                     cum=(lambda t, h: B.cum[:, t, h:h + 1], pick, B.cumT[:, :]))
                self.retire_semaphores()
                self.stage_branch_proj("chunk_proj", B, False)
                CB = self.sb(ctx2, "chunk_bias", [P, CH_H, SEQ])
                with ExitStack() as ctx3:
                    self.stage_chunk_bias(CB, self.sb(ctx3, "chunk_hankel", [P, CH_H, SEQ]))
                self.stage_attention("chunk", CH_H, q, k, v, lambda h, t: CB[:, h, SEQ - P - t * P:], causal,
                                     lambda h: B.OC[rows(h), h // 2, :])
            M = self.sb(ctx, "merged", [P, KD, SEQ])
            self.stage_merge(B, M)
            self.stage_gate("gate3", 2 * KD, 1.0)
            self.stage_residual("branch_out", M, alpha=ALPHA)
        self.stage_row_norm("ln1", LN_EPS, True, self.i["ln1_g_2"], self.i["ln1_b_2"])
        self.stage_scale("ffn2", None, 4 * KD)
        self.HT_life.close()
        with ExitStack() as ctx:
            YF = self.sb(ctx, "YF", [P, NCH // 2, SEQ])
            with ExitStack() as ctx2:
                H = [self.sb(ctx2, f"HT_{n}", [P, KD, SEQ], F32R) for n in ("hi", "lo")]
                with ExitStack() as ctx3:
                    self.HT = self.sb(ctx3, "HT_whole", [P, KD, SEQ])
                    self.stage_norm("norm_ffn2", LN_EPS, True, self.modA[:, 0, :], self.mod[:, 3 * KD:4 * KD], split=H)
                self.stage_up(YF, H)
            self.stage_gate("gate4", 5 * KD, 1.0)
            self.stage_down(YF, ALPHA)
        self.stage_row_norm("ln2", LN_EPS, True, self.i["ln2_g_2"], self.i["ln2_b_2"], out=self.out[0])


def lay_out(inputs):
    a = {k: np.ascontiguousarray(v) for k, v in inputs.items()}
    a["na_rpb"] = np.pad(a["na_rpb"][0], ((0, 0), (0, 0), (48, 48)))
    a["rel_bias_2"] = np.pad(a["rel_bias_2"][0][:, ::-1], ((0, 0), (383, 0)), mode="edge")
    a["shape_constants"] = shape_constants()
    return a


def kernel(**inputs):
    import concourse.bacc as bacc
    from concourse.bass_utils import run_bass_kernel_spmd

    nc = bacc.Bacc("TRN2", target_bir_lowering=False, num_devices=1)
    arrays, args = {}, {}
    for name, a in lay_out(inputs).items():
        arrays[f"in_{name}"] = a
        args[name] = nc.dram_tensor(f"in_{name}", a.shape, mybir.dt.from_np(a.dtype), kind="ExternalInput").ap()
    out = nc.dram_tensor("out", (1, SEQ, D), F32, kind="ExternalOutput").ap()
    Kernel(nc, args, out).build()
    r = run_bass_kernel_spmd(nc, [arrays], core_ids=[0])
    return r.results[0]["out"]
```
